# Optimizing a Trainium2 kernel written in Bass

```python
import math
import jax, jax.numpy as jnp
from jax import lax
import numpy as np

D_MODEL = 1024
BATCH = 1
SEQ = 512
DEPTH = 1

N_HEADS = 8
HEAD_DIM = 64
N_KV_HEADS = 2
IDX_HEADS = 8
IDX_DIM = 64
TOPK_MAX = 256
Q_BLOCK = 64
N_BUCKETS = 32
MAX_DISTANCE = 128
D_RNN = D_MODEL
N_RNN_BLOCKS = 8
RNN_BLOCK = D_RNN // N_RNN_BLOCKS
RNN_CONV = 4
LRU_C = 8.0
D_FF = 2816
FFN_CONV = 3
EPS = 1e-6

ATTN_WIDTH = N_HEADS * HEAD_DIM
KV_WIDTH = N_KV_HEADS * HEAD_DIM
SPLITS = (ATTN_WIDTH, KV_WIDTH, KV_WIDTH, IDX_HEADS * IDX_DIM, IDX_DIM, IDX_HEADS, D_RNN, D_RNN, D_MODEL, D_MODEL)
N_IN = 5448


def rms_norm(x, g):
    x32 = x.astype(jnp.float32)
    y = x32 * lax.rsqrt(jnp.mean(x32 * x32, axis=-1, keepdims=True) + EPS)
    return (y * g.astype(jnp.float32)).astype(x.dtype)

def causal_dwconv(x, w, b):
    width = w.shape[0]
    seq = x.shape[1]
    xp = jnp.pad(x, ((0, 0), (width - 1, 0), (0, 0)))
    y = xp[:, 0:seq] * w[0]
    for k in range(1, width):
        y = y + xp[:, k:k + seq] * w[k]
    return y + b

def t5_bucket(rel):
    max_exact = N_BUCKETS // 2
    n = jnp.maximum(rel, 0)
    nf = jnp.maximum(n, 1).astype(jnp.float32)
    large = max_exact + (jnp.log(nf / max_exact) / math.log(MAX_DISTANCE / max_exact)
                         * (N_BUCKETS - max_exact)).astype(jnp.int32)
    large = jnp.minimum(large, N_BUCKETS - 1)
    return jnp.where(n < max_exact, n, large)

def dsa_attention(q, k, v, q_idx, k_idx, w_idx, rel_bias):
    B, S = q.shape[0], q.shape[1]
    n_sel = min(TOPK_MAX, S // 4)
    nb = S // Q_BLOCK
    G = N_HEADS // N_KV_HEADS
    pos = jnp.arange(S, dtype=jnp.int32)
    gather = jax.vmap(lambda t_b, i_b: t_b[i_b])

    def to_blocks(t):
        return jnp.moveaxis(t.reshape((B, nb, Q_BLOCK) + t.shape[2:]), 1, 0)

    def block(args):
        qb, qib, wb, tb = args
        dots = jnp.einsum('bqhd,bsd->bqhs', qib, k_idx).astype(jnp.float32) * (IDX_DIM ** -0.5)
        score = jnp.einsum('bqh,bqhs->bqs', wb.astype(jnp.float32) * (IDX_HEADS ** -0.5), jax.nn.relu(dots))
        causal = pos[None, :] <= tb[:, None]
        score = jnp.where(causal[None], score, -jnp.inf)
        _, sel = lax.top_k(score, n_sel)
        valid = sel <= tb[None, :, None]
        ks = gather(k, sel)
        vs = gather(v, sel)
        qg = qb.reshape(B, Q_BLOCK, N_KV_HEADS, G, HEAD_DIM)
        logits = jnp.einsum('bqhgd,bqnhd->bqhgn', qg, ks).astype(jnp.float32) * (HEAD_DIM ** -0.5)
        bucket = t5_bucket(tb[None, :, None] - sel)
        bias = rel_bias[bucket].astype(jnp.float32)
        bias = bias.reshape(B, Q_BLOCK, n_sel, N_KV_HEADS, G).transpose(0, 1, 3, 4, 2)
        logits = jnp.where(valid[:, :, None, None, :], logits + bias, -jnp.inf)
        p = jax.nn.softmax(logits, axis=-1).astype(vs.dtype)
        o = jnp.einsum('bqhgn,bqnhd->bqhgd', p, vs)
        return o.reshape(B, Q_BLOCK, N_HEADS * HEAD_DIM)

    out = lax.map(block, (to_blocks(q), to_blocks(q_idx), to_blocks(w_idx), pos.reshape(nb, Q_BLOCK)))
    return jnp.moveaxis(out, 0, 1).reshape(B, S, N_HEADS * HEAD_DIM)

def rg_lru(x, w_rg, b_rg, w_ig, b_ig, lam):
    B, S = x.shape[0], x.shape[1]
    xb = x.reshape(B, S, N_RNN_BLOCKS, RNN_BLOCK)
    r = jax.nn.sigmoid(jnp.einsum('bsnc,ncd->bsnd', xb, w_rg).reshape(B, S, D_RNN) + b_rg)
    i = jax.nn.sigmoid(jnp.einsum('bsnc,ncd->bsnd', xb, w_ig).reshape(B, S, D_RNN) + b_ig)
    log_a = -LRU_C * r.astype(jnp.float32) * jax.nn.softplus(-lam.astype(jnp.float32))
    a = jnp.exp(log_a)
    mult = jnp.sqrt(-jnp.expm1(2.0 * log_a))
    u = x.astype(jnp.float32) * i.astype(jnp.float32) * mult

    def combine(left, right):
        a1, b1 = left
        a2, b2 = right
        return a1 * a2, a2 * b1 + b2

    _, h = lax.associative_scan(combine, (a, u), axis=1)
    return h.astype(x.dtype)

def first_inputs(seed: int = 0) -> dict:
    key = jax.random.key(seed)
    ks = jax.random.split(key, 32)
    f32 = jnp.float32

    def nrm(k, shape, scale):
        return jax.random.normal(k, shape, f32) * scale

    L = DEPTH
    a0 = jax.random.uniform(ks[13], (L, D_RNN), f32, 0.9, 0.999)
    p = a0 ** (1.0 / LRU_C)
    lam = jnp.log(p) - jnp.log1p(-p)
    return {
        "x": nrm(ks[0], (BATCH, SEQ, D_MODEL), 1.0),
        "c": nrm(ks[1], (BATCH, D_MODEL), 1.0),
        "w_ada": nrm(ks[2], (L, D_MODEL, 6 * D_MODEL), D_MODEL ** -0.5),
        "b_ada": nrm(ks[3], (L, 6 * D_MODEL), 0.02),
        "g_mix": 1.0 + nrm(ks[4], (L, D_MODEL), 0.02),
        "w_in": nrm(ks[5], (L, D_MODEL, N_IN), D_MODEL ** -0.5),
        "b_in": nrm(ks[6], (L, N_IN), 0.01),
        "rel_bias": nrm(ks[7], (N_BUCKETS, N_HEADS), 0.5),
        "conv_rnn_w": nrm(ks[8], (L, RNN_CONV, D_RNN), RNN_CONV ** -0.5),
        "conv_rnn_b": nrm(ks[9], (L, D_RNN), 0.01),
        "w_rg": nrm(ks[10], (L, N_RNN_BLOCKS, RNN_BLOCK, RNN_BLOCK), RNN_BLOCK ** -0.5),
        "b_rg": nrm(ks[11], (L, D_RNN), 0.01),
        "w_ig": nrm(ks[12], (L, N_RNN_BLOCKS, RNN_BLOCK, RNN_BLOCK), RNN_BLOCK ** -0.5),
        "b_ig": nrm(ks[14], (L, D_RNN), 0.01),
        "lru_lambda": lam,
        "w_o_attn": nrm(ks[15], (L, ATTN_WIDTH, D_MODEL), ATTN_WIDTH ** -0.5),
        "w_o_rnn": nrm(ks[16], (L, D_RNN, D_MODEL), D_RNN ** -0.5),
        "w_out": nrm(ks[17], (L, D_MODEL, D_MODEL), D_MODEL ** -0.5),
        "g_ffn": 1.0 + nrm(ks[18], (L, D_MODEL), 0.02),
        "w_up": nrm(ks[19], (L, D_MODEL, 2 * D_FF), D_MODEL ** -0.5),
        "conv_ffn_w": nrm(ks[20], (L, FFN_CONV, 2 * D_FF), FFN_CONV ** -0.5),
        "conv_ffn_b": nrm(ks[21], (L, 2 * D_FF), 0.01),
        "w_down": nrm(ks[22], (L, D_FF, D_MODEL), D_FF ** -0.5),
        "g_final": 1.0 + nrm(ks[23], (D_MODEL,), 0.02),
    }

def first_block(x, c, w_ada, b_ada, g_mix, w_in, b_in, rel_bias, conv_rnn_w, conv_rnn_b,
              w_rg, b_rg, w_ig, b_ig, lru_lambda, w_o_attn, w_o_rnn, w_out, g_ffn,
              w_up, conv_ffn_w, conv_ffn_b, w_down, g_final):
    B, S = x.shape[0], x.shape[1]
    cuts = []
    acc = 0
    for width in SPLITS[:-1]:
        acc += width
        cuts.append(acc)
    c_act = jax.nn.silu(c)
    h = x
    for l in range(DEPTH):
        mod = jnp.dot(c_act, w_ada[l]) + b_ada[l]
        sh1, sc1, ga1, sh2, sc2, ga2 = [m[:, None, :] for m in jnp.split(mod, 6, axis=-1)]

        xn = rms_norm(h, g_mix[l]) * (1.0 + sc1) + sh1
        proj = jnp.dot(xn, w_in[l]) + b_in[l]
        q, k, v, qi, ki, wi, xr, yr, gate_a, gate_b = jnp.split(proj, cuts, axis=-1)

        attn = dsa_attention(
            q.reshape(B, S, N_HEADS, HEAD_DIM),
            k.reshape(B, S, N_KV_HEADS, HEAD_DIM),
            v.reshape(B, S, N_KV_HEADS, HEAD_DIM),
            qi.reshape(B, S, IDX_HEADS, IDX_DIM), ki, wi, rel_bias)

        xr = causal_dwconv(xr, conv_rnn_w[l], conv_rnn_b[l])
        rnn = rg_lru(xr, w_rg[l], b_rg[l], w_ig[l], b_ig[l], lru_lambda[l]) * jax.nn.gelu(yr)

        merged = (jax.nn.sigmoid(gate_a) * jnp.dot(attn, w_o_attn[l])
                  + jax.nn.sigmoid(gate_b) * jnp.dot(rnn, w_o_rnn[l]))
        h = h + ga1 * jnp.dot(merged, w_out[l])

        xn = rms_norm(h, g_ffn[l]) * (1.0 + sc2) + sh2
        up = causal_dwconv(jnp.dot(xn, w_up[l]), conv_ffn_w[l], conv_ffn_b[l])
        val, gte = jnp.split(up, 2, axis=-1)
        h = h + ga2 * jnp.dot(jax.nn.silu(gte) * val, w_down[l])
    return rms_norm(h, g_final)


N_META = 16
HGRN_HEADS = 8
HGRN_EXPAND = 128
HGRN_FDIM = HGRN_HEADS * HGRN_EXPAND
HGRN_VDIM = D_MODEL
HGRN_HEAD_V = HGRN_VDIM // HGRN_HEADS
CONV_DIM = D_MODEL
CONV_WIDTH = 3
FFN_CONV_WIDTH = 3
CHUNK = 64
IN_SIZES = (HGRN_FDIM,
            HGRN_FDIM,
            HGRN_VDIM,
            HGRN_VDIM,
            CONV_DIM,
            CONV_DIM,
            CONV_DIM,
            D_MODEL,
            D_MODEL)
IN_TOTAL = sum(IN_SIZES)


def _split_points(sizes):
    pts, acc = [], 0
    for s in sizes[:-1]:
        acc += s
        pts.append(acc)
    return pts

def rmsnorm(x, w):
    xf = x.astype(jnp.float32)
    y = xf * lax.rsqrt(jnp.mean(xf * xf, axis=-1, keepdims=True) + EPS)
    return (y * w.astype(jnp.float32)).astype(x.dtype)

def causal_dwconv_2(x, w, b=None):
    K = w.shape[0]
    L = x.shape[1]
    xp = jnp.pad(x, ((0, 0), (K - 1, 0), (0, 0)))
    y = w[0] * xp[:, 0:L]
    for j in range(1, K):
        y = y + w[j] * xp[:, j:j + L]
    if b is not None:
        y = y + b
    return y

def layer_lower_bounds(lb_param):
    p = jax.nn.softmax(lb_param.astype(jnp.float32), axis=0)
    return jnp.cumsum(p, axis=0)[:DEPTH]

def hgrn2_chunked(q, k, v, logf):
    Bsz, H, T, DK = q.shape
    DV = v.shape[-1]
    n = T // CHUNK

    def to_chunks(a):
        return jnp.moveaxis(a.reshape(Bsz, H, n, CHUNK, a.shape[-1]), 2, 0)

    qc, kc, vc, gc = to_chunks(q), to_chunks(k), to_chunks(v), to_chunks(logf)
    causal = jnp.tril(jnp.ones((CHUNK, CHUNK), dtype=bool))[:, :, None]

    def step(S, inp):
        qb, kb, vb, gb = inp
        G = jnp.cumsum(gb, axis=-2)
        o_inter = jnp.einsum('bhtd,bhdv->bhtv', qb * jnp.exp(G), S)
        diff = G[:, :, :, None, :] - G[:, :, None, :, :]
        decay = jnp.exp(jnp.where(causal, diff, -jnp.inf))
        A = jnp.sum(qb[:, :, :, None, :] * kb[:, :, None, :, :] * decay, axis=-1)
        o = o_inter + jnp.einsum('bhts,bhsv->bhtv', A, vb)
        G_last = G[:, :, -1:, :]
        k_dec = kb * jnp.exp(G_last - G)
        S_new = jnp.exp(G_last[:, :, 0, :])[..., None] * S + jnp.einsum('bhsd,bhsv->bhdv', k_dec, vb)
        return S_new, o

    S0 = jnp.zeros((Bsz, H, DK, DV), jnp.float32)
    _, o = lax.scan(step, S0, (qc, kc, vc, gc))
    return jnp.moveaxis(o, 0, 2).reshape(Bsz, H, T, DV)

def hybrid_layer(h, lb, attn_norm_w, w_in, hgrn_norm_w, conv_w, w_out,
                 ffn_norm_w, w_up, ffn_conv_w, ffn_conv_b, w_down):
    Bsz, L, _ = h.shape
    dt = h.dtype
    u = rmsnorm(h, attn_norm_w)
    proj = u @ w_in
    q, f_raw, i_in, g_out, b_gate, c_gate, x_conv, gate_a, gate_b = jnp.split(
        proj, _split_points(IN_SIZES), axis=-1)

    q = jax.nn.silu(q.astype(jnp.float32))
    f = lb + (1.0 - lb) * jax.nn.sigmoid(f_raw.astype(jnp.float32))
    logf = jnp.log(f)
    k = 1.0 - f
    v = i_in.astype(jnp.float32)

    def heads(a):
        return jnp.transpose(a.reshape(Bsz, L, HGRN_HEADS, -1), (0, 2, 1, 3))

    pad = (-N_META) % CHUNK
    tpad = ((0, 0), (0, 0), (pad, 0), (0, 0))
    qh, kh, vh, gh = (jnp.pad(heads(a), tpad) for a in (q, k, v, logf))
    o = hgrn2_chunked(qh, kh, vh, gh)[:, :, pad:]
    o = jnp.transpose(o, (0, 2, 1, 3))
    o = rmsnorm(o, hgrn_norm_w).reshape(Bsz, L, HGRN_VDIM)
    y_a = (o * jax.nn.silu(g_out.astype(jnp.float32))).astype(dt)

    y_b = b_gate * causal_dwconv_2(c_gate * x_conv, conv_w)

    merged = jax.nn.sigmoid(gate_a) * y_a + jax.nn.sigmoid(gate_b) * y_b
    h = h + merged @ w_out

    u2 = rmsnorm(h, ffn_norm_w)
    a, val = jnp.split(u2 @ w_up, 2, axis=-1)
    a = causal_dwconv_2(a, ffn_conv_w, ffn_conv_b)
    h = h + (jax.nn.silu(a) * val) @ w_down
    return h

def second_inputs(seed: int = 0) -> dict:
    key = jax.random.key(seed)
    ks = jax.random.split(key, 16)
    f32 = jnp.float32
    nrm = lambda k, shape, s: jax.random.normal(k, shape, f32) * s
    return {
        "x": nrm(ks[0], (BATCH, SEQ, D_MODEL), 1.0),
        "meta_tokens": nrm(ks[1], (N_META, D_MODEL), 1.0),
        "lb_param": nrm(ks[2], (DEPTH + 1, HGRN_FDIM), 0.1),
        "attn_norm_w": 1.0 + nrm(ks[3], (DEPTH, D_MODEL), 0.02),
        "w_in": nrm(ks[4], (DEPTH, D_MODEL, IN_TOTAL), D_MODEL ** -0.5),
        "hgrn_norm_w": 1.0 + nrm(ks[5], (DEPTH, HGRN_HEAD_V), 0.02),
        "conv_w": nrm(ks[6], (DEPTH, CONV_WIDTH, CONV_DIM), CONV_WIDTH ** -0.5),
        "w_out": nrm(ks[7], (DEPTH, D_MODEL, D_MODEL), D_MODEL ** -0.5),
        "ffn_norm_w": 1.0 + nrm(ks[8], (DEPTH, D_MODEL), 0.02),
        "w_up": nrm(ks[9], (DEPTH, D_MODEL, 2 * D_FF), D_MODEL ** -0.5),
        "ffn_conv_w": nrm(ks[10], (DEPTH, FFN_CONV_WIDTH, D_FF), FFN_CONV_WIDTH ** -0.5),
        "ffn_conv_b": nrm(ks[11], (DEPTH, D_FF), 0.02),
        "w_down": nrm(ks[12], (DEPTH, D_FF, D_MODEL), D_FF ** -0.5),
        "final_norm_w": 1.0 + nrm(ks[13], (D_MODEL,), 0.02),
    }

def second_block(x, meta_tokens, lb_param, attn_norm_w, w_in, hgrn_norm_w, conv_w, w_out,
              ffn_norm_w, w_up, ffn_conv_w, ffn_conv_b, w_down, final_norm_w):
    Bsz = x.shape[0]
    meta = jnp.broadcast_to(meta_tokens.astype(x.dtype)[None], (Bsz, N_META, D_MODEL))
    h = jnp.concatenate([meta, x], axis=1)
    lbs = layer_lower_bounds(lb_param)
    for l in range(DEPTH):
        h = hybrid_layer(h, lbs[l], attn_norm_w[l], w_in[l], hgrn_norm_w[l], conv_w[l],
                         w_out[l], ffn_norm_w[l], w_up[l], ffn_conv_w[l], ffn_conv_b[l],
                         w_down[l])
    h = rmsnorm(h, final_norm_w)
    return h[:, N_META:]


def setup_inputs(seed=0):
    out = dict(first_inputs(seed))
    for name, value in second_inputs(seed + 1).items():
        if name != "x":
            out[name + "_2"] = value
    return out


def reference(
    x, c, w_ada, b_ada, g_mix, w_in, b_in, rel_bias, conv_rnn_w, conv_rnn_b, w_rg, b_rg, w_ig,
    b_ig, lru_lambda, w_o_attn, w_o_rnn, w_out, g_ffn, w_up, conv_ffn_w, conv_ffn_b, w_down,
    g_final, meta_tokens_2, lb_param_2, attn_norm_w_2, w_in_2, hgrn_norm_w_2, conv_w_2, w_out_2,
    ffn_norm_w_2, w_up_2, ffn_conv_w_2, ffn_conv_b_2, w_down_2, final_norm_w_2,
):
    x = first_block(
        x, c, w_ada, b_ada, g_mix, w_in, b_in, rel_bias, conv_rnn_w, conv_rnn_b, w_rg, b_rg,
        w_ig, b_ig, lru_lambda, w_o_attn, w_o_rnn, w_out, g_ffn, w_up, conv_ffn_w, conv_ffn_b,
        w_down, g_final,
    )
    return second_block(
        x, meta_tokens_2, lb_param_2, attn_norm_w_2, w_in_2, hgrn_norm_w_2, conv_w_2, w_out_2,
        ffn_norm_w_2, w_up_2, ffn_conv_w_2, ffn_conv_b_2, w_down_2, final_norm_w_2,
    )


_drawn_inputs = setup_inputs


def setup_inputs(seed=0):
    import zlib

    import numpy as np

    out = dict(_drawn_inputs(seed))
    spreads = {}
    factors = {'b_in': 3.155,
     'conv_rnn_b': 3.632,
     'b_rg': 23.412,
     'b_ig': 8.0,
     'g_ffn': 4.269,
     'conv_ffn_b': 8.0,
     'lb_param_2': 8.0,
     'attn_norm_w_2': 2.84,
     'hgrn_norm_w_2': 30.8,
     'ffn_norm_w_2': 13.705,
     'ffn_conv_b_2': 20.581,
     'final_norm_w_2': 7.687}
    for name, (base, spread) in spreads.items():
        noise = np.random.default_rng([zlib.crc32(name.encode()), seed]).standard_normal(out[name].shape)
        drawn = base * np.exp(spread * noise) if base else spread * noise
        out[name] = __import__('jax').numpy.asarray(drawn.astype(out[name].dtype))
    for name, factor in factors.items():
        out[name] = (out[name] * factor).astype(out[name].dtype)
    return out
```

```python
import numpy as np
import concourse.bass as bass
from concourse import mybir
from contextlib import ExitStack

F32 = mybir.dt.float32
F32R = mybir.dt.float32r
U32 = mybir.dt.uint32
ALU = mybir.AluOpType
ACT = mybir.ActivationFunctionType
P = 128

D = 1024
KC = D // P
S = 512
META = 16
T = META + S
PAD = P - META
TP = PAD + T
CH = TP // P
QT = S // P
NH, HD, TOPK = 8, 64, 128
FF = 2816
FC = FF // P
UNIT = KC * P
EPS = 1e-6
MASKED, TAKEN = -3.0e38, -3.4e38
LEVELS = [64, 32, 16, 8, 4, 2, 1]

U_QI, U_KI, U_Q, U_K, U_V, U_WI = 0, 4, 5, 9, 10, 11
U_RNN = 12
U_MRG = U_RNN + 2 * KC
U_OUT = U_MRG + 7 * (KC // 2)
U_UP = U_OUT + KC
U_DN = U_UP + 2 * FC
U_MIX2 = U_DN + 3 * KC
U_OUT2 = U_MIX2 + 9 * KC
U_UP2 = U_OUT2 + KC
U_DN2 = U_UP2 + 2 * FC
UNITS = U_DN2 + 3 * KC
G_PROJ = 0
G_RNN = 12
G_MRG = G_RNN + 2 * KC
G_OUT = G_MRG + 4 * KC
G_UP = G_OUT + KC
G_DN = G_UP + 2 * FC
G_MIX2 = G_DN + KC
G_OUT2 = G_MIX2 + 9 * KC
G_UP2 = G_OUT2 + KC
G_DN2 = G_UP2 + 2 * FC
RAW = 2
ADA_FIRST = 2 * KC

VEC = {}
_at = 0
for _n, _w in (("c", KC), ("b_ada", 6 * KC), ("g_mix", KC), ("b_qi", 4), ("b_ki", 1), ("b_q", 4), ("b_k", 1),
               ("rnn", 16 * KC), ("b_gates", 2 * KC), ("lam", KC), ("g_ffn", KC), ("ffn", 8 * FC), ("g_final", KC),
               ("lb0", KC), ("lb1", KC), ("attn_norm", KC), ("hgrn_norm", 1), ("conv2", 4 * KC), ("ffn_norm", KC),
               ("ffn2", 4 * FC), ("final2", KC)):
    VEC[_n] = _at
    _at += _w
NVEC = _at
C_ID, C_ONE, C_TRI = 0, P, 2 * P
C_LEV = 3 * P
C_RST = C_LEV + 64 * len(LEVELS)
NCONST = C_RST + TP
BIAS_W = S + P


def spans(n):
    return [(0, n)] if n <= 512 else [(0, (n // 2 + 1) // 2 * 2), ((n // 2 + 1) // 2 * 2, n - (n // 2 + 1) // 2 * 2)]


def region(n):
    return 0 if n <= 512 else 512 - spans(n)[0][1]


def build(nc, xT, metaT, vecs, rel, onehot, consts, rowbias, ada, gatew, units, scratch, out):
    with ExitStack() as ctx:
        def sb(name, shape, dt=F32, frame=ctx):
            return frame.enter_context(nc.sbuf_tensor(name, shape, dt))

        def sem(name):
            return ctx.enter_context(nc.semaphore(name))

        H = sb("H", [P, KC, T])
        XNhi = sb("XNhi", [P, KC, TP], F32R)
        XNlo = sb("XNlo", [P, KC, TP], F32R)
        raw = [sb(f"raw{s}", [P, UNIT]) for s in range(RAW)]
        Whi = [sb(f"Whi{s}", [P, KC, P], F32R) for s in range(2)]
        Wlo = [sb(f"Wlo{s}", [P, KC, P], F32R) for s in range(2)]
        V = sb("V", [P, NVEC])
        MOD = sb("MOD", [P, 6 * KC])
        AB1 = sb("AB1", [P, KC])
        AB2 = sb("AB2", [P, KC])
        CS = sb("CS", [P, KC])
        LAM = sb("LAM", [P, 8, KC])
        probe = sb("probe", [P, 32])
        ZERO = sb("ZERO", [P, KC])
        CON = sb("CON", [P, NCONST])
        sq = sb("sq", [P, 2, T])
        STD = sb("STD", [P, T])
        RSTD = sb("RSTD", [P, T])
        ident, ones, tri = CON[:, C_ID:C_ID + P], CON[:, C_ONE:C_ONE + P], CON[:, C_TRI:C_TRI + P]
        gp = [ctx.enter_context(nc.psum_tensor(f"gp{s}", [P, 1024], F32)) for s in range(2)]
        A45 = ctx.enter_context(nc.psum_tensor("A45", [P, 1024], F32))
        A67 = ctx.enter_context(nc.psum_tensor("A67", [P, 1024], F32))

        with ExitStack() as f:
            nt = sb("nt", [P, 2, T], frame=f)
            xf = sb("xf", [P, 2, T], frame=f)
        with ExitStack() as f:
            AThi = sb("AThi", [P, 4, S], F32R, f)
            ATlo = sb("ATlo", [P, 4, S], F32R, f)
            with ExitStack() as fa:
                QI = sb("QI", [P, 4, S], frame=fa)
                KI = sb("KI", [P, S], frame=fa)
                Q = sb("Q", [P, 4, S], frame=fa)
                K = sb("K", [P, S], frame=fa)
                VT = sb("VT", [P, QT, P], frame=fa)
                WI = sb("WI", [P, QT, NH], frame=fa)
                BIAS = sb("BIAS", [P, NH, S], frame=fa)
                PR = sb("PR", [P, 2, NH, S], frame=fa)
                SC = [None] + [sb(f"SC{i}", [P, (i + 1) * P], frame=fa) for i in range(1, QT)]
                NEG = [tri] + SC[1:]
                RL = sb("RL", [P, 2, S], frame=fa)
                PTs = sb("PTs", [P, 2, S], frame=fa)
                m8 = sb("m8", [P, 8], frame=fa)
                mx = sb("mx", [P, 2, NH], frame=fa)
                nmx = sb("nmx", [P, 2, NH], frame=fa)
                rs = sb("rs", [P, 2, NH], frame=fa)
                rr = sb("rr", [P, 2, NH], frame=fa)
                RBV = sb("RBV", [P, P + NH], frame=fa)
                OH = PR[0:32, 0, 0:2, :].rearrange("p h s -> p (h s)")[:, 0:BIAS_W]
                RB = PR[0:NH, 1, 0:2, :].rearrange("p h s -> p (h s)")[:, 0:BIAS_W]
                REL = sb("REL", [32, NH], frame=fa)
                AW = [sb(f"AW{s}", [P, UNIT], frame=fa) for s in range(2)]
            RNhi = sb("RNhi", [P, KC, S], F32R, f)
            RNlo = sb("RNlo", [P, KC, S], F32R, f)
            with ExitStack() as fr:
                XR = sb("XR", [P, 3 + S], frame=fr)
                XC, GY, RG, IG, DA, TH, A2, M2, MU, U1, UU, HS, RF = [
                    sb(f"rnn_{n}", [P, S], frame=fr) for n in
                    ("xc", "gelu", "r", "i", "a", "tanh", "a2", "m2", "mult", "u1", "u", "h", "out")]
                WG = sb("WG", [P, 2 * P], frame=fr)
            with ExitStack() as fm:
                MGhi = sb("MGhi", [P, KC, S], F32R, fm)
                MGlo = sb("MGlo", [P, KC, S], F32R, fm)
                SG = sb("SG", [P, 4, S], frame=fm)
                M1 = sb("M1", [P, 2, S], frame=fm)
                MB = sb("MB", [P, S], frame=fm)
                MF = sb("MF", [P, S], frame=fm)
        with ExitStack() as f:
            AChi = sb("AChi", [P, FC, S], F32R, f)
            AClo = sb("AClo", [P, FC, S], F32R, f)
            YV, YG, SL, AF = [sb(f"ffn_{n}", [P, S], frame=f) for n in ("val", "gate", "silu", "act")]
        with ExitStack() as f:
            M2hi = sb("M2hi", [P, KC, T], F32R, f)
            M2lo = sb("M2lo", [P, KC, T], F32R, f)
            HF, HL, HQ, HK, HG, EG, QG = [sb(f"h_{n}", [P, TP], frame=f) for n in
                                          ("sig", "logf", "q", "k", "G", "expG", "qG")]
            HV = sb("HV", [P, CH, P], frame=f)
            DD = sb("DD", [P, 2, TP], frame=f)
            EE = sb("EE", [P, 2, TP], frame=f)
            XX = sb("XX", [P, 2, TP], frame=f)
            AT2 = sb("AT2", [P, CH, P], frame=f)
            KDT = sb("KDT", [P, CH - 1, P], frame=f)
            ST = sb("ST", [P, CH - 1, P], frame=f)
            CG, BG, SO, SA, SB2, SQ, ON, YB, MF2, HST, HRS = [sb(f"h_{n}", [P, T], frame=f) for n in
                                                    ("cg", "bg", "silu_g", "sig_a", "sig_b", "sq", "on", "yb", "mf",
                                                     "std", "rstd")]
            CX = sb("CX", [P, 2 + T], frame=f)

        small_in = sem("small_in")
        x_in = sem("x_in")
        bias_saved = sem("bias_saved")
        bias_in = sem("bias_in")
        raw_in = [sem(f"raw_in{s}") for s in range(RAW)]
        ada_in = [sem(f"ada_in{s}") for s in range(2)]
        gate_in = sem("gate_in")
        hi_made = sem("hi_made")
        weights_ready = sem("weights_ready")
        unit_done = sem("unit_done")
        gp_free = [sem(f"gp_free{s}") for s in range(2)]
        cleared = sem("cleared")
        rb_mm, rb_copied = sem("rb_mm"), sem("rb_copied")
        silu_c, ada_done, mod_ready = sem("silu_c"), sem("ada_done"), sem("mod_ready")
        lam_neg, lam_exp, lam_done = sem("lam_neg"), sem("lam_exp"), sem("lam_done")
        lb_max, lb_exp, lb_done = sem("lb_max"), sem("lb_exp"), sem("lb_done")
        sq_ready, stat_mm, std_ready = sem("sq_ready"), sem("stat_mm"), sem("std_ready")
        nt_ready, xf_ready, xn_ready = sem("nt_ready"), sem("xf_ready"), sem("xn_ready")
        h_ready, out_ready, out_saved = sem("h_ready"), sem("out_ready"), sem("out_saved")
        proj_out, v_ready, wi_ready = sem("proj_out"), sem("v_ready"), sem("wi_ready")
        score_mm, relu_done, score_acc, sel_done = sem("score_mm"), sem("relu_done"), sem("score_acc"), sem("sel_done")
        logit_mm, logit_out, nmx_ready = sem("logit_mm"), sem("logit_out"), sem("nmx_ready")
        exp_done, p_ready, pt_mm, pt_copied = sem("exp_done"), sem("p_ready"), sem("pt_mm"), sem("pt_copied")
        pv_mm, at_hi, at_done = sem("pv_mm"), sem("at_hi"), sem("at_done")
        xr_pad, conv_first, xc_ready, gelu_ready = sem("xr_pad"), sem("conv_first"), sem("xc_ready"), sem("gelu_ready")
        gate_mm, ig_ready, a_ready, m2_ready = sem("gate_mm"), sem("ig_ready"), sem("a_ready"), sem("m2_ready")
        mult_ready, rnn_done = sem("mult_ready"), sem("rnn_done")
        sg_ready, merge_done = sem("sg_ready"), sem("merge_done")
        yv_first, yg_first, yg_ready, silu_ready, act_done = (sem("yv_first"), sem("yg_first"), sem("yg_ready"),
                                                              sem("silu_ready"), sem("act_done"))
        ya_first, ya_ready, silu2_ready, act2_done = sem("ya_first"), sem("ya_ready"), sem("silu2_ready"), sem("act2_done")
        pads2 = sem("pads2")
        sf_ready, lf_ready, hq_ready, hv_ready = sem("sf_ready"), sem("lf_ready"), sem("hq_ready"), sem("hv_ready")
        f_ready, d_ready, e_ready, lx_ready = sem("f_ready"), sem("d_ready"), sem("e_ready"), sem("lx_ready")
        lev_mm, lev_out = sem("lev_mm"), sem("lev_out")
        kdt_mm, kdt_ready, state_mm, state_ready = sem("kdt_mm"), sem("kdt_ready"), sem("state_mm"), sem("state_ready")
        eg_ready, qg_ready, o_mm, osq_ready, ostat_mm = (sem("eg_ready"), sem("qg_ready"), sem("o_mm"), sem("osq_ready"),
                                                         sem("ostat_mm"))
        ostd_ready, on_ready, cg_ready, cx_ready = sem("ostd_ready"), sem("on_ready"), sem("cg_ready"), sem("cx_ready")
        yb_first, side_ready, mix2_done = sem("yb_first"), sem("side_ready"), sem("mix2_done")

        def vec(name, k, w=1):
            return V[:, bass.ds(VEC[name] + k, w)]

        def slot_free(g, c=0):
            return (g + c) // 2 + 1

        NORMS = [dict(c0=META, n=S, feeds=0, h0=None), dict(c0=META, n=S, feeds=1, h0=0),
                 dict(c0=META, n=S, feeds=None, h0=KC), dict(c0=0, n=T, feeds=2, h0=2 * KC),
                 dict(c0=META - 2, n=S + 2, feeds=3, h0=3 * KC), dict(c0=META, n=S, feeds=None, h0=4 * KC)]

        def scale_bias(m, k):
            return {0: (AB1[:, k:k + 1], MOD[:, k:k + 1]), 1: (AB2[:, k:k + 1], MOD[:, 3 * KC + k:3 * KC + k + 1]),
                    3: (vec("attn_norm", k), ZERO[:, k:k + 1]), 4: (vec("ffn_norm", k), ZERO[:, k:k + 1])}[m]

        one_ahead = [xc_ready, rnn_done, merge_done, act_done, f_ready, qg_ready, o_mm, mix2_done, act2_done, lx_ready,
                     ig_ready, ostd_ready, on_ready, gate_mm]

        block = ctx.enter_context(nc.Block())

        @block.sync
        def _(sp):
            sp.dma_start(V[:, :], vecs).then_inc(small_in, 16)
            sp.dma_start(CON[:, :], consts).then_inc(small_in, 16)
            sp.dma_start(REL[:, :], rel).then_inc(small_in, 16)
            sp.dma_start(OH, onehot).then_inc(small_in, 16)
            sp.dma_start(RBV[:, :], rowbias.partition_broadcast(P)).then_inc(small_in, 16)
            sp.dma_start(H[:, :, META:T], xT).then_inc(x_in, 16)
            sp.dma_start(H[:, :, 0:META], metaT).then_inc(x_in, 16)

            def load_ada(first, last):
                with sp.Fori(first // 2, last // 2) as i:
                    for s in range(2):
                        sp.wait_ge(ada_done, i * 2 + s + 1)
                        sp.dma_start(AW[s][:, :], ada[bass.ds(i * 2 + s, 1), :, :]).then_inc(ada_in[s], 16)

            def load_units(first, last):
                with sp.Fori(first // RAW, last // RAW) as i:
                    for s in range(RAW):
                        sp.wait_ge(weights_ready, i * RAW + s + 1)
                        sp.dma_start(raw[s][:, :], units[bass.ds(i * RAW + s, 1), :, :]).then_inc(raw_in[s], 16)

            load_ada(0, ADA_FIRST)
            load_units(0, U_RNN)
            sp.wait_ge(rb_copied, 1)
            sp.dma_start(scratch, RB.rearrange("h (o m) -> h o m", o=1).to_broadcast([NH, P, BIAS_W])).then_inc(bias_saved, 16)
            sp.wait_ge(bias_saved, 16)
            sp.dma_start(BIAS[:, :, :], bass.AP(scratch.tensor, P - 1, [[BIAS_W - 1, P], [P * BIAS_W, NH], [1, S]])).then_inc(bias_in, 16)
            load_ada(ADA_FIRST, 6 * KC)
            load_units(U_RNN, UNITS)
            for k in range(KC):
                sp.wait_ge(out_ready, k + 1)
                sp.dma_start(out[:, k, :], H[:, k, META:T]).then_inc(out_saved, 16)
            sp.wait_ge(out_saved, 16 * KC)

        @block.gpsimd
        def _(pool):
            pool.memset(ZERO[:, :], 0.0).then_inc(weights_ready, RAW)
            pool.memset(XNhi[:, :, 0:PAD].bitcast(F32), 0.0).then_inc(cleared, 1)
            pool.memset(XNlo[:, :, 0:PAD].bitcast(F32), 0.0).then_inc(cleared, 1)
            with pool.Fori(0, UNITS // 2) as i:
                for s in range(2):
                    u = i * 2 + s
                    src = raw[s][:, :]
                    hi, lo = [w[s][:, :, :].rearrange("p k n -> p (k n)") for w in (Whi, Wlo)]
                    pool.wait_ge(raw_in[s], i * 16 + 16)
                    pool.wait_ge(unit_done, u + 1)
                    pool.tensor_tensor(probe[0:1, 0:1], src[0:1, 0:1], src[0:1, 0:1], ALU.add)
                    pool.tensor_scalar(hi, src, 1.0, 1.0, ALU.mult, ALU.mult).then_inc(hi_made, 1)
                    pool.wait_ge(hi_made, u + 1)
                    pool.tensor_tensor(lo, src, hi.bitcast(F32), ALU.subtract).then_inc(weights_ready, 1)

        @block.tensor
        def _(pe):
            def three(dst, s, k, rhi, rlo, start, stop):
                pe.matmul(dst, Whi[s][:, k, :], rhi, start=start, stop=False)
                pe.matmul(dst, Whi[s][:, k, :], rlo, start=False, stop=False)
                return pe.matmul(dst, Wlo[s][:, k, :], rhi, start=False, stop=stop)

            def unit(u, s, dst, n, hi, lo, c0, ks, first=0, last=None, arrive=None):
                pe.wait_ge(weights_ready, u + 1 + RAW)
                base = region(n)
                for j, k in enumerate(ks):
                    if arrive is not None:
                        pe.wait_ge(xn_ready, arrive + j + 1)
                    kc = first + j
                    for a, w in spans(n):
                        mm = three(dst[:, base + a:base + a + w], s, k, hi[:, kc, c0 + a:c0 + a + w],
                                   lo[:, kc, c0 + a:c0 + a + w], kc == 0, kc == last)
                return mm

            def unit_rows(u, s, dst, tiles, c0, w):
                pe.wait_ge(weights_ready, u + 1 + RAW)
                for t in range(tiles):
                    for k in range(KC):
                        o = dst[:, t * P:t * P + w]
                        xh, xl = [x[:, k, c0 + t * P:c0 + (t + 1) * P] for x in (XNhi, XNlo)]
                        pe.matmul(o, xh, Whi[s][:, k, 0:w], start=(k == 0), stop=False)
                        pe.matmul(o, xl, Whi[s][:, k, 0:w], start=False, stop=False)
                        mm = pe.matmul(o, xh, Wlo[s][:, k, 0:w], start=False, stop=(k == KC - 1))
                return mm

            def stats(m):
                n, base = NORMS[m]["n"], region(NORMS[m]["n"])
                if m:
                    pe.wait_ge(std_ready, m)
                for k in range(KC):
                    pe.wait_ge(sq_ready, KC * m + k + 1)
                    for a, w in spans(n):
                        mm = pe.matmul(A67[:, base + a:base + a + w], ones, sq[:, k % 2, a:a + w],
                                       start=(k == 0), stop=(k == KC - 1))
                    mm.then_inc(stat_mm, 1)

            def modulation(first, last):
                with pe.Fori(first // 4, last // 4) as i:
                    for c in range(4):
                        pe.wait_ge(ada_in[c % 2], i * 32 + 16 * (c // 2) + 16)
                        for k in range(KC):
                            mm = pe.matmul(gp[1][:, bass.ds(512 + i * 4 + c, 1)], AW[c % 2][:, k * P:(k + 1) * P],
                                           CS[:, k:k + 1], start=(k == 0), stop=(k == KC - 1))
                        mm.then_inc(ada_done, 1)

            pe.wait_ge(small_in, 16 * 5)
            pe.matmul(A67[0:NH, 0:512], REL[:, :], OH[:, 0:512], start=True, stop=True)
            pe.matmul(A67[0:NH, 512:BIAS_W], REL[:, :], OH[:, 512:BIAS_W], start=True, stop=True).then_inc(rb_mm, 1)
            pe.wait_ge(silu_c, 1)
            modulation(0, ADA_FIRST)
            pe.wait_ge(rb_copied, 1)
            stats(0)

            pe.wait_ge(cleared, 2)
            for u in range(12):
                pe.wait_ge(gp_free[u % 2], slot_free(u))
                if u < U_V:
                    unit(u, u % 2, gp[u % 2], S, XNhi, XNlo, P, range(KC), last=KC - 1,
                         arrive=0 if u == 0 else None).then_inc(unit_done, 1)
                else:
                    unit_rows(u, u % 2, gp[u % 2], QT, P, P if u == U_V else NH).then_inc(unit_done, 1)

            pe.wait_ge(proj_out, 5)
            n = 0
            for i in range(1, QT):
                for h in range(NH):
                    if n >= 2:
                        pe.wait_ge(relu_done, n - 1)
                    hp = (h % 2) * HD
                    pe.matmul(A45[:, (n % 2) * 512:(n % 2) * 512 + (i + 1) * P], QI[hp:hp + HD, h // 2, i * P:(i + 1) * P],
                              KI[hp:hp + HD, 0:(i + 1) * P], start=True, stop=True).then_inc(score_mm, 1)
                    n += 1
            modulation(ADA_FIRST, 6 * KC)

            pe.wait_ge(proj_out, 10)
            pe.wait_ge(relu_done, n)
            pe.wait_ge(v_ready, 1)

            def logits(i):
                for h in range(NH):
                    c = i * NH + h
                    if c >= 2:
                        pe.wait_ge(logit_out, c - 1)
                    hp = (h // 4) * HD
                    pe.matmul(A45[:, (c % 2) * 512:(c % 2) * 512 + (i + 1) * P], Q[hp:hp + HD, h % 4, i * P:(i + 1) * P],
                              K[hp:hp + HD, 0:(i + 1) * P], start=True, stop=True).then_inc(logit_mm, 1)

            def values(i, t0):
                pe.wait_ge(p_ready, i + 1)
                if i >= 1:
                    pe.wait_ge(at_done, i)
                blocks = [(kb, g) for kb in range(i + 1) for g in range(2)]
                for b in range(len(blocks) + 1):
                    if b < len(blocks):
                        kb, g = blocks[b]
                        if t0 + b >= 2:
                            pe.wait_ge(pt_copied, t0 + b - 1)
                        for j in range(4):
                            mm = pe.transpose(A67[:, g * 512 + j * P:g * 512 + (j + 1) * P],
                                              PR[:, i % 2, g * 4 + j, kb * P:(kb + 1) * P], ident)
                        mm.then_inc(pt_mm, 1)
                    if b >= 1:
                        kb, g = blocks[b - 1]
                        pe.wait_ge(pt_copied, t0 + b)
                        pe.matmul(gp[0][g * HD:(g + 1) * HD, 512:1024], VT[:, kb, g * HD:(g + 1) * HD], PTs[:, g, :],
                                  start=(kb == 0), stop=(kb == i)).then_inc(pv_mm, 1)
                return t0 + len(blocks)

            t0 = 0
            logits(0)
            for i in range(QT):
                if i + 1 < QT:
                    logits(i + 1)
                t0 = values(i, t0)

            pe.wait_ge(at_done, QT)
            with pe.Fori(0, KC) as i:
                for c in range(2):
                    pe.wait_ge(gp_free[c], slot_free(G_RNN) + i)
                    unit(U_RNN + i * 2 + c, c, gp[c], S, XNhi, XNlo, P, range(KC), last=KC - 1).then_inc(unit_done, 1)
                pe.wait_ge(gate_in, i * 16 + 16)
                pe.wait_ge(xc_ready, i + 2)
                pe.wait_ge(ig_ready, i * 2 + 1)
                for g in range(2):
                    pe.matmul(A45[:, g * 512:(g + 1) * 512], WG[:, g * P:(g + 1) * P], XC[:, :],
                              start=True, stop=True).then_inc(gate_mm, 1)

            with pe.Fori(0, 2) as i:
                for pr in range(2):
                    for c in range(4):
                        pe.wait_ge(gp_free[c % 2], slot_free(G_MRG, pr * 8 + c) + i * 8)
                        unit(U_MRG + i * 14 + pr * 7 + c, (pr * 7 + c) % 2, gp[c % 2], S, XNhi, XNlo, P, range(KC),
                             last=KC - 1).then_inc(unit_done, 1)
                    for q in range(2):
                        pe.wait_ge(gp_free[q], slot_free(G_MRG, pr * 8 + 4 + q) + i * 8)
                        mm = unit(U_MRG + i * 14 + pr * 7 + 4, (pr * 7 + 4) % 2, gp[q], S, AThi, ATlo, 0,
                                  range(4 * q, 4 * q + 4), last=3)
                    mm.then_inc(unit_done, 1)
                    pe.wait_ge(rnn_done, KC + 1)
                    for q in range(2):
                        pe.wait_ge(gp_free[q], slot_free(G_MRG, pr * 8 + 6 + q) + i * 8)
                        unit(U_MRG + i * 14 + pr * 7 + 5 + q, (pr * 7 + 5 + q) % 2, gp[q], S, RNhi, RNlo, 0, range(KC),
                             last=KC - 1).then_inc(unit_done, 1)

            def plain(u0, g0, hi, lo, c0, n, count):
                with pe.Fori(0, count // 2) as i:
                    for c in range(2):
                        pe.wait_ge(gp_free[c], slot_free(g0) + i)
                        unit(u0 + i * 2 + c, c, gp[c], n, hi, lo, c0, range(KC), last=KC - 1).then_inc(unit_done, 1)

            def down(u0, g0):
                with pe.Fori(0, KC // 2) as i:
                    for c in range(2):
                        pe.wait_ge(gp_free[c], slot_free(g0) + i)
                        for t in range(3):
                            unit(u0 + i * 6 + c * 3 + t, (c * 3 + t) % 2, gp[c], S, AChi, AClo, 0,
                                 range(min(KC, FC - t * KC)), first=t * KC, last=FC - 1).then_inc(unit_done, 1)

            pe.wait_ge(merge_done, KC + 1)
            plain(U_OUT, G_OUT, MGhi, MGlo, 0, S, KC)
            stats(1)
            pe.wait_ge(xn_ready, 2 * KC)
            plain(U_UP, G_UP, XNhi, XNlo, P, S, 2 * FC)
            pe.wait_ge(act_done, FC + 1)
            down(U_DN, G_DN)
            stats(2)

            stats(3)
            pe.wait_ge(xn_ready, 3 * KC)
            with pe.Fori(0, KC // 2) as i:
                for hh in range(2):
                    def gemm(c):
                        g = (hh * 9 + c) % 2
                        pe.wait_ge(gp_free[g], slot_free(G_MIX2, hh * 9 + c) + i * 9)
                        u = U_MIX2 + i * 18 + hh * 9 + c
                        if c == 2:
                            unit_rows(u, g, gp[g], CH, 0, P).then_inc(unit_done, 1)
                        else:
                            unit(u, g, gp[g], T, XNhi, XNlo, PAD, range(KC), last=KC - 1).then_inc(unit_done, 1)

                    def level(l):
                        b = LEVELS[l]
                        pe.wait_ge(lx_ready, i * 18 + hh * 9 + l + 2)
                        if l >= 2:
                            pe.wait_ge(lev_out, i * 16 + hh * 8 + l - 1)
                        for c in range(CH):
                            x = XX[:, l % 2, c * P:(c + 1) * P]
                            up = x.rearrange("p (j two b) -> p j two b", two=2, b=b)[:, :, 1, :]
                            mm = pe.matmul(A45[:, (l % 2) * 512 + c * 64:(l % 2) * 512 + (c + 1) * 64], x, up,
                                           start=True, stop=True)
                        mm.then_inc(lev_mm, 1)

                    gemm(0)
                    gemm(1)
                    gemm(2)
                    gemm(3)
                    pe.wait_ge(ostd_ready, i * 2 + hh + 1)
                    level(0)
                    level(1)
                    gemm(4)
                    level(2)
                    level(3)
                    gemm(5)
                    level(4)
                    level(5)
                    gemm(6)
                    level(6)
                    pe.wait_ge(lx_ready, i * 18 + hh * 9 + 8 + 1)
                    pe.wait_ge(on_ready, i * 2 + hh + 1)
                    for a, w in ((0, 512), (512, TP - 512)):
                        mm = pe.matmul(A67[:, a:a + w], ones, XX[:, 1, a:a + w], start=True, stop=True)
                    mm.then_inc(lev_mm, 1)
                    gemm(7)
                    pe.wait_ge(lx_ready, i * 18 + hh * 9 + 9 + 1)
                    pe.wait_ge(lev_out, i * 16 + hh * 8 + 8)
                    for c in range(CH - 1):
                        mm = pe.transpose(A67[:, c * P:(c + 1) * P], XX[:, 0, c * P:(c + 1) * P], ident)
                    mm.then_inc(kdt_mm, 1)
                    pe.wait_ge(kdt_ready, i * 2 + hh + 1)
                    pe.wait_ge(hv_ready, i * 2 + hh + 1)
                    for c in range(CH - 1):
                        mm = pe.matmul(A45[:, c * P:(c + 1) * P], KDT[:, c, :], HV[:, c, :], start=True, stop=True)
                    mm.then_inc(state_mm, 1)
                    gemm(8)
                    pe.wait_ge(state_ready, i * 2 + hh + 1)
                    pe.wait_ge(qg_ready, i * 2 + hh + 2)
                    for c in range(CH):
                        o = A67[:, c * P:(c + 1) * P]
                        mm = pe.matmul(o, HV[:, c, :], AT2[:, c, :], start=True, stop=(c == 0))
                        if c:
                            mm = pe.matmul(o, ST[:, c - 1, :], QG[:, c * P:(c + 1) * P], start=False, stop=True)
                    mm.then_inc(o_mm, 1)
                    pe.wait_ge(osq_ready, i * 2 + hh + 1)
                    b0 = region(T)
                    for a, w in spans(T):
                        mm = pe.matmul(A45[:, b0 + a:b0 + a + w], ones, SQ[:, a:a + w], start=True, stop=True)
                    mm.then_inc(ostat_mm, 1)

            pe.wait_ge(mix2_done, KC + 1)
            plain(U_OUT2, G_OUT2, M2hi, M2lo, 0, T, KC)
            stats(4)
            pe.wait_ge(xn_ready, 4 * KC)
            with pe.Fori(0, FC) as i:
                for c, (n, c0) in enumerate(((S + 2, P - 2), (S, P))):
                    pe.wait_ge(gp_free[c], slot_free(G_UP2) + i)
                    unit(U_UP2 + i * 2 + c, c, gp[c], n, XNhi, XNlo, c0, range(KC), last=KC - 1).then_inc(unit_done, 1)
            pe.wait_ge(act2_done, FC + 1)
            down(U_DN2, G_DN2)
            stats(5)

        @block.scalar
        def _(act):
            def norm_stats(m):
                q = NORMS[m]
                for k in range(KC):
                    if q["h0"] is None:
                        if k == 0:
                            act.wait_ge(x_in, 32)
                    else:
                        act.wait_ge(h_ready, q["h0"] + k + 1)
                    if KC * m + k >= 2:
                        act.wait_ge(stat_mm, KC * m + k - 1)
                    act.activation(sq[:, k % 2, 0:q["n"]], H[:, k, q["c0"]:q["c0"] + q["n"]],
                                   ACT.Square).then_inc(sq_ready, 1)
                act.wait_ge(stat_mm, KC * (m + 1))
                b = region(q["n"])
                act.activation(STD[:, 0:q["n"]], A67[:, b:b + q["n"]], ACT.Sqrt, bias=EPSC, scale=1.0 / D).then_inc(std_ready, 1)

            def norm_apply(m):
                q = NORMS[m]
                f = q["feeds"]
                for k in range(KC):
                    act.wait_ge(nt_ready, KC * f + k + 1)
                    if KC * f + k >= 2:
                        act.wait_ge(xn_ready, KC * f + k - 1)
                    a, b = scale_bias(m, k)
                    act.activation(xf[:, k % 2, 0:q["n"]], nt[:, k % 2, 0:q["n"]], ACT.Identity, bias=b,
                                   scale=a).then_inc(xf_ready, 1)

            EPSC = LAM[:, 7, 0:1]
            act.wait_ge(small_in, 16 * 5)
            act.activation(CS[:, :], vec("c", 0, KC), ACT.Silu).then_inc(silu_c, 1)
            act.wait_ge(rb_mm, 1)
            act.activation(RB, A67[0:NH, 0:BIAS_W], ACT.Copy).then_inc(rb_copied, 1)
            act.wait_ge(lam_neg, 1)
            act.activation(LAM[:, 1, :], LAM[:, 0, :], ACT.Exp).then_inc(lam_exp, 1)
            act.wait_ge(lb_max, 2)
            act.activation(LAM[:, 5, :], LAM[:, 3, :], ACT.Exp).then_inc(lb_exp, 1)
            act.activation(LAM[:, 6, :], LAM[:, 4, :], ACT.Exp).then_inc(lb_exp, 1)
            norm_stats(0)
            act.wait_ge(mod_ready, 2)
            norm_apply(0)

            outs = ([(QI[:, j, :], vec("b_qi", j)) for j in range(4)] + [(KI[:, :], vec("b_ki", 0))]
                    + [(Q[:, j, :], vec("b_q", j)) for j in range(4)] + [(K[:, :], vec("b_k", 0))])
            for u, (o, b) in enumerate(outs):
                act.wait_ge(unit_done, u + 1 + 2)
                act.activation(o, gp[u % 2][:, 0:S], ACT.Identity, bias=b).then_inc(gp_free[u % 2], 1)
                act.drain().then_inc(proj_out, 1)

            n = 0
            for i in range(1, QT):
                for h in range(NH):
                    act.wait_ge(score_mm, n + 1)
                    if n >= 2:
                        act.wait_ge(score_acc, n - 1)
                    act.activation(RL[:, n % 2, 0:(i + 1) * P], A45[:, (n % 2) * 512:(n % 2) * 512 + (i + 1) * P],
                                   ACT.Relu, scale=HD ** -0.5).then_inc(relu_done, 1)
                    n += 1

            t0 = 0
            for i in range(QT):
                w = (i + 1) * P
                act.wait_ge(nmx_ready, i + 1)
                for h in range(NH):
                    act.activation(PR[:, i % 2, h, 0:w], PR[:, i % 2, h, 0:w], ACT.Exp, bias=nmx[:, i % 2, h:h + 1],
                                   accum_out=rs[:, i % 2, h:h + 1]).then_inc(exp_done, 1)
                for b in range(2 * (i + 1)):
                    g = b % 2
                    act.wait_ge(pt_mm, t0 + b + 1)
                    if t0 + b >= 2:
                        act.wait_ge(pv_mm, t0 + b - 1)
                    act.activation(PTs[:, g, :], A67[:, g * 512:(g + 1) * 512], ACT.Copy).then_inc(pt_copied, 1)
                t0 += 2 * (i + 1)
                act.wait_ge(pv_mm, t0)
                act.activation(AThi[:, :, i * P:(i + 1) * P], gp[0][:, 512:1024].rearrange("p (j q) -> p j q", j=4),
                               ACT.Copy).then_inc(at_hi, 1)

            act.wait_ge(at_done, QT)
            act.wait_ge(xr_pad, 1)
            act.wait_ge(lam_done, 1)
            with act.Fori(0, KC) as i:
                def rv(c):
                    return V[:, bass.ds(VEC["rnn"] + i * 16 + c, 1)]
                act.wait_ge(gate_mm, i * 2 + 1)
                act.dma_start(WG[:, :], gatew[bass.ds(i, 1), :, :]).then_inc(gate_in, 16)
                act.wait_ge(unit_done, U_RNN + i * 2 + 1 + 2)
                act.wait_ge(xc_ready, i + 1)
                act.activation(XR[:, 3:3 + S], gp[0][:, 0:S], ACT.Identity, bias=rv(0)).then_inc(gp_free[0], 1)
                act.drain()
                act.wait_ge(rnn_done, i + 1)
                act.activation(XC[:, :], XR[:, 3:3 + S], ACT.Identity, bias=rv(6), scale=rv(5)).then_inc(conv_first, 1)
                act.wait_ge(unit_done, U_RNN + i * 2 + 2 + 2)
                act.activation(GY[:, :], gp[1][:, 0:S], ACT.Gelu_apprx_tanh, bias=rv(1)).then_inc(gp_free[1], 1)
                act.drain().then_inc(gelu_ready, 1)
                act.wait_ge(gate_mm, i * 2 + 3)
                act.activation(RG[:, :], A45[:, 0:512], ACT.Sigmoid, bias=rv(7)).then_inc(ig_ready, 1)
                act.activation(IG[:, :], A45[:, 512:1024], ACT.Sigmoid, bias=rv(8)).then_inc(ig_ready, 1)
                act.drain()
                act.activation(DA[:, :], RG[:, :], ACT.Exp, scale=LAM[:, 2, bass.ds(i, 1)])
                act.activation(TH[:, :], RG[:, :], ACT.Tanh, scale=LAM[:, 0, bass.ds(i, 1)])
                act.drain()
                act.activation(A2[:, :], DA[:, :], ACT.Square).then_inc(a_ready, 1)
                act.wait_ge(m2_ready, i + 1)
                act.activation(MU[:, :], M2[:, :], ACT.Sqrt).then_inc(mult_ready, 1)

            with act.Fori(0, 2) as i:
                for pr in range(2):
                    for c in range(4):
                        act.wait_ge(unit_done, U_MRG + i * 14 + pr * 7 + c + 1 + 2)
                        act.wait_ge(merge_done, i * 4 + pr * 2 + 1)
                        act.activation(SG[:, c, :], gp[c % 2][:, 0:S], ACT.Sigmoid,
                                       bias=V[:, bass.ds(VEC["b_gates"] + i * 8 + pr * 4 + c, 1)]).then_inc(gp_free[c % 2], 1)
                        act.drain().then_inc(sg_ready, 1)

            norm_stats(1)
            norm_apply(1)
            with act.Fori(0, FC) as i:
                def fv(c):
                    return V[:, bass.ds(VEC["ffn"] + i * 8 + c, 1)]
                act.wait_ge(unit_done, U_UP + i * 2 + 1 + 2)
                act.wait_ge(act_done, i + 1)
                act.activation(YV[:, :], gp[0][:, 0:S], ACT.Identity, bias=fv(3), scale=fv(2)).then_inc(yv_first, 1)
                act.wait_ge(unit_done, U_UP + i * 2 + 2 + 2)
                act.activation(YG[:, :], gp[1][:, 0:S], ACT.Identity, bias=fv(7), scale=fv(6)).then_inc(yg_first, 1)
                act.wait_ge(yg_ready, i + 1)
                act.activation(SL[:, :], YG[:, :], ACT.Silu).then_inc(silu_ready, 1)
            norm_stats(2)

            norm_stats(3)
            norm_apply(3)
            act.wait_ge(pads2, 1)
            act.wait_ge(lb_done, 1)
            with act.Fori(0, KC // 2) as i:
                for hh in range(2):
                    h = i * 2 + hh
                    b0 = region(T)

                    def psum(c):
                        g = (hh * 9 + c) % 2
                        act.wait_ge(unit_done, U_MIX2 + i * 18 + hh * 9 + c + 1 + 2)
                        return gp[g][:, b0:b0 + T], gp_free[g]

                    def decay(l, b):
                        act.wait_ge(d_ready, i * 16 + hh * 8 + l + 1)
                        n = i * 18 + hh * 9 + l
                        act.wait_ge(lx_ready, (n - 1 if l >= 2 else i * 18 + hh * 9) + 1)
                        dv, ev = [x[:, l % 2, :].rearrange("p (j two b) -> p j two b", two=2, b=b) for x in (DD, EE)]
                        act.activation(ev[:, :, 1, :], dv[:, :, 1, :], ACT.Exp)
                        act.activation(ev[:, :, 0, :], dv[:, :, 0, :], ACT.Exp, scale=-1.0).then_inc(e_ready, 1)

                    ps, free = psum(0)
                    act.wait_ge(f_ready, i * 4 + hh * 2 + 1)
                    act.activation(HF[:, PAD:TP], ps, ACT.Sigmoid).then_inc(free, 1)
                    act.drain().then_inc(sf_ready, 1)
                    act.activation(HL[:, PAD:TP], HF[:, PAD:TP], ACT.Ln, bias=LAM[:, 5, bass.ds(h, 1)],
                                   scale=LAM[:, 6, bass.ds(h, 1)]).then_inc(lf_ready, 1)
                    ps, free = psum(1)
                    act.wait_ge(qg_ready, h + 1)
                    act.activation(HQ[:, PAD:TP], ps, ACT.Silu).then_inc(free, 1)
                    act.drain().then_inc(hq_ready, 1)
                    psum(2)
                    act.wait_ge(o_mm, h + 1)
                    act.activation(HV[:, :, :].rearrange("p c v -> p (c v)"), gp[hh % 2][:, 0:TP],
                                   ACT.Copy).then_inc(gp_free[hh % 2], 1)
                    act.drain().then_inc(hv_ready, 1)
                    decay(0, LEVELS[0])
                    decay(1, LEVELS[1])
                    ps, free = psum(3)
                    act.wait_ge(mix2_done, h + 1)
                    act.activation(CG[:, :], ps, ACT.Copy).then_inc(free, 1)
                    act.drain().then_inc(cg_ready, 1)
                    decay(2, LEVELS[2])
                    decay(3, LEVELS[3])
                    act.wait_ge(cx_ready, h + 1)
                    act.activation(YB[:, :], CX[:, 2:2 + T], ACT.Copy, scale=V[:, bass.ds(VEC["conv2"] + h * 4 + 2, 1)]).then_inc(yb_first, 1)
                    decay(4, LEVELS[4])
                    decay(5, LEVELS[5])
                    ps, free = psum(5)
                    act.activation(BG[:, :], ps, ACT.Copy).then_inc(free, 1)
                    act.drain().then_inc(side_ready, 1)
                    decay(6, LEVELS[6])
                    act.activation(EG[:, P:TP], HG[:, P:TP], ACT.Exp).then_inc(eg_ready, 1)
                    act.wait_ge(d_ready, i * 16 + hh * 8 + 8)
                    act.wait_ge(lx_ready, i * 18 + hh * 9 + 8 + 1)
                    act.activation(EE[:, 1, 0:TP - P], DD[:, 1, 0:TP - P], ACT.Exp, scale=-1.0).then_inc(e_ready, 1)
                    ps, free = psum(6)
                    act.activation(SO[:, :], ps, ACT.Silu).then_inc(free, 1)
                    act.drain().then_inc(side_ready, 1)
                    act.wait_ge(kdt_mm, h + 1)
                    act.activation(KDT[:, :, :].rearrange("p c d -> p (c d)"), A67[:, 0:TP - P], ACT.Copy).then_inc(kdt_ready, 1)
                    for c, t in ((7, SA), (8, SB2)):
                        ps, free = psum(c)
                        act.activation(t[:, :], ps, ACT.Sigmoid).then_inc(free, 1)
                        act.drain().then_inc(side_ready, 1)
                    act.wait_ge(o_mm, h + 2)
                    act.activation(SQ[:, :], A67[:, PAD:TP], ACT.Square).then_inc(osq_ready, 1)
                    act.wait_ge(ostat_mm, h + 1)
                    act.activation(HST[:, :], A45[:, b0:b0 + T], ACT.Sqrt, bias=EPSC, scale=1.0 / P).then_inc(ostd_ready, 1)

            norm_stats(4)
            norm_apply(4)
            with act.Fori(0, FC) as i:
                def fw(c):
                    return V[:, bass.ds(VEC["ffn2"] + i * 4 + c, 1)]
                b0 = region(S + 2)
                act.wait_ge(unit_done, U_UP2 + i * 2 + 1 + 2)
                act.wait_ge(act2_done, i + 1)
                act.activation(YV[:, :], gp[0][:, b0 + 2:b0 + 2 + S], ACT.Identity, bias=fw(3), scale=fw(2)).then_inc(ya_first, 1)
                act.wait_ge(ya_ready, i + 1)
                act.activation(SL[:, :], YV[:, :], ACT.Silu).then_inc(silu2_ready, 1)
            norm_stats(5)

        @block.vector
        def _(dve):
            def norm_split(m):
                q = NORMS[m]
                f, n = q["feeds"], q["n"]
                o0 = TP - T + q["c0"]
                dve.wait_ge(std_ready, m + 1)
                dve.reciprocal(RSTD[:, 0:n], STD[:, 0:n])
                dve.drain()

                def scaled(k):
                    if KC * f + k >= 2:
                        dve.wait_ge(xf_ready, KC * f + k - 1)
                    dve.tensor_tensor(nt[:, k % 2, 0:n], H[:, k, q["c0"]:q["c0"] + n], RSTD[:, 0:n],
                                      ALU.mult).then_inc(nt_ready, 1)

                scaled(0)
                for k in range(KC):
                    if k + 1 < KC:
                        scaled(k + 1)
                    dve.wait_ge(xf_ready, KC * f + k + 1)
                    dve.tensor_copy(XNhi[:, k, o0:o0 + n], xf[:, k % 2, 0:n])
                    dve.drain()
                    dve.tensor_tensor(XNlo[:, k, o0:o0 + n], xf[:, k % 2, 0:n], XNhi[:, k, o0:o0 + n].bitcast(F32),
                                      ALU.subtract).then_inc(xn_ready, 1)

            def norm_final(m, g, done):
                dve.wait_ge(std_ready, m + 1)
                dve.reciprocal(RSTD[:, 0:S], STD[:, 0:S])
                dve.drain()
                for k in range(KC):
                    dve.scalar_tensor_tensor(H[:, k, META:T], H[:, k, META:T], vec(g, k), RSTD[:, 0:S], ALU.mult,
                                             ALU.mult).then_inc(done, 1)

            def residual(u0, per, c0, n, gate):
                b = region(n)
                with dve.Fori(0, KC // 2) as i:
                    for c in range(2):
                        dve.wait_ge(unit_done, u0 + i * (2 * per) + (c + 1) * per + 2)
                        hk = H[:, bass.ds(i * 2 + c, 1), c0:c0 + n].rearrange("p a n -> p (a n)")
                        src = gp[c][:, b:b + n] if n != S or c0 == META else None
                        if gate is None:
                            dve.tensor_tensor(hk, src, hk, ALU.add).then_inc(h_ready, 1)
                        else:
                            dve.scalar_tensor_tensor(hk, src, MOD[:, bass.ds(gate + i * 2 + c, 1)], hk, ALU.mult,
                                                     ALU.add).then_inc(h_ready, 1)
                        dve.drain().then_inc(gp_free[c], 1)

            dve.memset(LAM[:, 7, :], EPS).then_inc(unit_done, 2)
            dve.memset(sq[0:1, 0, 0:1], 0.0).then_inc(gp_free[0], 1)
            dve.memset(sq[0:1, 1, 0:1], 0.0).then_inc(gp_free[1], 1)
            dve.memset(LAM[:, 0, :], 0.0).then_inc(ada_done, 2)
            for j, s in enumerate(one_ahead):
                dve.memset(probe[0:1, 4 + j:5 + j], 0.0).then_inc(s, 1)
            dve.drain()
            dve.wait_ge(small_in, 16 * 5)
            lam, l0, l1 = vec("lam", 0, KC), vec("lb0", 0, KC), vec("lb1", 0, KC)
            dve.scalar_tensor_tensor(LAM[:, 0, :], lam, -1.0, lam, ALU.mult, ALU.min).then_inc(lam_neg, 1)
            dve.tensor_tensor(LAM[:, 2, :], l0, l1, ALU.max)
            dve.drain()
            dve.tensor_tensor(LAM[:, 3, :], l0, LAM[:, 2, :], ALU.subtract).then_inc(lb_max, 1)
            dve.tensor_tensor(LAM[:, 4, :], l1, LAM[:, 2, :], ALU.subtract).then_inc(lb_max, 1)
            dve.wait_ge(lb_exp, 2)
            dve.tensor_tensor(LAM[:, 6, :], LAM[:, 5, :], LAM[:, 6, :], ALU.add)
            dve.drain()
            dve.reciprocal(LAM[:, 6, :], LAM[:, 6, :])
            dve.drain()
            dve.tensor_tensor(LAM[:, 5, :], LAM[:, 5, :], LAM[:, 6, :], ALU.mult)
            dve.drain()
            dve.tensor_scalar(LAM[:, 6, :], LAM[:, 5, :], -1.0, 1.0, ALU.mult, ALU.add).then_inc(lb_done, 1)
            dve.wait_ge(lam_exp, 1)
            u, z, z2, pl = LAM[:, 1, :], LAM[:, 2, :], LAM[:, 3, :], LAM[:, 4, :]
            dve.tensor_scalar(z, u, 2.0, None, ALU.add)
            dve.drain()
            dve.reciprocal(z, z)
            dve.drain()
            dve.tensor_tensor(z, z, u, ALU.mult)
            dve.drain()
            dve.tensor_tensor(z2, z, z, ALU.mult)
            dve.drain()
            dve.tensor_scalar(pl, z2, 1.0 / 17, 1.0 / 15, ALU.mult, ALU.add)
            dve.drain()
            for odd in (13, 11, 9, 7, 5, 3, 1):
                dve.tensor_tensor(pl, pl, z2, ALU.mult)
                dve.drain()
                dve.tensor_scalar(pl, pl, 1.0 / odd, None, ALU.add)
                dve.drain()
            dve.tensor_tensor(pl, pl, z, ALU.mult)
            dve.tensor_scalar(LAM[:, 1, :], lam, -1.0, 0.0, ALU.mult, ALU.max)
            dve.drain()
            dve.scalar_tensor_tensor(pl, pl, 2.0, LAM[:, 1, :], ALU.mult, ALU.add)
            dve.drain()
            dve.tensor_scalar(LAM[:, 2, :], pl, -8.0, None, ALU.mult)
            dve.tensor_scalar(LAM[:, 0, :], pl, 8.0, None, ALU.mult)
            dve.drain().then_inc(lam_done, 1)

            dve.wait_ge(ada_done, ADA_FIRST + 2)
            dve.tensor_tensor(MOD[:, 0:ADA_FIRST], gp[1][:, 512:512 + ADA_FIRST], vec("b_ada", 0, ADA_FIRST), ALU.add).then_inc(mod_ready, 1)
            dve.drain()
            dve.scalar_tensor_tensor(AB1[:, :], MOD[:, KC:2 * KC], 1.0, vec("g_mix", 0, KC), ALU.add, ALU.mult).then_inc(mod_ready, 1)
            norm_split(0)

            dve.wait_ge(unit_done, U_V + 1 + 2)
            s = U_V % 2
            dve.tensor_tensor(VT[:, :, :], gp[s][:, 0:S].rearrange("p (t v) -> p t v", t=QT),
                              RBV[:, 0:P].rearrange("p (o v) -> p o v", o=1).to_broadcast([P, QT, P]), ALU.add).then_inc(gp_free[s], 1)
            dve.drain().then_inc(v_ready, 1)
            dve.wait_ge(unit_done, U_WI + 1 + 2)
            s = U_WI % 2
            dve.tensor_tensor(WI[:, :, :], gp[s][:, 0:S].rearrange("p (t v) -> p t v", t=QT)[:, :, 0:NH],
                              RBV[:, P:P + NH].rearrange("p (o v) -> p o v", o=1).to_broadcast([P, QT, NH]), ALU.add).then_inc(gp_free[s], 1)
            dve.drain()
            dve.tensor_scalar(WI[:, :, :], WI[:, :, :], NH ** -0.5, None, ALU.mult)
            dve.drain()

            n = 0
            for i in range(1, QT):
                w = (i + 1) * P
                for h in range(NH):
                    dve.wait_ge(relu_done, n + 1)
                    if h == 0:
                        dve.tensor_scalar(SC[i][:, :], RL[:, n % 2, 0:w], WI[:, i, h:h + 1], None, ALU.mult).then_inc(score_acc, 1)
                    else:
                        dve.drain()
                        dve.scalar_tensor_tensor(SC[i][:, :], RL[:, n % 2, 0:w], WI[:, i, h:h + 1], SC[i][:, :], ALU.mult,
                                                 ALU.add).then_inc(score_acc, 1)
                    n += 1
                dve.drain()
                dve.tensor_tensor(SC[i][:, i * P:w], SC[i][:, i * P:w], tri, ALU.add)
                dve.drain()
            for i in range(1, QT):
                for r in range(TOPK // 8):
                    dve.max(m8[:, :], SC[i][:, :])
                    dve.drain()
                    dve.match_replace(SC[i][:, :], m8[:, :], SC[i][:, :], TAKEN)
                    dve.drain()
                dve.tensor_scalar(NEG[i][:, :], SC[i][:, :], TAKEN, MASKED, ALU.not_equal, ALU.mult)
                dve.drain()
            dve.wait_ge(ada_done, 6 * KC + 2)
            dve.tensor_tensor(MOD[:, ADA_FIRST:], gp[1][:, 512 + ADA_FIRST:512 + 6 * KC], vec("b_ada", ADA_FIRST, 4 * KC), ALU.add)
            dve.drain()
            dve.scalar_tensor_tensor(AB2[:, :], MOD[:, 4 * KC:5 * KC], 1.0, vec("g_ffn", 0, KC), ALU.add, ALU.mult).then_inc(mod_ready, 1)

            dve.wait_ge(bias_in, 16)

            def logits(i):
                w = (i + 1) * P
                if i >= 2:
                    dve.wait_ge(pt_mm, i * (i - 1))
                for h in range(NH):
                    c = i * NH + h
                    pr = PR[:, i % 2, h, 0:w]
                    dve.wait_ge(logit_mm, c + 1)
                    dve.scalar_tensor_tensor(pr, A45[:, (c % 2) * 512:(c % 2) * 512 + w], HD ** -0.5,
                                             BIAS[:, h, S - w:S], ALU.mult, ALU.add).then_inc(logit_out, 1)
                    dve.drain()
                    dve.tensor_tensor_reduce(pr, pr, NEG[i][:, 0:w], 1.0, MASKED, ALU.add, ALU.max, mx[:, i % 2, h:h + 1])
                dve.drain()
                dve.tensor_scalar(nmx[:, i % 2, :], mx[:, i % 2, :], -1.0, None, ALU.mult).then_inc(nmx_ready, 1)

            logits(0)
            for i in range(QT):
                if i + 1 < QT:
                    logits(i + 1)
                dve.wait_ge(exp_done, NH * (i + 1))
                dve.reciprocal(rr[:, i % 2, :], rs[:, i % 2, :])
                dve.drain()
                for h in range(NH):
                    pr = PR[:, i % 2, h, 0:(i + 1) * P]
                    dve.tensor_scalar(pr, pr, rr[:, i % 2, h:h + 1], None, ALU.mult)
                dve.drain().then_inc(p_ready, 1)
                dve.wait_ge(at_hi, i + 1)
                dve.tensor_tensor(ATlo[:, :, i * P:(i + 1) * P], gp[0][:, 512:1024].rearrange("p (j q) -> p j q", j=4),
                                  AThi[:, :, i * P:(i + 1) * P].bitcast(F32), ALU.subtract).then_inc(at_done, 1)

            dve.drain()
            dve.memset(XR[:, 0:3], 0.0).then_inc(xr_pad, 1)
            with dve.Fori(0, KC) as i:
                def rv(c):
                    return V[:, bass.ds(VEC["rnn"] + i * 16 + c, 1)]
                dve.wait_ge(conv_first, i + 1)
                for tap in (2, 1, 0):
                    ins = dve.scalar_tensor_tensor(XC[:, :], XR[:, tap:tap + S], rv(2 + tap), XC[:, :], ALU.mult, ALU.add)
                    if tap:
                        dve.drain()
                ins.then_inc(xc_ready, 1)
                dve.drain()
                dve.wait_ge(ig_ready, i * 2 + 3)
                dve.tensor_tensor(U1[:, :], XC[:, :], IG[:, :], ALU.mult)
                dve.wait_ge(a_ready, i + 1)
                dve.scalar_tensor_tensor(M2[:, :], A2[:, :], 1.0, TH[:, :], ALU.add, ALU.mult).then_inc(m2_ready, 1)
                dve.drain()
                dve.wait_ge(mult_ready, i + 1)
                dve.tensor_tensor(UU[:, :], U1[:, :], MU[:, :], ALU.mult)
                dve.drain()
                dve.tensor_tensor_scan(HS[:, :], DA[:, :], UU[:, :], 0.0, ALU.mult, ALU.add)
                dve.drain()
                dve.wait_ge(gelu_ready, i + 1)
                dve.tensor_tensor(RF[:, :], HS[:, :], GY[:, :], ALU.mult)
                dve.drain()
                rhi, rlo = [x[:, bass.ds(i, 1), :].rearrange("p a n -> p (a n)") for x in (RNhi, RNlo)]
                dve.tensor_copy(rhi, RF[:, :])
                dve.drain()
                dve.tensor_tensor(rlo, RF[:, :], rhi.bitcast(F32), ALU.subtract).then_inc(rnn_done, 1)

            dve.drain()
            with dve.Fori(0, 2) as i:
                for pr in range(2):
                    dve.wait_ge(sg_ready, i * 8 + pr * 4 + 4)
                    dve.wait_ge(unit_done, U_MRG + i * 14 + pr * 7 + 5 + 2)
                    for q in range(2):
                        dve.tensor_tensor(M1[:, q, :], gp[q][:, 0:S], SG[:, 2 * q, :], ALU.mult).then_inc(gp_free[q], 1)
                    for q in range(2):
                        dve.wait_ge(unit_done, U_MRG + i * 14 + pr * 7 + 6 + q + 2)
                        dve.tensor_tensor(MB[:, :], gp[q][:, 0:S], SG[:, 2 * q + 1, :], ALU.mult).then_inc(gp_free[q], 1)
                        dve.drain()
                        dve.tensor_tensor(MF[:, :], MB[:, :], M1[:, q, :], ALU.add)
                        dve.drain()
                        mhi, mlo = [x[:, bass.ds(i * 4 + pr * 2 + q, 1), :].rearrange("p a n -> p (a n)") for x in (MGhi, MGlo)]
                        dve.tensor_copy(mhi, MF[:, :])
                        dve.drain()
                        dve.tensor_tensor(mlo, MF[:, :], mhi.bitcast(F32), ALU.subtract).then_inc(merge_done, 1)
                        dve.drain()
            residual(U_OUT, 1, META, S, 2 * KC)
            norm_split(1)

            def split_act(i, done):
                ahi, alo = [x[:, bass.ds(i, 1), :].rearrange("p a n -> p (a n)") for x in (AChi, AClo)]
                dve.drain()
                dve.tensor_copy(ahi, AF[:, :])
                dve.drain()
                dve.tensor_tensor(alo, AF[:, :], ahi.bitcast(F32), ALU.subtract).then_inc(done, 1)
                dve.drain()

            dve.drain()
            with dve.Fori(0, FC) as i:
                def fv(c):
                    return V[:, bass.ds(VEC["ffn"] + i * 8 + c, 1)]
                for c, (y, first) in enumerate(((YV, yv_first), (YG, yg_first))):
                    dve.wait_ge(first, i + 1)
                    dve.scalar_tensor_tensor(y[:, 1:S], gp[c][:, 0:S - 1], fv(4 * c + 1), y[:, 1:S], ALU.mult, ALU.add)
                    dve.drain()
                    dve.scalar_tensor_tensor(y[:, 2:S], gp[c][:, 0:S - 2], fv(4 * c), y[:, 2:S], ALU.mult,
                                             ALU.add).then_inc(gp_free[c], 1)
                dve.drain().then_inc(yg_ready, 1)
                dve.wait_ge(silu_ready, i + 1)
                dve.tensor_tensor(AF[:, :], SL[:, :], YV[:, :], ALU.mult)
                split_act(i, act_done)
            residual(U_DN, 3, META, S, 5 * KC)
            norm_final(2, "g_final", h_ready)

            norm_split(3)
            dve.drain()
            for t in (HQ, HK, HL):
                dve.memset(t[:, 0:PAD], 0.0)
            dve.memset(AT2[:, :, :], 0.0)
            dve.memset(CX[:, 0:2], 0.0)
            dve.drain().then_inc(pads2, 1)
            with dve.Fori(0, KC // 2) as i:
                for hh in range(2):
                    h = i * 2 + hh
                    b0 = region(T)
                    dve.wait_ge(sf_ready, h + 1)
                    dve.tensor_scalar(HK[:, PAD:TP], HF[:, PAD:TP], LAM[:, 6, bass.ds(h, 1)], LAM[:, 5, bass.ds(h, 1)],
                                      ALU.mult, ALU.add).then_inc(f_ready, 1)
                    dve.drain()
                    dve.tensor_scalar(HK[:, PAD:TP], HK[:, PAD:TP], -1.0, 1.0, ALU.mult, ALU.add)
                    dve.wait_ge(lf_ready, h + 1)
                    dve.tensor_tensor_scan(HG[:, :], CON[:, C_RST:C_RST + TP], HL[:, :], 0.0, ALU.mult, ALU.add).then_inc(f_ready, 1)
                    dve.drain()

                    def boundary(l):
                        b = LEVELS[l]
                        g = HG[:, :].rearrange("p (j t) -> p j t", t=2 * b)
                        dve.tensor_tensor(DD[:, l % 2, :].rearrange("p (j t) -> p j t", t=2 * b), g,
                                          g[:, :, b - 1:b].to_broadcast([P, TP // (2 * b), 2 * b]), ALU.subtract).then_inc(d_ready, 1)

                    def weigh(l):
                        b = LEVELS[l]
                        dve.wait_ge(e_ready, i * 16 + hh * 8 + l + 1)
                        x, e, q, k = [t.rearrange("p (j two b) -> p j two b", two=2, b=b)
                                      for t in (XX[:, l % 2, :], EE[:, l % 2, :], HQ[:, :], HK[:, :])]
                        dve.tensor_tensor(x[:, :, 1, :], q[:, :, 1, :], e[:, :, 1, :], ALU.mult)
                        dve.tensor_tensor(x[:, :, 0, :], k[:, :, 0, :], e[:, :, 0, :], ALU.mult)
                        dve.drain().then_inc(lx_ready, 1)

                    def place(l):
                        b = LEVELS[l]
                        dve.wait_ge(lev_mm, i * 16 + hh * 8 + l + 1)
                        dve.memset(probe[0:1, 1:2], 0.0)
                        m = CON[:, C_LEV + 64 * l:C_LEV + 64 * (l + 1)].bitcast(U32)
                        dve.copy_predicated(
                            AT2[:, :, :].rearrange("p c (j two b) -> p c j two b", two=2, b=b)[:, :, :, 1, :],
                            m.rearrange("p (o j b) -> p o j b", o=1, b=b).to_broadcast([P, CH, 64 // b, b]),
                            A45[:, (l % 2) * 512:(l % 2) * 512 + CH * 64].rearrange("p (c j b) -> p c j b", c=CH, b=b)
                        ).then_inc(lev_out, 1)

                    dve.wait_ge(hq_ready, h + 1)
                    dve.wait_ge(o_mm, h + 1)
                    boundary(0)
                    boundary(1)
                    for l in range(len(LEVELS)):
                        weigh(l)
                        if l + 2 < len(LEVELS):
                            boundary(l + 2)
                        if l >= 1:
                            place(l - 1)
                        if l == 2:
                            dve.wait_ge(cg_ready, h + 1)
                            dve.wait_ge(unit_done, U_MIX2 + i * 18 + hh * 9 + 4 + 1 + 2)
                            g = (hh * 9 + 4) % 2
                            dve.tensor_tensor(CX[:, 2:2 + T], gp[g][:, b0:b0 + T], CG[:, :], ALU.mult).then_inc(cx_ready, 1)
                            dve.drain().then_inc(gp_free[g], 1)
                    dve.tensor_tensor(XX[:, 1, :], HQ[:, :], HK[:, :], ALU.mult)
                    dve.drain().then_inc(lx_ready, 1)
                    g = HG[:, 0:TP - P].rearrange("p (c t) -> p c t", t=P)
                    dve.tensor_tensor(DD[:, 1, 0:TP - P].rearrange("p (c t) -> p c t", t=P), g,
                                      g[:, :, P - 1:P].to_broadcast([P, CH - 1, P]), ALU.subtract).then_inc(d_ready, 1)
                    place(len(LEVELS) - 1)
                    dve.drain()
                    dve.wait_ge(lev_mm, i * 16 + hh * 8 + 8)
                    dve.memset(probe[0:1, 2:3], 0.0)
                    dve.copy_predicated(AT2[:, :, :], ident.bitcast(U32).rearrange("p (o t) -> p o t", o=1).to_broadcast([P, CH, P]),
                                        A67[:, 0:TP].rearrange("p (c t) -> p c t", c=CH)).then_inc(lev_out, 1)
                    dve.wait_ge(e_ready, i * 16 + hh * 8 + 8)
                    dve.tensor_tensor(XX[:, 0, 0:TP - P], HK[:, 0:TP - P], EE[:, 1, 0:TP - P], ALU.mult)
                    dve.drain().then_inc(lx_ready, 1)
                    dve.wait_ge(eg_ready, h + 1)
                    dve.tensor_tensor(QG[:, P:TP], HQ[:, P:TP], EG[:, P:TP], ALU.mult).then_inc(qg_ready, 1)
                    dve.wait_ge(yb_first, h + 1)
                    for tap in (1, 0):
                        dve.scalar_tensor_tensor(YB[:, :], CX[:, tap:tap + T], V[:, bass.ds(VEC["conv2"] + h * 4 + tap, 1)],
                                                 YB[:, :], ALU.mult, ALU.add)
                        dve.drain()
                    dve.wait_ge(side_ready, i * 8 + hh * 4 + 1)
                    dve.tensor_tensor(YB[:, :], YB[:, :], BG[:, :], ALU.mult)
                    dve.wait_ge(state_mm, h + 1)
                    dve.tensor_copy(ST[:, 0, :], A45[:, 0:P])
                    for c in range(1, CH - 1):
                        dve.drain()
                        dve.scalar_tensor_tensor(ST[:, c, :], ST[:, c - 1, :], EG[:, c * P + P - 1:c * P + P],
                                                 A45[:, c * P:(c + 1) * P], ALU.mult, ALU.add)
                    dve.drain().then_inc(state_ready, 1)
                    dve.wait_ge(side_ready, i * 8 + hh * 4 + 4)
                    dve.tensor_tensor(YB[:, :], YB[:, :], SB2[:, :], ALU.mult)
                    dve.wait_ge(ostd_ready, h + 2)
                    dve.reciprocal(HRS[:, :], HST[:, :])
                    dve.drain()
                    dve.scalar_tensor_tensor(ON[:, :], A67[:, PAD:TP], vec("hgrn_norm", 0), HRS[:, :], ALU.mult,
                                             ALU.mult).then_inc(on_ready, 1)
                    dve.drain()
                    dve.tensor_tensor(ON[:, :], ON[:, :], SO[:, :], ALU.mult)
                    dve.drain()
                    dve.tensor_tensor(ON[:, :], ON[:, :], SA[:, :], ALU.mult)
                    dve.drain()
                    dve.tensor_tensor(MF2[:, :], ON[:, :], YB[:, :], ALU.add)
                    dve.drain()
                    mhi, mlo = [x[:, bass.ds(h, 1), :].rearrange("p a n -> p (a n)") for x in (M2hi, M2lo)]
                    dve.tensor_copy(mhi, MF2[:, :])
                    dve.drain()
                    dve.tensor_tensor(mlo, MF2[:, :], mhi.bitcast(F32), ALU.subtract).then_inc(mix2_done, 1)
                    dve.drain()
            residual(U_OUT2, 1, 0, T, None)
            norm_split(4)

            dve.drain()
            with dve.Fori(0, FC) as i:
                b0 = region(S + 2)
                dve.wait_ge(ya_first, i + 1)
                for tap in (1, 0):
                    ins = dve.scalar_tensor_tensor(YV[:, :], gp[0][:, b0 + tap:b0 + tap + S],
                                                   V[:, bass.ds(VEC["ffn2"] + i * 4 + tap, 1)], YV[:, :], ALU.mult, ALU.add)
                    if tap:
                        dve.drain()
                ins.then_inc(gp_free[0], 1)
                dve.drain().then_inc(ya_ready, 1)
                dve.wait_ge(silu2_ready, i + 1)
                dve.wait_ge(unit_done, U_UP2 + i * 2 + 2 + 2)
                dve.tensor_tensor(AF[:, :], gp[1][:, 0:S], SL[:, :], ALU.mult).then_inc(gp_free[1], 1)
                split_act(i, act2_done)
            residual(U_DN2, 3, META, S, None)
            norm_final(5, "final2", out_ready)


def _constants():
    c = np.zeros((P, NCONST), np.float32)
    c[:, C_ID:C_ID + P] = np.eye(P)
    c[:, C_ONE:C_ONE + P] = 1.0
    r = np.arange(P)
    c[:, C_TRI:C_TRI + P] = np.where(r[None, :] <= r[:, None], 0.0, MASKED)
    for l, b in enumerate(LEVELS):
        upper = r[(r % (2 * b)) >= b]
        c[:, C_LEV + 64 * l:C_LEV + 64 * (l + 1)] = ((r[:, None] // (2 * b) == upper[None, :] // (2 * b))
                                                     & (r[:, None] % (2 * b) < b))
    c[:, C_RST:] = (np.arange(TP) % P != 0)[None, :]
    return c


def _buckets():
    n = np.maximum(S - 1 - np.arange(BIAS_W), 0)
    large = 16 + (np.log(np.maximum(n, 1).astype(np.float32) / 16) / np.log(8.0) * 16).astype(np.int32)
    bucket = np.where(n < 16, n, np.minimum(large, 31))
    return (np.arange(32)[:, None] == bucket[None, :]).astype(np.float32)


def kernel(**inputs):
    import concourse.bacc as bacc
    from concourse.bass_utils import run_bass_kernel_spmd

    a = {k: np.ascontiguousarray(v) for k, v in inputs.items()}

    def chunks(w):
        k, n = w.shape
        return w.reshape(k // P, P, n // P, P).transpose(2, 1, 0, 3).reshape(n // P, P, (k // P) * P)

    def cols(v):
        return v.reshape(-1, P).T

    def heads(w, n):
        return w.reshape(w.shape[:-1] + (2, 4, HD)).swapaxes(-3, -2).reshape(w.shape[:-1] + (n,))

    w_in, b_in = a["w_in"][0], a["b_in"][0]
    cut = np.cumsum([512, 128, 128, 512, 64, 8, D, D, D, D])[:-1]
    wq, wk, wv, wqi, wki, wwi, wxr, wyr, wga, wgb = np.split(w_in, cut, axis=1)
    bq, bk, bv, bqi, bki, bwi, bxr, byr, bga, bgb = np.split(b_in, cut)
    wi_pad = np.concatenate([wwi, np.zeros((D, P - NH), np.float32)], 1)
    proj = [chunks(wqi), chunks(np.concatenate([wki, wki], 1)), chunks(heads(wq, 512)), chunks(wk), chunks(wv), chunks(wi_pad)]
    rnn = np.stack([chunks(wxr), chunks(wyr)], 1).reshape(2 * KC, P, UNIT)
    woa = a["w_o_attn"][0].reshape(2, 4, HD, D).swapaxes(0, 1).reshape(512, D)
    woa = chunks(woa).reshape(KC // 2, 2, P, 512).transpose(0, 2, 1, 3).reshape(KC // 2, 1, P, UNIT)
    gates = np.stack([chunks(wga), chunks(wgb)], 1).reshape(KC // 2, 4, P, UNIT)
    wor = chunks(a["w_o_rnn"][0]).reshape(KC // 2, 2, P, UNIT)
    merge = np.concatenate([gates, woa, wor], 1).reshape(-1, P, UNIT)

    def up(w):
        return chunks(w).reshape(2, FC, P, UNIT).swapaxes(0, 1).reshape(2 * FC, P, UNIT)

    def down(w):
        t = chunks(w)
        t = np.concatenate([t, np.zeros((KC, P, 3 * UNIT - FF), np.float32)], 2)
        return t.reshape(KC, P, 3, UNIT).transpose(0, 2, 1, 3).reshape(3 * KC, P, UNIT)

    w2 = chunks(a["w_in_2"][0]).reshape(9, KC, P, UNIT)
    mix2 = w2[[1, 0, 2, 5, 6, 4, 3, 7, 8]].swapaxes(0, 1).reshape(9 * KC, P, UNIT)
    units = np.concatenate(proj + [rnn, merge, chunks(a["w_out"][0]), up(a["w_up"][0]), down(a["w_down"][0]), mix2,
                                   chunks(a["w_out_2"][0]), up(a["w_up_2"][0]), down(a["w_down_2"][0])], 0)

    cw, fw, fb = a["conv_rnn_w"][0], a["conv_ffn_w"][0], a["conv_ffn_b"][0]
    rnn_rows = [bxr, byr, cw[0], cw[1], cw[2], cw[3], a["conv_rnn_b"][0], a["b_rg"][0], a["b_ig"][0]]
    rnn_rows += [np.zeros(D, np.float32)] * (16 - len(rnn_rows))

    def inter(rows):
        return np.stack([cols(r) for r in rows], 2).reshape(P, -1)

    ffn_rows = [fw[0, :FF], fw[1, :FF], fw[2, :FF], fb[:FF], fw[0, FF:], fw[1, FF:], fw[2, FF:], fb[FF:]]
    c2, f2 = a["conv_w_2"][0], a["ffn_conv_w_2"][0]
    parts = [("c", cols(a["c"][0])), ("b_ada", cols(a["b_ada"][0])), ("g_mix", cols(a["g_mix"][0])), ("b_qi", cols(bqi)),
             ("b_ki", cols(np.concatenate([bki, bki]))), ("b_q", cols(heads(bq, 512))), ("b_k", cols(bk)),
             ("rnn", inter(rnn_rows)), ("b_gates", inter([bga, bgb])), ("lam", cols(a["lru_lambda"][0])),
             ("g_ffn", cols(a["g_ffn"][0])), ("ffn", inter(ffn_rows)), ("g_final", cols(a["g_final"])),
             ("lb0", cols(a["lb_param_2"][0])), ("lb1", cols(a["lb_param_2"][1])), ("attn_norm", cols(a["attn_norm_w_2"][0])),
             ("hgrn_norm", cols(a["hgrn_norm_w_2"][0])), ("conv2", inter([c2[0], c2[1], c2[2], np.zeros(D, np.float32)])),
             ("ffn_norm", cols(a["ffn_norm_w_2"][0])),
             ("ffn2", inter([f2[0], f2[1], f2[2], a["ffn_conv_b_2"][0]])), ("final2", cols(a["final_norm_w_2"]))]
    assert [n for n, _ in parts] == list(VEC)
    gatew = np.concatenate([a["w_rg"][0], a["w_ig"][0]], 2)
    arrays = {
        "xT": a["x"][0].T.reshape(KC, P, S).swapaxes(0, 1),
        "metaT": a["meta_tokens_2"].T.reshape(KC, P, META).swapaxes(0, 1),
        "vecs": np.concatenate([v for _, v in parts], 1),
        "rel": a["rel_bias"],
        "onehot": _buckets(),
        "consts": _constants(),
        "rowbias": np.concatenate([bv, bwi]),
        "ada": chunks(a["w_ada"][0]),
        "gatew": gatew,
        "units": units,
    }
    nc = bacc.Bacc("TRN2", target_bir_lowering=False, num_devices=1)
    args, feed = [], {}
    for name, v in arrays.items():
        feed[name] = np.ascontiguousarray(v)
        args.append(nc.dram_tensor(name, v.shape, F32, kind="ExternalInput").ap())
    args.append(nc.dram_tensor("bias_rows", (NH, P, BIAS_W), F32, kind="Internal").ap())
    args.append(nc.dram_tensor("out", (P, KC, S), F32, kind="ExternalOutput").ap())
    build(nc, *args)
    r = run_bass_kernel_spmd(nc, [feed], core_ids=[0])
    o = np.asarray(r.results[0]["out"])
    return np.ascontiguousarray(o.transpose(2, 1, 0)).reshape(1, S, D)
```

```python
import numpy as np
import concourse.bass as bass
from concourse import mybir
from contextlib import ExitStack

F32 = mybir.dt.float32
F32R = mybir.dt.float32r
U32 = mybir.dt.uint32
ALU = mybir.AluOpType
ACT = mybir.ActivationFunctionType
P = 128

D = 1024
KC = D // P
S = 512
META = 16
T = META + S
PAD = P - META
TP = PAD + T
CH = TP // P
QT = S // P
NH, HD, TOPK = 8, 64, 128
FF = 2816
FC = FF // P
UNIT = KC * P
EPS = 1e-6
MASKED, TAKEN = -3.0e38, -3.4e38
LEVELS = [64, 32, 16, 8, 4, 2, 1]

U_QI, U_KI, U_WI, U_Q, U_V, U_K = 0, 4, 5, 6, 10, 11
U_RNN = 12
U_MRG = U_RNN + 3 * KC
U_OUT = U_MRG + 5 * (KC // 2)
U_UP = U_OUT + KC
U_DN = U_UP + 2 * FC
U_MIX2 = U_DN + 3 * KC
U_OUT2 = U_MIX2 + 9 * KC
U_UP2 = U_OUT2 + KC
U_DN2 = U_UP2 + 2 * FC
UNITS = U_DN2 + 3 * KC
G_PROJ = 0
G_RNN = 12
G_MRG = G_RNN + 3 * KC
G_OUT = G_MRG + 3 * KC
G_UP = G_OUT + KC
G_DN = G_UP + 2 * FC
G_MIX2 = G_DN + KC
G_OUT2 = G_MIX2 + 9 * KC
G_UP2 = G_OUT2 + KC
G_DN2 = G_UP2 + 2 * FC
RAW = 2
ADA_FIRST = 2 * KC
ADA_SLOTS = 6

VEC = {}
_at = 0
for _n, _w in (("b_ada", 6 * KC), ("g_mix", KC), ("b_qi", 4), ("b_ki", 1), ("b_wi", 1), ("b_q", 4),
               ("b_v", 1), ("b_k", 1),
               ("rnn", 16 * KC), ("b_gates", 2 * KC), ("lam", KC), ("g_ffn", KC), ("ffn", 8 * FC), ("g_final", KC),
               ("lb0", KC), ("lb1", KC), ("attn_norm", KC), ("hgrn_norm", 1), ("conv2", 4 * KC), ("ffn_norm", KC),
               ("ffn2", 4 * FC), ("final2", KC)):
    VEC[_n] = _at
    _at += _w
NVEC = _at
C_ID, C_ONE, C_TRI, C_MEAN, C_HMEAN = [j * P for j in range(5)]
C_LEV = 5 * P
C_RST = C_LEV + 64 * len(LEVELS)
NCONST = C_RST + TP
BIAS_W = S + P


def spans(n):
    return [(0, n)] if n <= 512 else [(0, (n // 2 + 1) // 2 * 2), ((n // 2 + 1) // 2 * 2, n - (n // 2 + 1) // 2 * 2)]


def region(n):
    return 0 if n <= 512 else 512 - spans(n)[0][1]


def build(nc, xT, metaT, vecs, rel, onehot, consts, crow, ada, gatew, units, scratch, out):
    with ExitStack() as ctx:
        def sb(name, shape, dt=F32, frame=ctx):
            return frame.enter_context(nc.sbuf_tensor(name, shape, dt))

        def sem(name):
            return ctx.enter_context(nc.semaphore(name))

        H = sb("H", [P, KC, T])
        XNhi = sb("XNhi", [P, KC, TP], F32R)
        XNlo = sb("XNlo", [P, KC, TP], F32R)
        raw = [sb(f"raw{s}", [P, UNIT]) for s in range(RAW)]
        Whi = [sb(f"Whi{s}", [P, KC, P], F32R) for s in range(2)]
        Wlo = [sb(f"Wlo{s}", [P, KC, P], F32R) for s in range(2)]
        V = sb("V", [P, NVEC])
        MOD = sb("MOD", [P, 6 * KC])
        AB1 = sb("AB1", [P, KC])
        AB2 = sb("AB2", [P, KC])
        LAM = sb("LAM", [P, 8, KC])
        probe = sb("probe", [P, 32])
        ZERO = sb("ZERO", [P, KC])
        CON = sb("CON", [P, NCONST])
        sq = sb("sq", [P, 2, T])
        RSTD = sb("RSTD", [P, T])
        ident, ones, tri, mean, head_mean = [CON[:, c:c + P] for c in (C_ID, C_ONE, C_TRI, C_MEAN, C_HMEAN)]
        gp = [ctx.enter_context(nc.psum_tensor(f"gp{s}", [P, 1024], F32)) for s in range(2)]
        A45 = ctx.enter_context(nc.psum_tensor("A45", [P, 1024], F32))
        A67 = ctx.enter_context(nc.psum_tensor("A67", [P, 1024], F32))

        with ExitStack() as f:
            nt = sb("nt", [P, 3, T], frame=f)
        with ExitStack() as f:
            with ExitStack() as fi:
                QI = sb("QI", [P, 4, S], frame=fi)
                KI = sb("KI", [P, S], frame=fi)
                RL = sb("RL", [P, 2, S], frame=fi)
                WIT = sb("WIT", [P, S], frame=fi)
            SGA = sb("SGA", [P, KC, S], frame=f)
            with ExitStack() as fw:
                AW = [sb(f"AW{s}", [P, UNIT], frame=fw) for s in range(ADA_SLOTS)]
            RNhi = sb("RNhi", [P, KC, S], F32R, f)
            RNlo = sb("RNlo", [P, KC, S], F32R, f)
            with ExitStack() as fq:
                Q = sb("Q", [P, 4, S], frame=fq)
                CR = sb("CR", [P, D], frame=fq)
                CS = sb("CS", [P, D], frame=fq)
            AThi = sb("AThi", [P, 4, S], F32R, f)
            ATlo = sb("ATlo", [P, 4, S], F32R, f)
            with ExitStack() as fa:
                K = sb("K", [P, S], frame=fa)
                VT = sb("VT", [P, QT, P], frame=fa)
                WI = sb("WI", [P, QT, NH], frame=fa)
                BIAS = sb("BIAS", [P, NH, S], frame=fa)
                SC = [None] + [sb(f"SC{i}", [P, (i + 1) * P], frame=fa) for i in range(1, QT)]
                NEG = [tri] + SC[1:]
                m8 = sb("m8", [P, QT, 8], frame=fa)
                mx, nmx, rs, rr = [sb(n, [P, 2, 4], frame=fa) for n in ("mx", "nmx", "rs", "rr")]
                with ExitStack() as fb:
                    OH = sb("OH", [32, BIAS_W], frame=fb)
                    RB = sb("RB", [NH, BIAS_W], frame=fb)
                    REL = sb("REL", [32, NH], frame=fb)
                    VV = sb("VV", [P, S], frame=fb)
                with ExitStack() as fr:
                    XR = sb("XR", [P, 3 + S], frame=fr)
                    XC, GY, RG, IG, DA, TH, M2, U1 = [sb(f"rnn_{n}", [P, S], frame=fr) for n in
                                                      ("xc", "gelu", "r", "i", "a", "tanh", "mult2", "u")]
                    A2 = HS = RG
                    MU, UU, RF = M2, U1, GY
                    WG = sb("WG", [P, 2 * P], frame=fr)
                with ExitStack() as fp:
                    PR = sb("PR", [P, 2, 4, S], frame=fp)
            PTs = sq[:, :, 0:S]
            with ExitStack() as fm:
                MGhi = sb("MGhi", [P, KC, S], F32R, fm)
                MGlo = sb("MGlo", [P, KC, S], F32R, fm)
                SGB = sb("SGB", [P, 2, S], frame=fm)
                M1 = sb("M1", [P, 2, S], frame=fm)
                MB = sb("MB", [P, S], frame=fm)
                MF = sb("MF", [P, S], frame=fm)
        with ExitStack() as f:
            AChi = sb("AChi", [P, FC, S], F32R, f)
            AClo = sb("AClo", [P, FC, S], F32R, f)
            YV, YG, SL, AF = [sb(f"ffn_{n}", [P, S], frame=f) for n in ("val", "gate", "silu", "act")]
        with ExitStack() as f:
            M2hi = sb("M2hi", [P, KC, T], F32R, f)
            M2lo = sb("M2lo", [P, KC, T], F32R, f)
            HF, HL, HQ, HK, HG, EG, QG = [sb(f"h_{n}", [P, TP], frame=f) for n in
                                          ("sig", "logf", "q", "k", "G", "expG", "qG")]
            HVT = sb("HVT", [P, TP], frame=f)
            HV = sb("HV", [P, CH, P], frame=f)
            DD = sb("DD", [P, 2, TP], frame=f)
            EE = sb("EE", [P, 2, TP], frame=f)
            XX = sb("XX", [P, 2, TP], frame=f)
            AT2 = sb("AT2", [P, CH, P], frame=f)
            KDT = sb("KDT", [P, CH - 1, P], frame=f)
            ST = sb("ST", [P, CH - 1, P], frame=f)
            CG, BG, SO, SA, SB2, SQ, ON, YB, MF2, HRS = [sb(f"h_{n}", [P, T], frame=f) for n in
                                                    ("cg", "bg", "silu_g", "sig_a", "sig_b", "sq", "on", "yb", "mf",
                                                     "rstd")]
            CX = sb("CX", [P, 2 + T], frame=f)

        small_in = sem("small_in")
        x_in = sem("x_in")
        bias_saved = sem("bias_saved")
        bias_in = sem("bias_in")
        raw_in = [sem(f"raw_in{s}") for s in range(RAW)]
        ada_in = [sem(f"ada_in{s}") for s in range(ADA_SLOTS)]
        gate_in = sem("gate_in")
        hi_made = sem("hi_made")
        weights_ready = sem("weights_ready")
        unit_done = sem("unit_done")
        gp_free = [sem(f"gp_free{s}") for s in range(2)]
        cleared = sem("cleared")
        rb_mm, rb_copied = sem("rb_mm"), sem("rb_copied")
        silu_c, ada_done, mod_ready = sem("silu_c"), sem("ada_done"), sem("mod_ready")
        lam_neg, lam_exp, lam_done = sem("lam_neg"), sem("lam_exp"), sem("lam_done")
        lb_max, lb_exp, lb_done = sem("lb_max"), sem("lb_exp"), sem("lb_done")
        sq_ready, stat_mm, rstd_ready = sem("sq_ready"), sem("stat_mm"), sem("rstd_ready")
        nt_ready, xhi_ready, xn_ready = sem("nt_ready"), sem("xhi_ready"), sem("xn_ready")
        h_ready, out_ready, out_saved = sem("h_ready"), sem("out_ready"), sem("out_saved")
        proj_out, wi_mm, wi_ready, v_mm, v_ready = (sem("proj_out"), sem("wi_mm"), sem("wi_ready"), sem("v_mm"),
                                                    sem("v_ready"))
        score_mm, relu_done, score_acc, sel_done = sem("score_mm"), sem("relu_done"), sem("score_acc"), sem("sel_done")
        logit_mm, logit_out, nmx_ready = sem("logit_mm"), sem("logit_out"), sem("nmx_ready")
        exp_done, p_ready, pt_mm, pt_copied = sem("exp_done"), sem("p_ready"), sem("pt_mm"), sem("pt_copied")
        pv_mm, at_hi, at_done = sem("pv_mm"), sem("at_hi"), sem("at_done")
        xr_pad, conv_first, xc_ready, gelu_ready = sem("xr_pad"), sem("conv_first"), sem("xc_ready"), sem("gelu_ready")
        gate_mm, ig_ready, a_ready, m2_ready = sem("gate_mm"), sem("ig_ready"), sem("a_ready"), sem("m2_ready")
        mult_ready, u1_done, rnn_done = sem("mult_ready"), sem("u1_done"), sem("rnn_done")
        sga_ready = sem("sga_ready")
        sg_ready, merge_done = sem("sg_ready"), sem("merge_done")
        yv_first, yg_first, yg_ready, silu_ready, act_done = (sem("yv_first"), sem("yg_first"), sem("yg_ready"),
                                                              sem("silu_ready"), sem("act_done"))
        ya_first, ya_ready, silu2_ready, act2_done = sem("ya_first"), sem("ya_ready"), sem("silu2_ready"), sem("act2_done")
        pads2 = sem("pads2")
        sf_ready, lf_ready, hq_ready = sem("sf_ready"), sem("lf_ready"), sem("hq_ready")
        hvt_ready, hv_mm, hv_ready = sem("hvt_ready"), sem("hv_mm"), sem("hv_ready")
        f_ready, d_ready, e_ready, lx_ready = sem("f_ready"), sem("d_ready"), sem("e_ready"), sem("lx_ready")
        lev_mm, lev_out = sem("lev_mm"), sem("lev_out")
        kdt_mm, kdt_ready, state_mm, state_ready = sem("kdt_mm"), sem("kdt_ready"), sem("state_mm"), sem("state_ready")
        eg_ready, qg_ready, o_mm, osq_ready, ostat_mm = (sem("eg_ready"), sem("qg_ready"), sem("o_mm"), sem("osq_ready"),
                                                         sem("ostat_mm"))
        orstd_ready, on_ready, cg_ready, cx_ready = sem("orstd_ready"), sem("on_ready"), sem("cg_ready"), sem("cx_ready")
        yb_first, side_ready, mix2_done = sem("yb_first"), sem("side_ready"), sem("mix2_done")

        def vec(name, k, w=1):
            return V[:, bass.ds(VEC[name] + k, w)]

        def slot_free(g, c=0):
            return (g + c) // 2 + 1

        NORMS = [dict(c0=META, n=S, feeds=0, h0=None), dict(c0=META, n=S, feeds=1, h0=0),
                 dict(c0=META, n=S, feeds=None, h0=KC), dict(c0=0, n=T, feeds=2, h0=2 * KC),
                 dict(c0=META - 2, n=S + 2, feeds=3, h0=3 * KC), dict(c0=META, n=S, feeds=None, h0=4 * KC)]

        def scale_bias(m, k):
            return {0: (AB1[:, k:k + 1], MOD[:, k:k + 1]), 1: (AB2[:, k:k + 1], MOD[:, 3 * KC + k:3 * KC + k + 1]),
                    3: (vec("attn_norm", k), ZERO[:, k:k + 1]), 4: (vec("ffn_norm", k), ZERO[:, k:k + 1])}[m]

        one_ahead = [xc_ready, rnn_done, merge_done, act_done, f_ready, qg_ready, o_mm, mix2_done, act2_done, lx_ready,
                     ig_ready, orstd_ready, on_ready, gate_mm, hv_mm, u1_done]

        block = ctx.enter_context(nc.Block())

        @block.sync
        def _(sp):
            sp.dma_start(V[:, :], vecs).then_inc(small_in, 16)
            sp.dma_start(CON[:, :], consts).then_inc(small_in, 16)
            sp.dma_start(CR[:, :], crow.partition_broadcast(P)).then_inc(small_in, 16)
            sp.dma_start(REL[:, :], rel).then_inc(small_in, 16)
            sp.dma_start(OH[:, :], onehot).then_inc(small_in, 16)
            sp.dma_start(H[:, :, META:T], xT).then_inc(x_in, 16)
            sp.dma_start(H[:, :, 0:META], metaT).then_inc(x_in, 16)

            def load_ada(i, s):
                sp.wait_ge(ada_done, i * ADA_SLOTS + s + 1)
                sp.dma_start(AW[s][:, :], ada[bass.ds(i * ADA_SLOTS + s, 1), :, :]).then_inc(ada_in[s], 16)

            with sp.Fori(0, 3) as i:
                for s in range(ADA_SLOTS):
                    load_ada(i, s)
            def load_units(first, last):
                with sp.Fori(first // RAW, last // RAW) as i:
                    for s in range(RAW):
                        sp.wait_ge(weights_ready, i * RAW + s + 1)
                        sp.dma_start(raw[s][:, :], units[bass.ds(i * RAW + s, 1), :, :]).then_inc(raw_in[s], 16)

            load_units(0, RAW)
            sp.wait_ge(rb_copied, 1)
            sp.dma_start(scratch, RB[:, :].rearrange("h (o m) -> h o m", o=1).to_broadcast([NH, P, BIAS_W])).then_inc(bias_saved, 16)
            with sp.Fori(0, (U_RNN - RAW) // 2) as i:
                for b in range(2):
                    for s in range(3):
                        load_ada(i + 3, b * 3 + s)
                    sp.wait_ge(weights_ready, i * 2 + b + RAW + 1)
                    sp.dma_start(raw[b][:, :], units[bass.ds(i * 2 + b + RAW, 1), :, :]).then_inc(raw_in[b], 16)
            sp.wait_ge(bias_saved, 16)
            sp.dma_start(BIAS[:, :, :], bass.AP(scratch.tensor, P - 1, [[BIAS_W - 1, P], [P * BIAS_W, NH], [1, S]])).then_inc(bias_in, 16)
            load_units(U_RNN, UNITS)
            for k in range(KC):
                sp.wait_ge(out_ready, k + 1)
                sp.dma_start(out[:, k, :], H[:, k, META:T]).then_inc(out_saved, 16)
            sp.wait_ge(out_saved, 16 * KC)

        @block.gpsimd
        def _(pool):
            pool.memset(ZERO[:, :], 0.0).then_inc(weights_ready, RAW)
            pool.memset(XNhi[:, :, 0:PAD].bitcast(F32), 0.0).then_inc(cleared, 1)
            pool.memset(XNlo[:, :, 0:PAD].bitcast(F32), 0.0).then_inc(cleared, 1)
            with pool.Fori(0, UNITS // 2) as i:
                for s in range(2):
                    u = i * 2 + s
                    src = raw[s][:, :]
                    hi, lo = [w[s][:, :, :].rearrange("p k n -> p (k n)") for w in (Whi, Wlo)]
                    pool.wait_ge(raw_in[s], i * 16 + 16)
                    pool.wait_ge(unit_done, u + 1)
                    pool.tensor_tensor(probe[0:1, 0:1], src[0:1, 0:1], src[0:1, 0:1], ALU.add)
                    pool.tensor_scalar(hi, src, 1.0, 1.0, ALU.mult, ALU.mult).then_inc(hi_made, 1)
                    pool.wait_ge(hi_made, u + 1)
                    pool.tensor_tensor(lo, src, hi.bitcast(F32), ALU.subtract).then_inc(weights_ready, 1)

        @block.tensor
        def _(pe):
            def three(dst, s, k, rhi, rlo, start, stop):
                pe.matmul(dst, Whi[s][:, k, :], rhi, start=start, stop=False)
                pe.matmul(dst, Whi[s][:, k, :], rlo, start=False, stop=False)
                return pe.matmul(dst, Wlo[s][:, k, :], rhi, start=False, stop=stop)

            def unit(u, s, dst, n, hi, lo, c0, ks, first=0, last=None, arrive=None):
                pe.wait_ge(weights_ready, u + 1 + RAW)
                base = region(n)
                for j, k in enumerate(ks):
                    if arrive is not None:
                        pe.wait_ge(xn_ready, arrive + j + 1)
                    kc = first + j
                    for a, w in spans(n):
                        mm = three(dst[:, base + a:base + a + w], s, k, hi[:, kc, c0 + a:c0 + a + w],
                                   lo[:, kc, c0 + a:c0 + a + w], kc == 0, kc == last)
                return mm

            def stat(m, k, turn=None, start=False, stop=False):
                n, base = NORMS[m]["n"], region(NORMS[m]["n"])
                if m and start:
                    pe.wait_ge(rstd_ready, m)
                pe.wait_ge(sq_ready, KC * m + 1 + (k if turn is None else turn))
                for a, w in spans(n):
                    mm = pe.matmul(A67[:, base + a:base + a + w], mean, sq[:, k % 2, a:a + w], start=start, stop=stop)
                mm.then_inc(stat_mm, 1)

            def stats(m):
                for k in range(KC):
                    stat(m, k, start=(k == 0), stop=(k == KC - 1))

            pe.wait_ge(small_in, 16 * 5)
            pe.matmul(A45[0:NH, 0:512], REL[:, :], OH[:, 0:512], start=True, stop=True)
            pe.matmul(A45[0:NH, 512:BIAS_W], REL[:, :], OH[:, 512:BIAS_W], start=True, stop=True).then_inc(rb_mm, 1)
            stats(0)

            def score(n):
                i, h = 1 + n // NH, n % NH
                if n >= 4:
                    pe.wait_ge(relu_done, n - 3)
                hp = (h % 2) * HD
                pe.matmul((A45, A67)[n % 4 // 2][:, (n % 2) * 512:(n % 2) * 512 + (i + 1) * P],
                          QI[hp:hp + HD, h // 2, i * P:(i + 1) * P], KI[hp:hp + HD, 0:(i + 1) * P],
                          start=True, stop=True).then_inc(score_mm, 1)

            pe.wait_ge(cleared, 2)
            for u in range(U_RNN):
                pe.wait_ge(gp_free[u % 2], slot_free(u))
                unit(u, u % 2, gp[u % 2], S, XNhi, XNlo, P, range(KC), last=KC - 1,
                     arrive=0 if u == 0 else None).then_inc(unit_done, 1)
                if u == U_WI + 1:
                    pe.wait_ge(proj_out, U_WI + 1)
                    for t in range(QT):
                        mm = pe.transpose(gp[0][:, 512 + t * NH:512 + (t + 1) * NH], WIT[0:NH, t * P:(t + 1) * P], ident[0:NH, 0:NH])
                    mm.then_inc(wi_mm, 1)
                    pe.wait_ge(rb_copied, 1)
                if u > U_WI:
                    for n in range(4):
                        score((u - U_WI - 1) * 4 + n)
            pe.wait_ge(proj_out, U_V + 1)
            pe.wait_ge(wi_ready, 1)
            for t in range(QT):
                mm = pe.transpose(gp[0][:, 512 + t * P:512 + (t + 1) * P], VV[:, t * P:(t + 1) * P], ident)
            mm.then_inc(v_mm, 1)

            pe.wait_ge(relu_done, NH * (QT - 1))
            with pe.Fori(0, KC // 2) as i:
                for b in range(2):
                    for c in range(3):
                        g = b * 3 + c
                        pe.wait_ge(gp_free[g % 2], slot_free(G_RNN, g) + i * 3)
                        unit(U_RNN + i * 6 + g, g % 2, gp[g % 2], S, XNhi, XNlo, P, range(KC), last=KC - 1).then_inc(unit_done, 1)
                        if c == 1:
                            pe.wait_ge(gate_in, i * 32 + b * 16 + 16)
                            pe.wait_ge(xc_ready, i * 2 + b + 2)
                            pe.wait_ge(ig_ready, i * 4 + b * 2 + 1)
                            for r in range(2):
                                pe.matmul(A45[:, r * 512:(r + 1) * 512], WG[:, r * P:(r + 1) * P], XC[:, :],
                                          start=True, stop=True).then_inc(gate_mm, 1)

            pe.wait_ge(ig_ready, 2 * KC + 1)
            pe.wait_ge(v_ready, 1)

            def logits(i, g):
                for j in range(4):
                    c = i * NH + g * 4 + j
                    if c >= 2:
                        pe.wait_ge(logit_out, c - 1)
                    pe.matmul(A45[:, (c % 2) * 512:(c % 2) * 512 + (i + 1) * P], Q[g * HD:(g + 1) * HD, j, i * P:(i + 1) * P],
                              K[g * HD:(g + 1) * HD, 0:(i + 1) * P], start=True, stop=True).then_inc(logit_mm, 1)

            def values(i, g):
                pe.wait_ge(p_ready, i * 2 + g + 1)
                if i >= 2 and g == 0:
                    pe.wait_ge(at_done, i - 1)
                t0 = i * (i + 1) + g * (i + 1)
                for kb in range(i + 2):
                    if kb <= i:
                        t = t0 + kb
                        if t >= 2:
                            pe.wait_ge(pt_copied, t - 1)
                        for j in range(4):
                            mm = pe.transpose(A67[:, (t % 2) * 512 + j * P:(t % 2) * 512 + (j + 1) * P],
                                              PR[:, g, j, kb * P:(kb + 1) * P], ident)
                        mm.then_inc(pt_mm, 1)
                    if kb >= 1:
                        t = t0 + kb - 1
                        pe.wait_ge(pt_copied, t + 1)
                        pe.matmul(gp[i % 2][g * HD:(g + 1) * HD, 512:1024], VT[:, kb - 1, g * HD:(g + 1) * HD], PTs[:, t % 2, :],
                                  start=(kb == 1), stop=(kb == i + 1)).then_inc(pv_mm, 1)

            logits(0, 0)
            logits(0, 1)
            for i in range(QT):
                for g in range(2):
                    values(i, g)
                    if i + 1 < QT:
                        logits(i + 1, g)

            with pe.Fori(0, 2) as i:
                for pr in range(2):
                    for c in range(2):
                        pe.wait_ge(gp_free[c], slot_free(G_MRG, pr * 6 + c) + i * 6)
                        unit(U_MRG + i * 10 + pr * 5 + c, (pr * 5 + c) % 2, gp[c], S, XNhi, XNlo, P, range(KC),
                             last=KC - 1).then_inc(unit_done, 1)
                    pe.wait_ge(at_done, QT)
                    for q in range(2):
                        pe.wait_ge(gp_free[q], slot_free(G_MRG, pr * 6 + 2 + q) + i * 6)
                        mm = unit(U_MRG + i * 10 + pr * 5 + 2, (pr * 5 + 2) % 2, gp[q], S, AThi, ATlo, 0,
                                  range(4 * q, 4 * q + 4), last=3)
                    mm.then_inc(unit_done, 1)
                    pe.wait_ge(rnn_done, KC + 1)
                    for q in range(2):
                        pe.wait_ge(gp_free[q], slot_free(G_MRG, pr * 6 + 4 + q) + i * 6)
                        unit(U_MRG + i * 10 + pr * 5 + 3 + q, (pr * 5 + 3 + q) % 2, gp[q], S, RNhi, RNlo, 0, range(KC),
                             last=KC - 1).then_inc(unit_done, 1)

            def with_stats(m, product):
                product(0, 0)
                product(0, 1)
                stat(m, 0, start=True)
                with pe.Fori(1, KC // 2) as i:
                    product(i, 0)
                    stat(m, 1, turn=i * 2 - 1)
                    product(i, 1)
                    stat(m, 0, turn=i * 2)
                stat(m, KC - 1, stop=True)

            def plain(u0, g0, hi, lo, c0, n):
                def product(i, c):
                    pe.wait_ge(gp_free[c], slot_free(g0) + i)
                    unit(u0 + i * 2 + c, c, gp[c], n, hi, lo, c0, range(KC), last=KC - 1).then_inc(unit_done, 1)
                return product

            def down(u0, g0):
                def product(i, c):
                    pe.wait_ge(gp_free[c], slot_free(g0) + i)
                    for t in range(3):
                        unit(u0 + i * 6 + c * 3 + t, (c * 3 + t) % 2, gp[c], S, AChi, AClo, 0,
                             range(min(KC, FC - t * KC)), first=t * KC, last=FC - 1).then_inc(unit_done, 1)
                return product

            def up(u0, g0, f, halves):
                pe.wait_ge(weights_ready, u0 + 2 + RAW)
                for c in range(2):
                    pe.wait_ge(gp_free[c], slot_free(g0))
                for k in range(KC):
                    pe.wait_ge(xn_ready, KC * f + k + 1)
                    for c, (n, c0) in enumerate(halves):
                        for a, w in spans(n):
                            b = region(n) + a
                            mm = three(gp[c][:, b:b + w], c, k, XNhi[:, k, c0 + a:c0 + a + w], XNlo[:, k, c0 + a:c0 + a + w],
                                       k == 0, k == KC - 1)
                        if k == KC - 1:
                            mm.then_inc(unit_done, 1)
                with pe.Fori(1, FC) as i:
                    for c, (n, c0) in enumerate(halves):
                        pe.wait_ge(gp_free[c], slot_free(g0) + i)
                        unit(u0 + i * 2 + c, c, gp[c], n, XNhi, XNlo, c0, range(KC), last=KC - 1).then_inc(unit_done, 1)

            pe.wait_ge(merge_done, KC + 1)
            with_stats(1, plain(U_OUT, G_OUT, MGhi, MGlo, 0, S))
            up(U_UP, G_UP, 1, ((S, P), (S, P)))
            pe.wait_ge(act_done, FC + 1)
            with_stats(2, down(U_DN, G_DN))

            stats(3)
            with pe.Fori(0, KC // 2) as i:
                for hh in range(2):
                    def gemm(c):
                        g = (hh * 9 + c) % 2
                        pe.wait_ge(gp_free[g], slot_free(G_MIX2, hh * 9 + c) + i * 9)
                        u = U_MIX2 + i * 18 + hh * 9 + c
                        unit(u, g, gp[g], T, XNhi, XNlo, PAD, range(KC), last=KC - 1,
                             arrive=2 * KC if (hh, c) == (0, 0) else None).then_inc(unit_done, 1)

                    def level(l):
                        b = LEVELS[l]
                        pe.wait_ge(lx_ready, i * 18 + hh * 9 + l + 2)
                        if l >= 2:
                            pe.wait_ge(lev_out, i * 16 + hh * 8 + l - 1)
                        for c in range(CH):
                            x = XX[:, l % 2, c * P:(c + 1) * P]
                            up = x.rearrange("p (j two b) -> p j two b", two=2, b=b)[:, :, 1, :]
                            mm = pe.matmul(A45[:, (l % 2) * 512 + c * 64:(l % 2) * 512 + (c + 1) * 64], x, up,
                                           start=True, stop=True)
                        mm.then_inc(lev_mm, 1)

                    gemm(0)
                    gemm(1)
                    gemm(2)
                    gemm(3)
                    pe.wait_ge(hvt_ready, i * 2 + hh + 1)
                    pe.wait_ge(on_ready, i * 2 + hh + 1)
                    for c in range(CH):
                        mm = pe.transpose(A67[:, c * P:(c + 1) * P], HVT[:, c * P:(c + 1) * P], ident)
                    mm.then_inc(hv_mm, 1)
                    pe.wait_ge(orstd_ready, i * 2 + hh + 1)
                    level(0)
                    level(1)
                    gemm(4)
                    level(2)
                    level(3)
                    gemm(5)
                    level(4)
                    level(5)
                    gemm(6)
                    level(6)
                    pe.wait_ge(lx_ready, i * 18 + hh * 9 + 8 + 1)
                    pe.wait_ge(hv_ready, i * 2 + hh + 1)
                    for a, w in ((0, 512), (512, TP - 512)):
                        mm = pe.matmul(A67[:, a:a + w], ones, XX[:, 1, a:a + w], start=True, stop=True)
                    mm.then_inc(lev_mm, 1)
                    gemm(7)
                    pe.wait_ge(lx_ready, i * 18 + hh * 9 + 9 + 1)
                    pe.wait_ge(lev_out, i * 16 + hh * 8 + 8)
                    for c in range(CH - 1):
                        mm = pe.transpose(A67[:, c * P:(c + 1) * P], XX[:, 0, c * P:(c + 1) * P], ident)
                    mm.then_inc(kdt_mm, 1)
                    pe.wait_ge(kdt_ready, i * 2 + hh + 1)
                    for c in range(CH - 1):
                        mm = pe.matmul(A45[:, c * P:(c + 1) * P], KDT[:, c, :], HV[:, c, :], start=True, stop=True)
                    mm.then_inc(state_mm, 1)
                    gemm(8)
                    pe.wait_ge(state_ready, i * 2 + hh + 1)
                    pe.wait_ge(qg_ready, i * 2 + hh + 2)
                    for c in range(CH):
                        o = A67[:, c * P:(c + 1) * P]
                        mm = pe.matmul(o, HV[:, c, :], AT2[:, c, :], start=True, stop=(c == 0))
                        if c:
                            mm = pe.matmul(o, ST[:, c - 1, :], QG[:, c * P:(c + 1) * P], start=False, stop=True)
                    mm.then_inc(o_mm, 1)
                    pe.wait_ge(osq_ready, i * 2 + hh + 1)
                    b0 = region(T)
                    for a, w in spans(T):
                        mm = pe.matmul(A45[:, b0 + a:b0 + a + w], head_mean, SQ[:, a:a + w], start=True, stop=True)
                    mm.then_inc(ostat_mm, 1)

            pe.wait_ge(mix2_done, KC + 1)
            with_stats(4, plain(U_OUT2, G_OUT2, M2hi, M2lo, META - 2, S + 2))
            up(U_UP2, G_UP2, 3, ((S + 2, P - 2), (S, P)))
            pe.wait_ge(act2_done, FC + 1)
            with_stats(5, down(U_DN2, G_DN2))

        @block.scalar
        def _(act):
            def norm_stats(m):
                q = NORMS[m]
                for k in range(KC):
                    if q["h0"] is None:
                        if k == 0:
                            act.wait_ge(x_in, 32)
                    else:
                        act.wait_ge(h_ready, q["h0"] + k + 1)
                    if KC * m + k >= 2:
                        act.wait_ge(stat_mm, KC * m + k - 1)
                    act.activation(sq[:, k % 2, 0:q["n"]], H[:, k, q["c0"]:q["c0"] + q["n"]],
                                   ACT.Square).then_inc(sq_ready, 1)
                act.wait_ge(stat_mm, KC * (m + 1))
                r, b = RSTD[:, 0:q["n"]], region(q["n"])
                act.activation(r, A67[:, b:b + q["n"]], ACT.Ln, bias=EPSC)
                act.drain()
                act.activation(r, r, ACT.Exp, scale=-0.5).then_inc(rstd_ready, 1)

            def norm_apply(m):
                q = NORMS[m]
                f, n = q["feeds"], q["n"]
                o0 = TP - T + q["c0"]
                for k in range(KC):
                    act.wait_ge(nt_ready, KC * f + k + 1)
                    act.activation(XNhi[:, k, o0:o0 + n], nt[:, k % 3, 0:n], ACT.Identity,
                                   bias=scale_bias(m, k)[1]).then_inc(xhi_ready, 1)

            EPSC = LAM[:, 7, 0:1]
            act.wait_ge(small_in, 16 * 5)
            act.activation(CS[:, :], CR[:, :], ACT.Silu).then_inc(silu_c, 1)
            act.wait_ge(rb_mm, 1)
            act.activation(RB[:, :], A45[0:NH, 0:BIAS_W], ACT.Copy).then_inc(rb_copied, 1)
            act.wait_ge(lam_neg, 1)
            act.activation(LAM[:, 1, :], LAM[:, 0, :], ACT.Exp).then_inc(lam_exp, 1)
            act.wait_ge(lb_max, 2)
            act.activation(LAM[:, 5, :], LAM[:, 3, :], ACT.Exp).then_inc(lb_exp, 1)
            act.activation(LAM[:, 6, :], LAM[:, 4, :], ACT.Exp).then_inc(lb_exp, 1)
            norm_stats(0)
            act.wait_ge(mod_ready, 2)
            norm_apply(0)

            def relu(n):
                i = 1 + n // NH
                act.wait_ge(score_mm, n + 1)
                if n >= 2:
                    act.wait_ge(score_acc, n - 1)
                act.activation(RL[:, n % 2, 0:(i + 1) * P], (A45, A67)[n % 4 // 2][:, (n % 2) * 512:(n % 2) * 512 + (i + 1) * P],
                               ACT.Relu, scale=HD ** -0.5).then_inc(relu_done, 1)

            outs = ([(QI[:, j, :], vec("b_qi", j)) for j in range(4)] + [(KI[:, :], vec("b_ki", 0)), (WIT[:, :], vec("b_wi", 0))]
                    + [(Q[:, j, :], vec("b_q", j)) for j in range(4)] + [(VV[:, :], vec("b_v", 0)), (K[:, :], vec("b_k", 0))])
            for u, (o, b) in enumerate(outs):
                act.wait_ge(unit_done, u + 1 + 2)
                if u == U_V:
                    act.wait_ge(bias_saved, 16)
                act.activation(o, gp[u % 2][:, 0:S], ACT.Identity, bias=b).then_inc(gp_free[u % 2], 1)
                act.drain().then_inc(proj_out, 1)
                if u > U_WI:
                    for n in range(4):
                        relu((u - U_WI - 1) * 4 + n)
            act.wait_ge(v_mm, 1)
            act.activation(VT[:, :, :].rearrange("p t v -> p (t v)"), gp[0][:, 512:1024], ACT.Copy).then_inc(v_ready, 1)

            act.wait_ge(xr_pad, 1)
            act.wait_ge(lam_done, 1)
            act.wait_ge(score_acc, NH * (QT - 1))
            with act.Fori(0, KC // 2) as i:
                for b in range(2):
                    blk = i * 2 + b

                    def rv(c):
                        return V[:, bass.ds(VEC["rnn"] + i * 32 + b * 16 + c, 1)]

                    def psum(c):
                        g = b * 3 + c
                        act.wait_ge(unit_done, U_RNN + i * 6 + g + 1 + 2)
                        return gp[g % 2][:, 0:S], gp_free[g % 2]

                    act.wait_ge(gate_mm, i * 4 + b * 2 + 1)
                    act.dma_start(WG[:, :], gatew[bass.ds(blk, 1), :, :]).then_inc(gate_in, 16)
                    ps, free = psum(0)
                    act.wait_ge(xc_ready, blk + 1)
                    act.activation(XR[:, 3:3 + S], ps, ACT.Identity, bias=rv(0)).then_inc(free, 1)
                    act.drain()
                    act.wait_ge(u1_done, blk + 1)
                    act.activation(XC[:, :], XR[:, 3:3 + S], ACT.Identity, bias=rv(6), scale=rv(5)).then_inc(conv_first, 1)
                    ps, free = psum(1)
                    act.wait_ge(rnn_done, blk + 1)
                    act.activation(GY[:, :], ps, ACT.Gelu_apprx_tanh, bias=rv(1)).then_inc(free, 1)
                    act.drain().then_inc(gelu_ready, 1)
                    act.wait_ge(gate_mm, i * 4 + b * 2 + 3)
                    act.activation(RG[:, :], A45[:, 0:512], ACT.Sigmoid, bias=rv(7)).then_inc(ig_ready, 1)
                    act.activation(IG[:, :], A45[:, 512:1024], ACT.Sigmoid, bias=rv(8)).then_inc(ig_ready, 1)
                    act.drain()
                    act.activation(DA[:, :], RG[:, :], ACT.Exp, scale=LAM[:, 2, bass.ds(blk, 1)])
                    act.activation(TH[:, :], RG[:, :], ACT.Tanh, scale=LAM[:, 0, bass.ds(blk, 1)])
                    act.drain()
                    act.activation(A2[:, :], DA[:, :], ACT.Square).then_inc(a_ready, 1)
                    act.wait_ge(m2_ready, blk + 1)
                    act.activation(MU[:, :], M2[:, :], ACT.Sqrt).then_inc(mult_ready, 1)
                    ps, free = psum(2)
                    act.activation(SGA[:, bass.ds(blk, 1), :].rearrange("p a n -> p (a n)"), ps, ACT.Sigmoid,
                                   bias=V[:, bass.ds(VEC["b_gates"] + i * 4 + b * 2, 1)]).then_inc(free, 1)
                    act.drain().then_inc(sga_ready, 1)

            def exps(i, g):
                act.wait_ge(nmx_ready, i * 2 + g + 1)
                for j in range(4):
                    p = PR[:, g, j, 0:(i + 1) * P]
                    act.activation(p, p, ACT.Exp, bias=nmx[:, g, j:j + 1], accum_out=rs[:, g, j:j + 1]).then_inc(exp_done, 1)

            exps(0, 0)
            exps(0, 1)
            for i in range(QT):
                for g in range(2):
                    t0 = i * (i + 1) + g * (i + 1)
                    for t in range(t0, t0 + i + 1):
                        act.wait_ge(pt_mm, t + 1)
                        if t >= 2:
                            act.wait_ge(pv_mm, t - 1)
                        act.activation(PTs[:, t % 2, :], A67[:, (t % 2) * 512:(t % 2 + 1) * 512], ACT.Copy).then_inc(pt_copied, 1)
                    if g == 1:
                        act.wait_ge(pv_mm, (i + 1) * (i + 2))
                        act.activation(AThi[:, :, i * P:(i + 1) * P], gp[i % 2][:, 512:1024].rearrange("p (j q) -> p j q", j=4),
                                       ACT.Copy).then_inc(at_hi, 1)
                    if i + 1 < QT:
                        exps(i + 1, g)

            act.wait_ge(at_done, QT)
            with act.Fori(0, 2) as i:
                for pr in range(2):
                    for c in range(2):
                        act.wait_ge(unit_done, U_MRG + i * 10 + pr * 5 + c + 1 + 2)
                        act.wait_ge(merge_done, i * 4 + pr * 2 + 1)
                        act.activation(SGB[:, c, :], gp[c][:, 0:S], ACT.Sigmoid,
                                       bias=V[:, bass.ds(VEC["b_gates"] + i * 8 + pr * 4 + c * 2 + 1, 1)]).then_inc(gp_free[c], 1)
                        act.drain().then_inc(sg_ready, 1)

            norm_stats(1)
            norm_apply(1)
            with act.Fori(0, FC) as i:
                def fv(c):
                    return V[:, bass.ds(VEC["ffn"] + i * 8 + c, 1)]
                act.wait_ge(unit_done, U_UP + i * 2 + 1 + 2)
                act.wait_ge(act_done, i + 1)
                act.activation(YV[:, :], gp[0][:, 0:S], ACT.Identity, bias=fv(3), scale=fv(2)).then_inc(yv_first, 1)
                act.wait_ge(unit_done, U_UP + i * 2 + 2 + 2)
                act.activation(YG[:, :], gp[1][:, 0:S], ACT.Identity, bias=fv(7), scale=fv(6)).then_inc(yg_first, 1)
                act.wait_ge(yg_ready, i + 1)
                act.activation(SL[:, :], YG[:, :], ACT.Silu).then_inc(silu_ready, 1)
            norm_stats(2)

            norm_stats(3)
            norm_apply(3)
            act.wait_ge(pads2, 1)
            act.wait_ge(lb_done, 1)
            with act.Fori(0, KC // 2) as i:
                for hh in range(2):
                    h = i * 2 + hh
                    b0 = region(T)

                    def psum(c):
                        g = (hh * 9 + c) % 2
                        act.wait_ge(unit_done, U_MIX2 + i * 18 + hh * 9 + c + 1 + 2)
                        return gp[g][:, b0:b0 + T], gp_free[g]

                    def decay(l, b):
                        act.wait_ge(d_ready, i * 16 + hh * 8 + l + 1)
                        n = i * 18 + hh * 9 + l
                        act.wait_ge(lx_ready, (n - 1 if l >= 2 else i * 18 + hh * 9) + 1)
                        dv, ev = [x[:, l % 2, :].rearrange("p (j two b) -> p j two b", two=2, b=b) for x in (DD, EE)]
                        act.activation(ev[:, :, 1, :], dv[:, :, 1, :], ACT.Exp)
                        act.activation(ev[:, :, 0, :], dv[:, :, 0, :], ACT.Exp, scale=-1.0).then_inc(e_ready, 1)

                    ps, free = psum(0)
                    act.wait_ge(f_ready, i * 4 + hh * 2 + 1)
                    act.activation(HF[:, PAD:TP], ps, ACT.Sigmoid).then_inc(free, 1)
                    act.drain().then_inc(sf_ready, 1)
                    act.activation(HL[:, PAD:TP], HF[:, PAD:TP], ACT.Ln, bias=LAM[:, 5, bass.ds(h, 1)],
                                   scale=LAM[:, 6, bass.ds(h, 1)]).then_inc(lf_ready, 1)
                    ps, free = psum(1)
                    act.wait_ge(qg_ready, h + 1)
                    act.activation(HQ[:, PAD:TP], ps, ACT.Silu).then_inc(free, 1)
                    act.drain().then_inc(hq_ready, 1)
                    ps, free = psum(2)
                    act.wait_ge(hv_mm, h + 1)
                    act.activation(HVT[:, PAD:TP], ps, ACT.Copy).then_inc(free, 1)
                    act.drain().then_inc(hvt_ready, 1)
                    decay(0, LEVELS[0])
                    decay(1, LEVELS[1])
                    ps, free = psum(3)
                    act.wait_ge(mix2_done, h + 1)
                    act.activation(CG[:, :], ps, ACT.Copy).then_inc(free, 1)
                    act.drain().then_inc(cg_ready, 1)
                    act.wait_ge(hv_mm, h + 2)
                    act.wait_ge(o_mm, h + 1)
                    act.activation(HV[:, :, :].rearrange("p c v -> p (c v)"), A67[:, 0:TP], ACT.Copy).then_inc(hv_ready, 1)
                    decay(2, LEVELS[2])
                    decay(3, LEVELS[3])
                    act.wait_ge(cx_ready, h + 1)
                    act.activation(YB[:, :], CX[:, 2:2 + T], ACT.Copy, scale=V[:, bass.ds(VEC["conv2"] + h * 4 + 2, 1)]).then_inc(yb_first, 1)
                    decay(4, LEVELS[4])
                    decay(5, LEVELS[5])
                    ps, free = psum(5)
                    act.activation(BG[:, :], ps, ACT.Copy).then_inc(free, 1)
                    act.drain().then_inc(side_ready, 1)
                    decay(6, LEVELS[6])
                    act.activation(EG[:, P:TP], HG[:, P:TP], ACT.Exp).then_inc(eg_ready, 1)
                    act.wait_ge(d_ready, i * 16 + hh * 8 + 8)
                    act.wait_ge(lx_ready, i * 18 + hh * 9 + 8 + 1)
                    act.activation(EE[:, 1, 0:TP - P], DD[:, 1, 0:TP - P], ACT.Exp, scale=-1.0).then_inc(e_ready, 1)
                    ps, free = psum(6)
                    act.activation(SO[:, :], ps, ACT.Silu).then_inc(free, 1)
                    act.drain().then_inc(side_ready, 1)
                    act.wait_ge(kdt_mm, h + 1)
                    act.activation(KDT[:, :, :].rearrange("p c d -> p (c d)"), A67[:, 0:TP - P], ACT.Copy).then_inc(kdt_ready, 1)
                    for c, t in ((7, SA), (8, SB2)):
                        ps, free = psum(c)
                        act.activation(t[:, :], ps, ACT.Sigmoid).then_inc(free, 1)
                        act.drain().then_inc(side_ready, 1)
                    act.wait_ge(o_mm, h + 2)
                    act.activation(SQ[:, :], A67[:, PAD:TP], ACT.Square).then_inc(osq_ready, 1)
                    act.wait_ge(ostat_mm, h + 1)
                    act.activation(HRS[:, :], A45[:, b0:b0 + T], ACT.Ln, bias=EPSC)
                    act.drain()
                    act.activation(HRS[:, :], HRS[:, :], ACT.Exp, scale=-0.5).then_inc(orstd_ready, 1)

            norm_stats(4)
            norm_apply(4)
            with act.Fori(0, FC) as i:
                def fw(c):
                    return V[:, bass.ds(VEC["ffn2"] + i * 4 + c, 1)]
                b0 = region(S + 2)
                act.wait_ge(unit_done, U_UP2 + i * 2 + 1 + 2)
                act.wait_ge(act2_done, i + 1)
                act.activation(YV[:, :], gp[0][:, b0 + 2:b0 + 2 + S], ACT.Identity, bias=fw(3), scale=fw(2)).then_inc(ya_first, 1)
                act.wait_ge(ya_ready, i + 1)
                act.activation(SL[:, :], YV[:, :], ACT.Silu).then_inc(silu2_ready, 1)
            norm_stats(5)

        @block.vector
        def _(dve):
            def norm_split(m):
                q = NORMS[m]
                f, n, c0 = q["feeds"], q["n"], q["c0"]
                o0 = TP - T + c0
                dve.wait_ge(rstd_ready, m + 1)

                def scaled(k):
                    dve.scalar_tensor_tensor(nt[:, k % 3, 0:n], H[:, k, c0:c0 + n], scale_bias(m, k)[0], RSTD[:, 0:n], ALU.mult,
                                             ALU.mult).then_inc(nt_ready, 1)

                scaled(0)
                scaled(1)
                for k in range(KC):
                    if k + 2 < KC:
                        if k:
                            dve.drain()
                        scaled(k + 2)
                    dve.wait_ge(xhi_ready, KC * f + k + 1)
                    dve.scalar_tensor_tensor(XNlo[:, k, o0:o0 + n], nt[:, k % 3, 0:n], scale_bias(m, k)[1],
                                             XNhi[:, k, o0:o0 + n].bitcast(F32), ALU.add, ALU.subtract).then_inc(xn_ready, 1)

            def norm_final(m, g, done):
                dve.wait_ge(rstd_ready, m + 1)
                for k in range(KC):
                    dve.scalar_tensor_tensor(H[:, k, META:T], H[:, k, META:T], vec(g, k), RSTD[:, 0:S], ALU.mult,
                                             ALU.mult).then_inc(done, 1)

            def residual(u0, per, c0, n, gate):
                b = region(n)
                with dve.Fori(0, KC // 2) as i:
                    for c in range(2):
                        dve.wait_ge(unit_done, u0 + i * (2 * per) + (c + 1) * per + 2)
                        hk = H[:, bass.ds(i * 2 + c, 1), c0:c0 + n].rearrange("p a n -> p (a n)")
                        src = gp[c][:, b:b + n]
                        if gate is None:
                            dve.tensor_tensor(hk, src, hk, ALU.add).then_inc(h_ready, 1)
                        else:
                            dve.scalar_tensor_tensor(hk, src, MOD[:, bass.ds(gate + i * 2 + c, 1)], hk, ALU.mult,
                                                     ALU.add).then_inc(h_ready, 1)
                        dve.drain().then_inc(gp_free[c], 1)

            dve.memset(LAM[:, 7, :], EPS).then_inc(unit_done, 2)
            dve.memset(sq[0:1, 0, 0:1], 0.0).then_inc(gp_free[0], 1)
            dve.memset(sq[0:1, 1, 0:1], 0.0).then_inc(gp_free[1], 1)
            dve.memset(LAM[:, 0, :], 0.0).then_inc(ada_done, ADA_SLOTS)
            for j, s in enumerate(one_ahead):
                dve.memset(probe[0:1, 4 + j:5 + j], 0.0).then_inc(s, 1)
            dve.drain()
            dve.wait_ge(small_in, 16 * 5)
            lam, l0, l1 = vec("lam", 0, KC), vec("lb0", 0, KC), vec("lb1", 0, KC)
            dve.scalar_tensor_tensor(LAM[:, 0, :], lam, -1.0, lam, ALU.mult, ALU.min).then_inc(lam_neg, 1)
            dve.tensor_tensor(LAM[:, 2, :], l0, l1, ALU.max)
            dve.drain()
            dve.tensor_tensor(LAM[:, 3, :], l0, LAM[:, 2, :], ALU.subtract).then_inc(lb_max, 1)
            dve.tensor_tensor(LAM[:, 4, :], l1, LAM[:, 2, :], ALU.subtract).then_inc(lb_max, 1)
            dve.wait_ge(lb_exp, 2)
            dve.tensor_tensor(LAM[:, 6, :], LAM[:, 5, :], LAM[:, 6, :], ALU.add)
            dve.drain()
            dve.reciprocal(LAM[:, 6, :], LAM[:, 6, :])
            dve.drain()
            dve.tensor_tensor(LAM[:, 5, :], LAM[:, 5, :], LAM[:, 6, :], ALU.mult)
            dve.drain()
            dve.tensor_scalar(LAM[:, 6, :], LAM[:, 5, :], -1.0, 1.0, ALU.mult, ALU.add).then_inc(lb_done, 1)
            dve.wait_ge(lam_exp, 1)
            u, z, z2, pl = LAM[:, 1, :], LAM[:, 2, :], LAM[:, 3, :], LAM[:, 4, :]
            dve.tensor_scalar(z, u, 2.0, None, ALU.add)
            dve.drain()
            dve.reciprocal(z, z)
            dve.drain()
            dve.tensor_tensor(z, z, u, ALU.mult)
            dve.drain()
            dve.tensor_tensor(z2, z, z, ALU.mult)
            dve.drain()
            dve.tensor_scalar(pl, z2, 1.0 / 17, 1.0 / 15, ALU.mult, ALU.add)
            dve.drain()
            for odd in (13, 11, 9, 7, 5, 3, 1):
                dve.tensor_tensor(pl, pl, z2, ALU.mult)
                dve.drain()
                dve.tensor_scalar(pl, pl, 1.0 / odd, None, ALU.add)
                dve.drain()
            dve.tensor_tensor(pl, pl, z, ALU.mult)
            dve.tensor_scalar(LAM[:, 1, :], lam, -1.0, 0.0, ALU.mult, ALU.max)
            dve.drain()
            dve.scalar_tensor_tensor(pl, pl, 2.0, LAM[:, 1, :], ALU.mult, ALU.add)
            dve.drain()
            dve.tensor_scalar(LAM[:, 2, :], pl, -8.0, None, ALU.mult)
            dve.tensor_scalar(LAM[:, 0, :], pl, 8.0, None, ALU.mult)
            dve.drain().then_inc(lam_done, 1)

            def modulation(first, last):
                for c in range(first, last):
                    w = AW[c % ADA_SLOTS]
                    dve.wait_ge(ada_in[c % ADA_SLOTS], 16 * (c // ADA_SLOTS + 1))
                    dve.tensor_tensor_reduce(w[:, :], w[:, :], CS[:, :], 1.0, 0.0, ALU.mult, ALU.add,
                                             MOD[:, c:c + 1]).then_inc(ada_done, 1)

            dve.wait_ge(silu_c, 1)
            modulation(0, ADA_FIRST)
            dve.drain()
            dve.tensor_tensor(MOD[:, 0:ADA_FIRST], MOD[:, 0:ADA_FIRST], vec("b_ada", 0, ADA_FIRST), ALU.add).then_inc(mod_ready, 1)
            dve.drain()
            dve.scalar_tensor_tensor(AB1[:, :], MOD[:, KC:2 * KC], 1.0, vec("g_mix", 0, KC), ALU.add, ALU.mult).then_inc(mod_ready, 1)
            dve.drain()
            norm_split(0)

            modulation(ADA_FIRST, 6 * KC - 16)
            dve.wait_ge(wi_mm, 1)
            dve.tensor_scalar(WI[:, :, :].rearrange("p t h -> p (t h)"), gp[0][:, 512:512 + QT * NH], NH ** -0.5, None,
                              ALU.mult).then_inc(wi_ready, 1)
            dve.drain()
            for n in range(NH * (QT - 1)):
                i, h = 1 + n // NH, n % NH
                w = (i + 1) * P
                dve.wait_ge(relu_done, n + 1)
                if h == 0:
                    dve.tensor_scalar(SC[i][:, :], RL[:, n % 2, 0:w], WI[:, i, h:h + 1], None, ALU.mult).then_inc(score_acc, 1)
                else:
                    dve.drain()
                    dve.scalar_tensor_tensor(SC[i][:, :], RL[:, n % 2, 0:w], WI[:, i, h:h + 1], SC[i][:, :], ALU.mult,
                                             ALU.add).then_inc(score_acc, 1)
                if h == NH - 1:
                    dve.drain()
                    dve.tensor_tensor(SC[i][:, i * P:w], SC[i][:, i * P:w], tri, ALU.add)
                    dve.drain()
                if n % 4 == 3:
                    c = 6 * KC - 16 + 3 * (n // 4)
                    modulation(c, min(c + 3, 6 * KC))
            dve.drain()
            dve.tensor_tensor(MOD[:, ADA_FIRST:], MOD[:, ADA_FIRST:], vec("b_ada", ADA_FIRST, 4 * KC), ALU.add)
            dve.drain()
            dve.scalar_tensor_tensor(AB2[:, :], MOD[:, 4 * KC:5 * KC], 1.0, vec("g_ffn", 0, KC), ALU.add, ALU.mult).then_inc(mod_ready, 1)

            def take(tiles):
                for i in tiles:
                    dve.max(m8[:, i, :], SC[i][:, :])
                dve.drain()
                for i in tiles:
                    dve.match_replace(SC[i][:, :], m8[:, i, :], SC[i][:, :], TAKEN)
                dve.drain()

            dve.wait_ge(v_ready, 1)
            dve.memset(XR[:, 0:3], 0.0).then_inc(xr_pad, 1)
            assert KC * 2 * 8 == TOPK
            with dve.Fori(0, KC // 2) as i:
                for b in range(2):
                    blk = i * 2 + b

                    def rv(c):
                        return V[:, bass.ds(VEC["rnn"] + i * 32 + b * 16 + c, 1)]
                    dve.wait_ge(conv_first, blk + 1)
                    for tap in (2, 1, 0):
                        ins = dve.scalar_tensor_tensor(XC[:, :], XR[:, tap:tap + S], rv(2 + tap), XC[:, :], ALU.mult, ALU.add)
                        if tap:
                            dve.drain()
                    ins.then_inc(xc_ready, 1)
                    take((1, 2, 3))
                    dve.wait_ge(ig_ready, i * 4 + b * 2 + 3)
                    dve.tensor_tensor(U1[:, :], XC[:, :], IG[:, :], ALU.mult).then_inc(u1_done, 1)
                    dve.wait_ge(a_ready, blk + 1)
                    dve.scalar_tensor_tensor(M2[:, :], A2[:, :], 1.0, TH[:, :], ALU.add, ALU.mult).then_inc(m2_ready, 1)
                    take((1, 2, 3))
                    dve.wait_ge(mult_ready, blk + 1)
                    dve.tensor_tensor(UU[:, :], U1[:, :], MU[:, :], ALU.mult)
                    dve.drain()
                    dve.tensor_tensor_scan(HS[:, :], DA[:, :], UU[:, :], 0.0, ALU.mult, ALU.add)
                    dve.drain()
                    dve.wait_ge(gelu_ready, blk + 1)
                    dve.tensor_tensor(RF[:, :], HS[:, :], GY[:, :], ALU.mult)
                    dve.drain()
                    rhi, rlo = [x[:, bass.ds(blk, 1), :].rearrange("p a n -> p (a n)") for x in (RNhi, RNlo)]
                    dve.tensor_copy(rhi, RF[:, :])
                    dve.drain()
                    dve.tensor_tensor(rlo, RF[:, :], rhi.bitcast(F32), ALU.subtract).then_inc(rnn_done, 1)
            for i in range(1, QT):
                dve.tensor_scalar(NEG[i][:, :], SC[i][:, :], TAKEN, MASKED, ALU.not_equal, ALU.mult)
            dve.drain()
            dve.wait_ge(bias_in, 16)

            def logits(i, g):
                w = (i + 1) * P
                if i >= 1:
                    dve.wait_ge(pt_mm, (i - 1) * i + (g + 1) * i)
                for j in range(4):
                    c = i * NH + g * 4 + j
                    pr = PR[:, g, j, 0:w]
                    dve.wait_ge(logit_mm, c + 1)
                    dve.scalar_tensor_tensor(pr, A45[:, (c % 2) * 512:(c % 2) * 512 + w], HD ** -0.5,
                                             BIAS[:, g * 4 + j, S - w:S], ALU.mult, ALU.add).then_inc(logit_out, 1)
                    dve.drain()
                    dve.tensor_tensor_reduce(pr, pr, NEG[i][:, 0:w], 1.0, MASKED, ALU.add, ALU.max, mx[:, g, j:j + 1])
                dve.drain()
                dve.tensor_scalar(nmx[:, g, :], mx[:, g, :], -1.0, None, ALU.mult).then_inc(nmx_ready, 1)

            logits(0, 0)
            logits(0, 1)
            for i in range(QT):
                for g in range(2):
                    dve.wait_ge(exp_done, NH * i + 4 * (g + 1))
                    dve.reciprocal(rr[:, g, :], rs[:, g, :])
                    dve.drain()
                    for j in range(4):
                        pr = PR[:, g, j, 0:(i + 1) * P]
                        dve.tensor_scalar(pr, pr, rr[:, g, j:j + 1], None, ALU.mult)
                    dve.drain().then_inc(p_ready, 1)
                    if i + 1 < QT:
                        logits(i + 1, g)
                dve.wait_ge(at_hi, i + 1)
                dve.tensor_tensor(ATlo[:, :, i * P:(i + 1) * P], gp[i % 2][:, 512:1024].rearrange("p (j q) -> p j q", j=4),
                                  AThi[:, :, i * P:(i + 1) * P].bitcast(F32), ALU.subtract).then_inc(at_done, 1)

            dve.drain()
            dve.wait_ge(sga_ready, KC)
            with dve.Fori(0, 2) as i:
                for pr in range(2):
                    dve.wait_ge(unit_done, U_MRG + i * 10 + pr * 5 + 3 + 2)
                    for q in range(2):
                        ga = SGA[:, bass.ds(i * 4 + pr * 2 + q, 1), :].rearrange("p a n -> p (a n)")
                        dve.tensor_tensor(M1[:, q, :], gp[q][:, 0:S], ga, ALU.mult).then_inc(gp_free[q], 1)
                    dve.wait_ge(sg_ready, i * 4 + pr * 2 + 2)
                    for q in range(2):
                        dve.wait_ge(unit_done, U_MRG + i * 10 + pr * 5 + 4 + q + 2)
                        dve.tensor_tensor(MB[:, :], gp[q][:, 0:S], SGB[:, q, :], ALU.mult).then_inc(gp_free[q], 1)
                        dve.drain()
                        dve.tensor_tensor(MF[:, :], MB[:, :], M1[:, q, :], ALU.add)
                        dve.drain()
                        mhi, mlo = [x[:, bass.ds(i * 4 + pr * 2 + q, 1), :].rearrange("p a n -> p (a n)") for x in (MGhi, MGlo)]
                        dve.tensor_copy(mhi, MF[:, :])
                        dve.drain()
                        dve.tensor_tensor(mlo, MF[:, :], mhi.bitcast(F32), ALU.subtract).then_inc(merge_done, 1)
                        dve.drain()
            residual(U_OUT, 1, META, S, 2 * KC)
            norm_split(1)

            def split_act(i, done):
                ahi, alo = [x[:, bass.ds(i, 1), :].rearrange("p a n -> p (a n)") for x in (AChi, AClo)]
                dve.drain()
                dve.tensor_copy(ahi, AF[:, :])
                dve.drain()
                dve.tensor_tensor(alo, AF[:, :], ahi.bitcast(F32), ALU.subtract).then_inc(done, 1)
                dve.drain()

            dve.drain()
            with dve.Fori(0, FC) as i:
                def fv(c):
                    return V[:, bass.ds(VEC["ffn"] + i * 8 + c, 1)]
                for c, (y, first) in enumerate(((YV, yv_first), (YG, yg_first))):
                    dve.wait_ge(first, i + 1)
                    dve.scalar_tensor_tensor(y[:, 1:S], gp[c][:, 0:S - 1], fv(4 * c + 1), y[:, 1:S], ALU.mult, ALU.add)
                    dve.drain()
                    dve.scalar_tensor_tensor(y[:, 2:S], gp[c][:, 0:S - 2], fv(4 * c), y[:, 2:S], ALU.mult,
                                             ALU.add).then_inc(gp_free[c], 1)
                dve.drain().then_inc(yg_ready, 1)
                dve.wait_ge(silu_ready, i + 1)
                dve.tensor_tensor(AF[:, :], SL[:, :], YV[:, :], ALU.mult)
                split_act(i, act_done)
            residual(U_DN, 3, META, S, 5 * KC)
            norm_final(2, "g_final", h_ready)

            norm_split(3)
            dve.drain()
            for t in (HQ, HK, HL, HVT):
                dve.memset(t[:, 0:PAD], 0.0)
            dve.memset(AT2[:, :, :], 0.0)
            dve.memset(CX[:, 0:2], 0.0)
            dve.drain().then_inc(pads2, 1)
            with dve.Fori(0, KC // 2) as i:
                for hh in range(2):
                    h = i * 2 + hh
                    b0 = region(T)
                    dve.wait_ge(sf_ready, h + 1)
                    dve.tensor_scalar(HK[:, PAD:TP], HF[:, PAD:TP], LAM[:, 6, bass.ds(h, 1)], LAM[:, 5, bass.ds(h, 1)],
                                      ALU.mult, ALU.add).then_inc(f_ready, 1)
                    dve.drain()
                    dve.tensor_scalar(HK[:, PAD:TP], HK[:, PAD:TP], -1.0, 1.0, ALU.mult, ALU.add)
                    dve.wait_ge(lf_ready, h + 1)
                    dve.tensor_tensor_scan(HG[:, :], CON[:, C_RST:C_RST + TP], HL[:, :], 0.0, ALU.mult, ALU.add).then_inc(f_ready, 1)
                    dve.drain()

                    def boundary(l):
                        b = LEVELS[l]
                        g = HG[:, :].rearrange("p (j t) -> p j t", t=2 * b)
                        dve.tensor_tensor(DD[:, l % 2, :].rearrange("p (j t) -> p j t", t=2 * b), g,
                                          g[:, :, b - 1:b].to_broadcast([P, TP // (2 * b), 2 * b]), ALU.subtract).then_inc(d_ready, 1)

                    def weigh(l):
                        b = LEVELS[l]
                        dve.wait_ge(e_ready, i * 16 + hh * 8 + l + 1)
                        x, e, q, k = [t.rearrange("p (j two b) -> p j two b", two=2, b=b)
                                      for t in (XX[:, l % 2, :], EE[:, l % 2, :], HQ[:, :], HK[:, :])]
                        dve.tensor_tensor(x[:, :, 1, :], q[:, :, 1, :], e[:, :, 1, :], ALU.mult)
                        dve.tensor_tensor(x[:, :, 0, :], k[:, :, 0, :], e[:, :, 0, :], ALU.mult)
                        dve.drain().then_inc(lx_ready, 1)

                    def place(l):
                        b = LEVELS[l]
                        dve.wait_ge(lev_mm, i * 16 + hh * 8 + l + 1)
                        dve.memset(probe[0:1, 1:2], 0.0)
                        m = CON[:, C_LEV + 64 * l:C_LEV + 64 * (l + 1)].bitcast(U32)
                        dve.copy_predicated(
                            AT2[:, :, :].rearrange("p c (j two b) -> p c j two b", two=2, b=b)[:, :, :, 1, :],
                            m.rearrange("p (o j b) -> p o j b", o=1, b=b).to_broadcast([P, CH, 64 // b, b]),
                            A45[:, (l % 2) * 512:(l % 2) * 512 + CH * 64].rearrange("p (c j b) -> p c j b", c=CH, b=b)
                        ).then_inc(lev_out, 1)

                    dve.wait_ge(hq_ready, h + 1)
                    dve.wait_ge(o_mm, h + 1)
                    boundary(0)
                    boundary(1)
                    for l in range(len(LEVELS)):
                        weigh(l)
                        if l + 2 < len(LEVELS):
                            boundary(l + 2)
                        if l >= 1:
                            place(l - 1)
                        if l == 2:
                            dve.wait_ge(cg_ready, h + 1)
                            dve.wait_ge(unit_done, U_MIX2 + i * 18 + hh * 9 + 4 + 1 + 2)
                            g = (hh * 9 + 4) % 2
                            dve.tensor_tensor(CX[:, 2:2 + T], gp[g][:, b0:b0 + T], CG[:, :], ALU.mult).then_inc(cx_ready, 1)
                            dve.drain().then_inc(gp_free[g], 1)
                    dve.tensor_tensor(XX[:, 1, :], HQ[:, :], HK[:, :], ALU.mult)
                    dve.drain().then_inc(lx_ready, 1)
                    g = HG[:, 0:TP - P].rearrange("p (c t) -> p c t", t=P)
                    dve.tensor_tensor(DD[:, 1, 0:TP - P].rearrange("p (c t) -> p c t", t=P), g,
                                      g[:, :, P - 1:P].to_broadcast([P, CH - 1, P]), ALU.subtract).then_inc(d_ready, 1)
                    place(len(LEVELS) - 1)
                    dve.drain()
                    dve.wait_ge(lev_mm, i * 16 + hh * 8 + 8)
                    dve.memset(probe[0:1, 2:3], 0.0)
                    dve.copy_predicated(AT2[:, :, :], ident.bitcast(U32).rearrange("p (o t) -> p o t", o=1).to_broadcast([P, CH, P]),
                                        A67[:, 0:TP].rearrange("p (c t) -> p c t", c=CH)).then_inc(lev_out, 1)
                    dve.wait_ge(e_ready, i * 16 + hh * 8 + 8)
                    dve.tensor_tensor(XX[:, 0, 0:TP - P], HK[:, 0:TP - P], EE[:, 1, 0:TP - P], ALU.mult)
                    dve.drain().then_inc(lx_ready, 1)
                    dve.wait_ge(eg_ready, h + 1)
                    dve.tensor_tensor(QG[:, P:TP], HQ[:, P:TP], EG[:, P:TP], ALU.mult).then_inc(qg_ready, 1)
                    dve.wait_ge(yb_first, h + 1)
                    for tap in (1, 0):
                        dve.scalar_tensor_tensor(YB[:, :], CX[:, tap:tap + T], V[:, bass.ds(VEC["conv2"] + h * 4 + tap, 1)],
                                                 YB[:, :], ALU.mult, ALU.add)
                        dve.drain()
                    dve.wait_ge(side_ready, i * 8 + hh * 4 + 1)
                    dve.tensor_tensor(YB[:, :], YB[:, :], BG[:, :], ALU.mult)
                    dve.wait_ge(state_mm, h + 1)
                    dve.tensor_copy(ST[:, 0, :], A45[:, 0:P])
                    for c in range(1, CH - 1):
                        dve.drain()
                        dve.scalar_tensor_tensor(ST[:, c, :], ST[:, c - 1, :], EG[:, c * P + P - 1:c * P + P],
                                                 A45[:, c * P:(c + 1) * P], ALU.mult, ALU.add)
                    dve.drain().then_inc(state_ready, 1)
                    dve.wait_ge(side_ready, i * 8 + hh * 4 + 4)
                    dve.tensor_tensor(YB[:, :], YB[:, :], SB2[:, :], ALU.mult)
                    dve.wait_ge(orstd_ready, h + 2)
                    dve.scalar_tensor_tensor(ON[:, :], A67[:, PAD:TP], vec("hgrn_norm", 0), HRS[:, :], ALU.mult,
                                             ALU.mult).then_inc(on_ready, 1)
                    dve.drain()
                    dve.tensor_tensor(ON[:, :], ON[:, :], SO[:, :], ALU.mult)
                    dve.drain()
                    dve.tensor_tensor(ON[:, :], ON[:, :], SA[:, :], ALU.mult)
                    dve.drain()
                    dve.tensor_tensor(MF2[:, :], ON[:, :], YB[:, :], ALU.add)
                    dve.drain()
                    mhi, mlo = [x[:, bass.ds(h, 1), :].rearrange("p a n -> p (a n)") for x in (M2hi, M2lo)]
                    dve.tensor_copy(mhi, MF2[:, :])
                    dve.drain()
                    dve.tensor_tensor(mlo, MF2[:, :], mhi.bitcast(F32), ALU.subtract).then_inc(mix2_done, 1)
                    dve.drain()
            residual(U_OUT2, 1, META - 2, S + 2, None)
            norm_split(4)

            dve.drain()
            with dve.Fori(0, FC) as i:
                b0 = region(S + 2)
                dve.wait_ge(ya_first, i + 1)
                for tap in (1, 0):
                    ins = dve.scalar_tensor_tensor(YV[:, :], gp[0][:, b0 + tap:b0 + tap + S],
                                                   V[:, bass.ds(VEC["ffn2"] + i * 4 + tap, 1)], YV[:, :], ALU.mult, ALU.add)
                    if tap:
                        dve.drain()
                ins.then_inc(gp_free[0], 1)
                dve.drain().then_inc(ya_ready, 1)
                dve.wait_ge(silu2_ready, i + 1)
                dve.wait_ge(unit_done, U_UP2 + i * 2 + 2 + 2)
                dve.tensor_tensor(AF[:, :], gp[1][:, 0:S], SL[:, :], ALU.mult).then_inc(gp_free[1], 1)
                split_act(i, act2_done)
            residual(U_DN2, 3, META, S, None)
            norm_final(5, "final2", out_ready)


def _constants():
    c = np.zeros((P, NCONST), np.float32)
    c[:, C_ID:C_ID + P] = np.eye(P)
    c[:, C_ONE:C_ONE + P] = 1.0
    c[:, C_MEAN:C_MEAN + P] = 1.0 / D
    c[:, C_HMEAN:C_HMEAN + P] = 1.0 / P
    r = np.arange(P)
    c[:, C_TRI:C_TRI + P] = np.where(r[None, :] <= r[:, None], 0.0, MASKED)
    for l, b in enumerate(LEVELS):
        upper = r[(r % (2 * b)) >= b]
        c[:, C_LEV + 64 * l:C_LEV + 64 * (l + 1)] = ((r[:, None] // (2 * b) == upper[None, :] // (2 * b))
                                                     & (r[:, None] % (2 * b) < b))
    c[:, C_RST:] = (np.arange(TP) % P != 0)[None, :]
    return c


def _buckets():
    n = np.maximum(S - 1 - np.arange(BIAS_W), 0)
    large = 16 + (np.log(np.maximum(n, 1).astype(np.float32) / 16) / np.log(8.0) * 16).astype(np.int32)
    bucket = np.where(n < 16, n, np.minimum(large, 31))
    return (np.arange(32)[:, None] == bucket[None, :]).astype(np.float32)


def kernel(**inputs):
    import concourse.bacc as bacc
    from concourse.bass_utils import run_bass_kernel_spmd

    a = {k: np.ascontiguousarray(v) for k, v in inputs.items()}

    def chunks(w):
        k, n = w.shape
        return w.reshape(k // P, P, n // P, P).transpose(2, 1, 0, 3).reshape(n // P, P, (k // P) * P)

    def cols(v):
        return v.reshape(-1, P).T

    def heads(w, n):
        return w.reshape(w.shape[:-1] + (2, 4, HD)).swapaxes(-3, -2).reshape(w.shape[:-1] + (n,))

    w_in, b_in = a["w_in"][0], a["b_in"][0]
    cut = np.cumsum([512, 128, 128, 512, 64, 8, D, D, D, D])[:-1]
    wq, wk, wv, wqi, wki, wwi, wxr, wyr, wga, wgb = np.split(w_in, cut, axis=1)
    bq, bk, bv, bqi, bki, bwi, bxr, byr, bga, bgb = np.split(b_in, cut)
    wi_pad = np.concatenate([wwi, np.zeros((D, P - NH), np.float32)], 1)
    proj = [chunks(wqi), chunks(np.concatenate([wki, wki], 1)), chunks(wi_pad), chunks(heads(wq, 512)), chunks(wv), chunks(wk)]
    rnn = np.stack([chunks(wxr), chunks(wyr), chunks(wga)], 1).reshape(3 * KC, P, UNIT)
    woa = a["w_o_attn"][0].reshape(2, 4, HD, D).swapaxes(0, 1).reshape(512, D)
    woa = chunks(woa).reshape(KC // 2, 2, P, 512).transpose(0, 2, 1, 3).reshape(KC // 2, 1, P, UNIT)
    gates = chunks(wgb).reshape(KC // 2, 2, P, UNIT)
    wor = chunks(a["w_o_rnn"][0]).reshape(KC // 2, 2, P, UNIT)
    merge = np.concatenate([gates, woa, wor], 1).reshape(-1, P, UNIT)

    def up(w):
        return chunks(w).reshape(2, FC, P, UNIT).swapaxes(0, 1).reshape(2 * FC, P, UNIT)

    def down(w):
        t = chunks(w)
        t = np.concatenate([t, np.zeros((KC, P, 3 * UNIT - FF), np.float32)], 2)
        return t.reshape(KC, P, 3, UNIT).transpose(0, 2, 1, 3).reshape(3 * KC, P, UNIT)

    w2 = chunks(a["w_in_2"][0]).reshape(9, KC, P, UNIT)
    mix2 = w2[[1, 0, 2, 5, 6, 4, 3, 7, 8]].swapaxes(0, 1).reshape(9 * KC, P, UNIT)
    units = np.concatenate(proj + [rnn, merge, chunks(a["w_out"][0]), up(a["w_up"][0]), down(a["w_down"][0]), mix2,
                                   chunks(a["w_out_2"][0]), up(a["w_up_2"][0]), down(a["w_down_2"][0])], 0)

    cw, fw, fb = a["conv_rnn_w"][0], a["conv_ffn_w"][0], a["conv_ffn_b"][0]
    rnn_rows = [bxr, byr, cw[0], cw[1], cw[2], cw[3], a["conv_rnn_b"][0], a["b_rg"][0], a["b_ig"][0]]
    rnn_rows += [np.zeros(D, np.float32)] * (16 - len(rnn_rows))

    def inter(rows):
        return np.stack([cols(r) for r in rows], 2).reshape(P, -1)

    ffn_rows = [fw[0, :FF], fw[1, :FF], fw[2, :FF], fb[:FF], fw[0, FF:], fw[1, FF:], fw[2, FF:], fb[FF:]]
    c2, f2 = a["conv_w_2"][0], a["ffn_conv_w_2"][0]
    parts = [("b_ada", cols(a["b_ada"][0])), ("g_mix", cols(a["g_mix"][0])), ("b_qi", cols(bqi)),
             ("b_ki", cols(np.concatenate([bki, bki]))),
             ("b_wi", cols(np.concatenate([bwi, np.zeros(P - NH, np.float32)]))), ("b_q", cols(heads(bq, 512))),
             ("b_v", cols(bv)), ("b_k", cols(bk)),
             ("rnn", inter(rnn_rows)), ("b_gates", inter([bga, bgb])), ("lam", cols(a["lru_lambda"][0])),
             ("g_ffn", cols(a["g_ffn"][0])), ("ffn", inter(ffn_rows)), ("g_final", cols(a["g_final"])),
             ("lb0", cols(a["lb_param_2"][0])), ("lb1", cols(a["lb_param_2"][1])), ("attn_norm", cols(a["attn_norm_w_2"][0])),
             ("hgrn_norm", cols(a["hgrn_norm_w_2"][0])), ("conv2", inter([c2[0], c2[1], c2[2], np.zeros(D, np.float32)])),
             ("ffn_norm", cols(a["ffn_norm_w_2"][0])),
             ("ffn2", inter([f2[0], f2[1], f2[2], a["ffn_conv_b_2"][0]])), ("final2", cols(a["final_norm_w_2"]))]
    assert [n for n, _ in parts] == list(VEC)
    gatew = np.concatenate([a["w_rg"][0], a["w_ig"][0]], 2)
    arrays = {
        "xT": a["x"][0].T.reshape(KC, P, S).swapaxes(0, 1),
        "metaT": a["meta_tokens_2"].T.reshape(KC, P, META).swapaxes(0, 1),
        "vecs": np.concatenate([v for _, v in parts], 1),
        "rel": a["rel_bias"],
        "onehot": _buckets(),
        "consts": _constants(),
        "crow": a["c"][0],
        "ada": a["w_ada"][0].T.reshape(6 * KC, P, D),
        "gatew": gatew,
        "units": units,
    }
    nc = bacc.Bacc("TRN2", target_bir_lowering=False, num_devices=1)
    args, feed = [], {}
    for name, v in arrays.items():
        feed[name] = np.ascontiguousarray(v)
        args.append(nc.dram_tensor(name, v.shape, F32, kind="ExternalInput").ap())
    args.append(nc.dram_tensor("bias_rows", (NH, P, BIAS_W), F32, kind="Internal").ap())
    args.append(nc.dram_tensor("out", (P, KC, S), F32, kind="ExternalOutput").ap())
    build(nc, *args)
    r = run_bass_kernel_spmd(nc, [feed], core_ids=[0])
    o = np.asarray(r.results[0]["out"])
    return np.ascontiguousarray(o.transpose(2, 1, 0)).reshape(1, S, D)
```

```python
import numpy as np
import concourse.bass as bass
from concourse import mybir
from contextlib import ExitStack

F32 = mybir.dt.float32
F32R = mybir.dt.float32r
U32 = mybir.dt.uint32
ALU = mybir.AluOpType
ACT = mybir.ActivationFunctionType
P = 128

D = 1024
KC = D // P
S = 512
META = 16
T = META + S
PAD = P - META
TP = PAD + T
CH = TP // P
QT = S // P
NH, HD, TOPK = 8, 64, 128
FF = 2816
FC = FF // P
UNIT = KC * P
EPS = 1e-6
MASKED, TAKEN = -3.0e38, -3.4e38
LEVELS = [64, 32, 16, 8, 4, 2, 1]

U_QI, U_KI, U_WI, U_Q = 0, 4, 5, 6
U_RNN = 10
U_V = U_RNN + 3 * KC
U_K = U_V + 1
U_ROUT = U_K + 1
U_MRG = U_ROUT + KC
U_OUT = U_MRG + 3 * (KC // 2)
U_UP = U_OUT + KC
U_DN = U_UP + 2 * FC
U_MIX2 = U_DN + 3 * KC
U_OUT2 = U_MIX2 + 9 * KC
U_UP2 = U_OUT2 + KC
U_DN2 = U_UP2 + 2 * FC
UNITS = U_DN2 + 3 * KC
G_PROJ = 0
G_RNN = 10
G_KV = G_RNN + 3 * KC
G_ROUT = G_KV + 2
G_MRG = G_ROUT + KC
G_OUT = G_MRG + 2 * KC
G_UP = G_OUT + KC
G_DN = G_UP + 2 * FC
G_MIX2 = G_DN + KC
G_OUT2 = G_MIX2 + 9 * KC
G_UP2 = G_OUT2 + KC
G_DN2 = G_UP2 + 2 * FC
RAW = 2
ADA_FIRST = 2 * KC
ADA_SECOND = 2 * KC
ADA_SLOTS = 8

VEC = {}
_at = 0
for _n, _w in (("b_ada", 6 * KC), ("g_mix", KC), ("b_qi", 4), ("b_ki", 1), ("b_wi", 1), ("b_q", 4),
               ("b_v", 1), ("b_k", 1),
               ("rnn", 16 * KC), ("b_gates", 2 * KC), ("lam", KC), ("g_ffn", KC), ("ffn", 8 * FC), ("g_final", KC),
               ("lb0", KC), ("lb1", KC), ("attn_norm", KC), ("hgrn_norm", 1), ("conv2", 4 * KC), ("ffn_norm", KC),
               ("ffn2", 4 * FC), ("final2", KC)):
    VEC[_n] = _at
    _at += _w
NVEC = _at
C_ID, C_MEAN, C_ONE, C_TRI, C_HMEAN, C_EMEAN = [j * P for j in range(6)]
C_LEV = 6 * P
C_RST = C_LEV + 64 * len(LEVELS)
NCONST = C_RST + TP
BIAS_W = S + P


def spans(n):
    return [(0, n)] if n <= 512 else [(0, (n // 2 + 1) // 2 * 2), ((n // 2 + 1) // 2 * 2, n - (n // 2 + 1) // 2 * 2)]


def region(n):
    return 0 if n <= 512 else 512 - spans(n)[0][1]


def build(nc, xT, metaT, vecs, rel, onehot, consts, crow, ada, gatew, units, scratch, out):
    with ExitStack() as ctx:
        def sb(name, shape, dt=F32, frame=ctx):
            return frame.enter_context(nc.sbuf_tensor(name, shape, dt))

        def sem(name):
            return ctx.enter_context(nc.semaphore(name))

        H = sb("H", [P, KC, T])
        XNhi = sb("XNhi", [P, KC, T], F32R)
        XNlo = sb("XNlo", [P, KC, T], F32R)
        raw = [sb(f"raw{s}", [P, UNIT]) for s in range(RAW)]
        Whi = [sb(f"Whi{s}", [P, KC, P], F32R) for s in range(2)]
        Wlo = [sb(f"Wlo{s}", [P, KC, P], F32R) for s in range(2)]
        V = sb("V", [P, NVEC])
        MOD = sb("MOD", [P, 6 * KC])
        MOD4 = sb("MOD4", [P, 4])
        AB1 = sb("AB1", [P, KC])
        AB2 = sb("AB2", [P, KC])
        GW = sb("GW", [P, KC])
        MSQ = sb("MSQ", [P, KC, META])
        MRS = sb("MRS", [P, META])
        LAM = sb("LAM", [P, 9, KC])
        probe = sb("probe", [P, 32])
        ZERO = sb("ZERO", [P, KC])
        ONES = sb("ONES", [1, P])
        CON = sb("CON", [P, NCONST])
        sq = sb("sq", [P, 2, T])
        CS = sb("CS", [P, D])
        SQS = sb("SQS", [P, T])
        RSTD = sb("RSTD", [P, T])
        ident, ones, tri, mean, head_mean, eps_mean = [CON[:, c:c + P] for c in (C_ID, C_ONE, C_TRI, C_MEAN, C_HMEAN, C_EMEAN)]
        gp = [ctx.enter_context(nc.psum_tensor(f"gp{s}", [P, 1024], F32)) for s in range(2)]
        A45 = ctx.enter_context(nc.psum_tensor("A45", [P, 1024], F32))
        A67 = ctx.enter_context(nc.psum_tensor("A67", [P, 1024], F32))

        with ExitStack() as f:
            nt = sb("nt", [P, 3, T], frame=f)
            RST1 = sb("RST1", [P, S], frame=f)
        with ExitStack() as f:
            with ExitStack() as fi:
                QI = sb("QI", [P, 4, S], frame=fi)
                KI = sb("KI", [P, S], frame=fi)
                RL = sb("RL", [P, 2, S], frame=fi)
                WIT = sb("WIT", [P, S], frame=fi)
            RG8 = sb("RG8", [P, KC, S], frame=f)
            with ExitStack() as fw:
                AW = [sb(f"AW{s}", [P, UNIT], frame=fw) for s in range(ADA_SLOTS)]
            RNhi = sb("RNhi", [P, KC, S], F32R, f)
            RNlo = sb("RNlo", [P, KC, S], F32R, f)
            with ExitStack() as fq:
                Q = sb("Q", [P, 4, S], frame=fq)
                CR = sb("CR", [P, D], frame=fq)
            AThi = sb("AThi", [P, 4, S], F32R, f)
            ATlo = sb("ATlo", [P, 4, S], F32R, f)
            with ExitStack() as fa:
                K = sb("K", [P, S], frame=fa)
                VT = sb("VT", [P, QT, P], frame=fa)
                WI = sb("WI", [P, QT, NH], frame=fa)
                BIAS = sb("BIAS", [P, NH, S], frame=fa)
                SC = [None] + [sb(f"SC{i}", [P, (i + 1) * P], frame=fa) for i in range(1, QT)]
                NEG = [tri] + SC[1:]
                m8 = sb("m8", [P, QT, 8], frame=fa)
                mx, nmx, rs, rr = [sb(n, [P, 2, 4], frame=fa) for n in ("mx", "nmx", "rs", "rr")]
                with ExitStack() as fb:
                    OH = sb("OH", [32, BIAS_W], frame=fb)
                    RB = sb("RB", [NH, BIAS_W], frame=fb)
                    REL = sb("REL", [32, NH], frame=fb)
                with ExitStack() as fr:
                    XR = sb("XR", [P, 3 + S], frame=fr)
                    XC, GY, RG, IG, DA, TH, M2, U1 = [sb(f"rnn_{n}", [P, S], frame=fr) for n in
                                                      ("xc", "gelu", "r", "i", "a", "tanh", "mult2", "u")]
                    A2 = HS = RG
                    MU, UU, RF = M2, U1, GY
                    WG = sb("WG", [P, 2 * P], frame=fr)
                with ExitStack() as fp:
                    PR = sb("PR", [P, 2, 4, S], frame=fp)
            PTs = sq[:, :, 0:S]
            VV = RSTD[:, 0:S]
            with ExitStack() as fm:
                MGhi = sb("MGhi", [P, KC, S], F32R, fm)
                MGlo = sb("MGlo", [P, KC, S], F32R, fm)
                SG = sb("SG", [P, 2, S], frame=fm)
                AWM = [sb("AWM", [P, UNIT], frame=fm), sq[:, :, :].rearrange("p a n -> p (a n)")[:, 0:UNIT]]
                MB = sb("MB", [P, S], frame=fm)
                MF = sb("MF", [P, S], frame=fm)
        with ExitStack() as f:
            AChi = sb("AChi", [P, FC, S], F32R, f)
            AClo = sb("AClo", [P, FC, S], F32R, f)
            SQG = sb("SQG", [P, 2, S], frame=f)
            SQGS = sb("SQGS", [P, S], frame=f)
            YV, YG, SL, AF = [sb(f"ffn_{n}", [P, S], frame=f) for n in ("val", "gate", "silu", "act")]
        with ExitStack() as f:
            M2hi = sb("M2hi", [P, KC, T], F32R, f)
            M2lo = sb("M2lo", [P, KC, T], F32R, f)
            HF, HL, HQ, HK, HG, EG, QG = [sb(f"h_{n}", [P, TP], frame=f) for n in
                                          ("sig", "logf", "q", "k", "G", "expG", "qG")]
            HVT = sb("HVT", [P, TP], frame=f)
            HV = sb("HV", [P, CH, P], frame=f)
            DD = sb("DD", [P, 2, TP], frame=f)
            EE = sb("EE", [P, 2, TP], frame=f)
            XX = sb("XX", [P, 2, TP], frame=f)
            AT2 = sb("AT2", [P, CH, P], frame=f)
            KDT = sb("KDT", [P, CH - 1, P], frame=f)
            ST = sb("ST", [P, CH - 1, P], frame=f)
            CG, BG, SO, SA, SB2, SQ, ON, YB, MF2, HRS = [sb(f"h_{n}", [P, T], frame=f) for n in
                                                    ("cg", "bg", "silu_g", "sig_a", "sig_b", "sq", "on", "yb", "mf",
                                                     "rstd")]
            CX = sb("CX", [P, 2 + T], frame=f)

        small_in = sem("small_in")
        eps_ready, row_ready, row_mm = sem("eps_ready"), sem("row_ready"), sem("row_mm")
        con_in = sem("con_in")
        x_in = sem("x_in")
        bias_saved = sem("bias_saved")
        bias_in = sem("bias_in")
        raw_in = [sem(f"raw_in{s}") for s in range(RAW)]
        ada_in = [sem(f"ada_in{s}") for s in range(ADA_SLOTS)]
        ada3_in = [sem(f"ada3_in{s}") for s in range(2)]
        gate_in = sem("gate_in")
        hi_made = sem("hi_made")
        weights_ready = sem("weights_ready")
        unit_done = sem("unit_done")
        gp_free = [sem(f"gp_free{s}") for s in range(2)]
        rb_mm, rb_copied = sem("rb_mm"), sem("rb_copied")
        silu_c, ada_done, mod_ready = sem("silu_c"), sem("ada_done"), sem("mod_ready")
        lam_neg, lam_exp, lam_done = sem("lam_neg"), sem("lam_exp"), sem("lam_done")
        lb_max, lb_exp, lb_done = sem("lb_max"), sem("lb_exp"), sem("lb_done")
        sq_ready, stat_mm, rstd_ready = sem("sq_ready"), sem("stat_mm"), sem("rstd_ready")
        sums_ready, sumg_ready, statg_mm = sem("sums_ready"), sem("sumg_ready"), sem("statg_mm")
        sqg_ready, rst1_ready, meta_sq, meta_mm, meta_rstd, meta_xn = [sem(n) for n in ("sqg_ready", "rst1_ready", "meta_sq", "meta_mm",
                                                                              "meta_rstd", "meta_xn")]
        nt_ready, xhi_ready, xn_ready = sem("nt_ready"), sem("xhi_ready"), sem("xn_ready")
        h_ready, out_ready, out_saved = sem("h_ready"), sem("out_ready"), sem("out_saved")
        proj_out, wi_mm, wi_ready, v_mm, v_ready = (sem("proj_out"), sem("wi_mm"), sem("wi_ready"), sem("v_mm"),
                                                    sem("v_ready"))
        score_mm, relu_done, score_acc = sem("score_mm"), sem("relu_done"), sem("score_acc")
        logit_mm, logit_out, nmx_ready = sem("logit_mm"), sem("logit_out"), sem("nmx_ready")
        exp_done, p_ready, pt_mm, pt_copied = sem("exp_done"), sem("p_ready"), sem("pt_mm"), sem("pt_copied")
        pv_mm, at_hi, at_done = sem("pv_mm"), sem("at_hi"), sem("at_done")
        xr_pad, conv_first, xc_ready, gelu_ready = sem("xr_pad"), sem("conv_first"), sem("xc_ready"), sem("gelu_ready")
        gate_mm, ig_ready, a_ready, m2_ready = sem("gate_mm"), sem("ig_ready"), sem("a_ready"), sem("m2_ready")
        mult_ready, u1_done, rnn_done = sem("mult_ready"), sem("u1_done"), sem("rnn_done")
        rgate_ready, at_half = sem("rgate_ready"), sem("at_half")
        sg_ready, merge_done = sem("sg_ready"), sem("merge_done")
        yv_first, yg_first, yg_ready, silu_ready, act_done = (sem("yv_first"), sem("yg_first"), sem("yg_ready"),
                                                              sem("silu_ready"), sem("act_done"))
        ya_first, ya_ready, silu2_ready, act2_done = sem("ya_first"), sem("ya_ready"), sem("silu2_ready"), sem("act2_done")
        pads2 = sem("pads2")
        sf_ready, lf_ready, hq_ready = sem("sf_ready"), sem("lf_ready"), sem("hq_ready")
        hvt_ready, hv_mm, hv_ready = sem("hvt_ready"), sem("hv_mm"), sem("hv_ready")
        f_ready, d_ready, e_ready, lx_ready = sem("f_ready"), sem("d_ready"), sem("e_ready"), sem("lx_ready")
        lev_mm, lev_out = sem("lev_mm"), sem("lev_out")
        kdt_mm, kdt_ready, state_mm, state_ready = sem("kdt_mm"), sem("kdt_ready"), sem("state_mm"), sem("state_ready")
        eg_ready, qg_ready, o_mm, osq_ready, ostat_mm = (sem("eg_ready"), sem("qg_ready"), sem("o_mm"), sem("osq_ready"),
                                                         sem("ostat_mm"))
        orstd_ready, on_ready, cg_ready, cx_ready = sem("orstd_ready"), sem("on_ready"), sem("cg_ready"), sem("cx_ready")
        yb_first, side_ready, mix2_done = sem("yb_first"), sem("side_ready"), sem("mix2_done")

        def vec(name, k, w=1):
            return V[:, bass.ds(VEC[name] + k, w)]

        def first_chunk(l):
            return 1 if P - LEVELS[l] <= PAD else 0

        def slot_free(g, c=0):
            return (g + c) // 2 + 1

        FUSED = 2
        NORMS = [dict(c0=META, n=S, feeds=0, h0=None), dict(c0=META, n=S, feeds=1, h0=0),
                 dict(c0=META, n=S, feeds=2, h0=KC), dict(c0=META - 2, n=S + 2, feeds=3, h0=2 * KC),
                 dict(c0=META, n=S, feeds=None, h0=3 * KC)]

        def scale_bias(m, k):
            return {0: (AB1[:, k:k + 1], MOD[:, k:k + 1]), 1: (AB2[:, k:k + 1], MOD[:, 3 * KC + k:3 * KC + k + 1]),
                    2: (GW[:, k:k + 1], ZERO[:, k:k + 1]), 3: (vec("ffn_norm", k), ZERO[:, k:k + 1])}[m]

        one_ahead = [xc_ready, rnn_done, merge_done, act_done, f_ready, qg_ready, o_mm, mix2_done, act2_done, lx_ready,
                     ig_ready, orstd_ready, on_ready, gate_mm, hv_mm, u1_done]

        block = ctx.enter_context(nc.Block())

        @block.sync
        def _(sp):
            sp.dma_start(CR[0:1, :], crow.rearrange("(o d) -> o d", o=1)).then_inc(small_in, 16)
            sp.dma_start(REL[:, :], rel).then_inc(small_in, 16)
            sp.dma_start(OH[:, :], onehot).then_inc(small_in, 16)
            sp.dma_start(V[:, :], vecs).then_inc(small_in, 16)
            sp.dma_start(CON[:, 0:C_ONE], consts[:, 0:C_ONE]).then_inc(small_in, 16)
            sp.dma_start(H[:, :, META:T], xT).then_inc(x_in, 16)
            sp.dma_start(H[:, :, 0:META], metaT).then_inc(x_in, 16)

            def load_ada(i, s):
                sp.wait_ge(ada_done, i * ADA_SLOTS + s + 1)
                sp.dma_start(AW[s][:, :], ada[bass.ds(i * ADA_SLOTS + s, 1), :, :]).then_inc(ada_in[s], 16)

            with sp.Fori(0, ADA_FIRST // ADA_SLOTS) as i:
                for s in range(ADA_SLOTS):
                    load_ada(i, s)
            def load_units(first, last):
                with sp.Fori(first // RAW, last // RAW) as i:
                    for s in range(RAW):
                        sp.wait_ge(weights_ready, i * RAW + s + 1)
                        sp.dma_start(raw[s][:, :], units[bass.ds(i * RAW + s, 1), :, :]).then_inc(raw_in[s], 16)

            load_units(0, RAW)
            with sp.Fori(0, ADA_SECOND // ADA_SLOTS) as i:
                for b in range(4):
                    sp.wait_ge(weights_ready, i * 4 + b + RAW + 1)
                    sp.dma_start(raw[b % 2][:, :], units[bass.ds(i * 4 + b + RAW, 1), :, :]).then_inc(raw_in[b % 2], 16)
                    for c in range(2):
                        load_ada(i + ADA_FIRST // ADA_SLOTS, b * 2 + c)
            sp.dma_start(CON[:, C_ONE:], consts[:, C_ONE:]).then_inc(con_in, 16)
            load_units(U_RNN, U_RNN + 2)
            sp.wait_ge(rb_copied, 1)
            sp.dma_start(scratch, RB[:, :].rearrange("h (o m) -> h o m", o=1).to_broadcast([NH, P, BIAS_W])).then_inc(bias_saved, 16)
            sp.wait_ge(bias_saved, 16)
            sp.dma_start(BIAS[:, :, :], bass.AP(scratch.tensor, P - 1, [[BIAS_W - 1, P], [P * BIAS_W, NH], [1, S]])).then_inc(bias_in, 16)
            load_units(U_RNN + 2, U_MRG + 4)
            sp.wait_ge(at_done, QT)
            with sp.Fori(0, 2) as i:
                for pr in range(2):
                    def unit_ahead(c):
                        n = pr * 3 + c
                        sp.wait_ge(weights_ready, U_MRG + 4 + i * 6 + n + 1)
                        sp.dma_start(raw[n % 2][:, :], units[bass.ds(U_MRG + 4 + i * 6 + n, 1), :, :]).then_inc(raw_in[n % 2], 16)

                    def two_chunks(n):
                        for c in range(2):
                            sp.wait_ge(ada_done, ADA_FIRST + ADA_SECOND + ADA_SLOTS + i * 8 + pr * 4 + n + c - 1)
                            sp.dma_start(AWM[c][:, :], ada[bass.ds(ADA_FIRST + ADA_SECOND + i * 8 + pr * 4 + n + c, 1), :, :]).then_inc(ada3_in[c], 16)

                    two_chunks(0)
                    unit_ahead(0)
                    unit_ahead(1)
                    two_chunks(2)
                    unit_ahead(2)
            load_units(U_MRG + 4 + 12, UNITS)
            for k in range(KC):
                sp.wait_ge(out_ready, k + 1)
                sp.dma_start(out[:, k, :], H[:, k, META:T]).then_inc(out_saved, 16)
            sp.wait_ge(out_saved, 16 * KC)

        @block.gpsimd
        def _(pool):
            pool.memset(ZERO[:, :], 0.0).then_inc(weights_ready, RAW)
            with pool.Fori(0, UNITS // 2) as i:
                for s in range(2):
                    u = i * 2 + s
                    src = raw[s][:, :]
                    hi, lo = [w[s][:, :, :].rearrange("p k n -> p (k n)") for w in (Whi, Wlo)]
                    pool.wait_ge(raw_in[s], i * 16 + 16)
                    pool.wait_ge(unit_done, u + 1)
                    pool.tensor_tensor(probe[0:1, 0:1], src[0:1, 0:1], src[0:1, 0:1], ALU.add)
                    pool.tensor_scalar(hi, src, 1.0, 1.0, ALU.mult, ALU.mult).then_inc(hi_made, 1)
                    pool.wait_ge(hi_made, u + 1)
                    pool.tensor_tensor(lo, src, hi.bitcast(F32), ALU.subtract).then_inc(weights_ready, 1)

        @block.tensor
        def _(pe):
            def three(dst, s, k, rhi, rlo, start, stop):
                pe.matmul(dst, Whi[s][:, k, :], rhi, start=start, stop=False)
                pe.matmul(dst, Whi[s][:, k, :], rlo, start=False, stop=False)
                return pe.matmul(dst, Wlo[s][:, k, :], rhi, start=False, stop=stop)

            def unit(u, s, dst, n, hi, lo, c0, ks, first=0, last=None, arrive=None):
                pe.wait_ge(weights_ready, u + 1 + RAW)
                base = region(n)
                for j, k in enumerate(ks):
                    kc = first + j
                    if arrive is not None:
                        pe.wait_ge(arrive[0], arrive[1] + kc + 1)
                    for a, w in spans(n):
                        mm = three(dst[:, base + a:base + a + w], s, k, hi[:, kc, c0 + a:c0 + a + w],
                                   lo[:, kc, c0 + a:c0 + a + w], kc == 0, kc == last)
                return mm

            def first_pair(u0, g0, f, halves):
                lag = 6
                for j in range(KC + lag):
                    for c, k in ((0, j), (1, j - lag)):
                        if 0 <= k < KC:
                            if k == 0:
                                pe.wait_ge(weights_ready, u0 + c + 1 + RAW)
                                pe.wait_ge(gp_free[c], slot_free(g0))
                            if c == 0:
                                pe.wait_ge(xn_ready, KC * f + k + 1)
                            n, c0 = halves[c]
                            for a, w in spans(n):
                                b = region(n) + a
                                mm = three(gp[c][:, b:b + w], c, k, XNhi[:, k, c0 + a:c0 + a + w], XNlo[:, k, c0 + a:c0 + a + w],
                                           k == 0, k == KC - 1)
                            if k == KC - 1:
                                mm.then_inc(unit_done, 1)

            def first_stats():
                for k in range(KC):
                    pe.wait_ge(sq_ready, k + 1)
                    pe.matmul(A67[:, 0:S], mean, sq[:, k % 2, 0:S], start=(k == 0), stop=(k == KC - 1)).then_inc(stat_mm, 1)

            def stats(m):
                n, base = NORMS[m]["n"], region(NORMS[m]["n"])
                pe.wait_ge(rstd_ready, m)
                pe.wait_ge(sums_ready, (KC - 1) * m)
                if m == FUSED:
                    pe.wait_ge(sumg_ready, KC - 1)
                last = (KC - 1) % 2
                for total, part in ((True, (SQS, SQGS[:, :] if m == FUSED else None)), (False, (sq[:, last], SQG[:, last, :]))):
                    if not total:
                        pe.wait_ge(sq_ready, KC * (m + 1))
                    if m == FUSED:
                        pe.matmul(A45[:, 0:n], eps_mean, part[0][:, 0:n], start=total, stop=False)
                        if not total:
                            pe.wait_ge(sqg_ready, KC)
                        mm = pe.matmul(A45[:, 0:n], mean, part[1], start=False, stop=not total)
                        if not total:
                            mm.then_inc(statg_mm, 1)
                    for a, w in spans(n):
                        mm = pe.matmul(A67[:, base + a:base + a + w], mean, part[0][:, a:a + w], start=total, stop=not total)
                mm.then_inc(stat_mm, 1)

            pe.wait_ge(small_in, 16 * 5)
            pe.wait_ge(row_ready, 1)
            pe.matmul(A67[:, 0:512], ONES[:, :], CR[0:1, 0:512], start=True, stop=True)
            pe.matmul(A67[:, 512:D], ONES[:, :], CR[0:1, 512:D], start=True, stop=True).then_inc(row_mm, 1)
            pe.matmul(A45[0:NH, 0:512], REL[:, :], OH[:, 0:512], start=True, stop=True)
            pe.matmul(A45[0:NH, 512:BIAS_W], REL[:, :], OH[:, 512:BIAS_W], start=True, stop=True).then_inc(rb_mm, 1)
            pe.wait_ge(meta_sq, 1)
            for k in range(KC):
                mm = pe.matmul(gp[0][:, 512:512 + META], mean, MSQ[:, k, :], start=(k == 0), stop=(k == KC - 1))
            mm.then_inc(meta_mm, 1)
            pe.wait_ge(silu_c, 1)
            first_stats()

            def score(n):
                i, h = 1 + n // NH, n % NH
                if n >= 4:
                    pe.wait_ge(relu_done, n - 3)
                hp = (h % 2) * HD
                pe.matmul((A45, A67)[n % 4 // 2][:, (n % 2) * 512:(n % 2) * 512 + (i + 1) * P],
                          QI[hp:hp + HD, h // 2, i * P:(i + 1) * P], KI[hp:hp + HD, 0:(i + 1) * P],
                          start=True, stop=True).then_inc(score_mm, 1)

            first_pair(0, 0, 0, ((S, META), (S, META)))
            for u in range(2, U_RNN):
                pe.wait_ge(gp_free[u % 2], slot_free(u))
                unit(u, u % 2, gp[u % 2], S, XNhi, XNlo, META, range(KC), last=KC - 1).then_inc(unit_done, 1)
                if u == U_WI + 1:
                    pe.wait_ge(proj_out, U_WI + 1)
                    pe.wait_ge(meta_rstd, 1)
                    for t in range(QT):
                        mm = pe.transpose(gp[0][:, 512 + t * NH:512 + (t + 1) * NH], WIT[0:NH, t * P:(t + 1) * P], ident[0:NH, 0:NH])
                    mm.then_inc(wi_mm, 1)
                    pe.wait_ge(rb_copied, 1)
                if u > U_WI:
                    for n in range(6):
                        score((u - U_WI - 1) * 6 + n)

            pe.wait_ge(relu_done, NH * (QT - 1))
            with pe.Fori(0, KC // 2) as i:
                for b in range(2):
                    def product(c, k0=0, k1=KC):
                        g = b * 3 + c
                        pe.wait_ge(gp_free[g % 2], slot_free(G_RNN, g) + i * 3)
                        mm = unit(U_RNN + i * 6 + g, g % 2, gp[g % 2], S, XNhi, XNlo, META, range(k0, k1), first=k0, last=KC - 1)
                        if k1 == KC:
                            mm.then_inc(unit_done, 1)

                    product(0)
                    product(1)
                    product(2, 0, 1)
                    pe.wait_ge(gate_in, i * 32 + b * 16 + 16)
                    pe.wait_ge(xc_ready, i * 2 + b + 2)
                    pe.wait_ge(ig_ready, i * 4 + b * 2 + 1)
                    for r in range(2):
                        pe.matmul(A45[:, r * 512:(r + 1) * 512], WG[:, r * P:(r + 1) * P], XC[:, :],
                                  start=True, stop=True).then_inc(gate_mm, 1)
                    product(2, 1)

            for c, u in enumerate((U_V, U_K)):
                pe.wait_ge(gp_free[c], slot_free(G_KV))
                unit(u, u % 2, gp[c], S, XNhi, XNlo, META, range(KC), last=KC - 1).then_inc(unit_done, 1)
            pe.wait_ge(proj_out, U_RNN + 1)
            pe.wait_ge(wi_ready, 1)
            for t in range(QT):
                mm = pe.transpose(gp[0][:, 512 + t * P:512 + (t + 1) * P], VV[:, t * P:(t + 1) * P], ident)
            mm.then_inc(v_mm, 1)

            pe.wait_ge(ig_ready, 2 * KC + 1)
            pe.wait_ge(proj_out, U_RNN + 2)
            pe.wait_ge(v_ready, 1)

            def logits(i, g):
                for j in range(4):
                    c = i * NH + g * 4 + j
                    if c >= 2:
                        pe.wait_ge(logit_out, c - 1)
                    pe.matmul(A45[:, (c % 2) * 512:(c % 2) * 512 + (i + 1) * P], Q[g * HD:(g + 1) * HD, j, i * P:(i + 1) * P],
                              K[g * HD:(g + 1) * HD, 0:(i + 1) * P], start=True, stop=True).then_inc(logit_mm, 1)

            def values(i, g):
                pe.wait_ge(p_ready, i * 2 + g + 1)
                if i >= 2 and g == 0:
                    pe.wait_ge(at_done, i - 1)
                t0 = i * (i + 1) + g * (i + 1)
                for kb in range(i + 2):
                    if kb <= i:
                        t = t0 + kb
                        if t >= 2:
                            pe.wait_ge(pt_copied, t - 1)
                        for j in range(4):
                            mm = pe.transpose(A67[:, (t % 2) * 512 + j * P:(t % 2) * 512 + (j + 1) * P],
                                              PR[:, g, j, kb * P:(kb + 1) * P], ident)
                        mm.then_inc(pt_mm, 1)
                    if kb >= 1:
                        t = t0 + kb - 1
                        pe.wait_ge(pt_copied, t + 1)
                        pe.matmul(gp[i % 2][g * HD:(g + 1) * HD, 512:1024], VT[:, kb - 1, g * HD:(g + 1) * HD], PTs[:, t % 2, :],
                                  start=(kb == 1), stop=(kb == i + 1)).then_inc(pv_mm, 1)

            def rout(j):
                pe.wait_ge(gp_free[j % 2], slot_free(G_ROUT, j))
                unit(U_ROUT + j, j % 2, gp[j % 2], S, RNhi, RNlo, 0, range(KC), last=KC - 1).then_inc(unit_done, 1)

            logits(0, 0)
            logits(0, 1)
            for i in range(QT):
                for g in range(2):
                    values(i, g)
                    if i + 1 < QT:
                        logits(i + 1, g)
                    if i == 0 and g == 0:
                        pe.wait_ge(rnn_done, KC + 1)
                    rout(i * 2 + g)

            with pe.Fori(0, 2) as i:
                for pr in range(2):
                    for c in range(2):
                        pe.wait_ge(gp_free[c], slot_free(G_MRG, pr * 4 + c) + i * 4)
                        unit(U_MRG + i * 6 + pr * 3 + c, (pr * 3 + c) % 2, gp[c], S, XNhi, XNlo, META, range(KC),
                             last=KC - 1).then_inc(unit_done, 1)
                    pe.wait_ge(at_done, QT)
                    for q in range(2):
                        pe.wait_ge(gp_free[q], slot_free(G_MRG, pr * 4 + 2 + q) + i * 4)
                        mm = unit(U_MRG + i * 6 + pr * 3 + 2, (pr * 3 + 2) % 2, gp[q], S, AThi, ATlo, 0,
                                  range(4 * q, 4 * q + 4), last=3)
                        mm.then_inc((at_half, unit_done)[q], 1)

            def with_stats(m, product, begin):
                begin(product)
                with pe.Fori(1, KC // 2) as i:
                    product(i, 0)
                    product(i, 1)
                stats(m)

            def plain(u0, g0, hi, lo, c0, n, arrive):
                def product(i, c, k0=0, k1=KC, first=False):
                    pe.wait_ge(gp_free[c], slot_free(g0) + i)
                    mm = unit(u0 + i * 2 + c, c, gp[c], n, hi, lo, c0, range(k0, k1), first=k0, last=KC - 1,
                              arrive=arrive if first else None)
                    if k1 == KC:
                        mm.then_inc(unit_done, 1)

                def begin(product):
                    product(0, 0, 0, KC - 1, first=True)
                    product(0, 1, 0, 3)
                    product(0, 0, KC - 1, KC, first=True)
                    product(0, 1, 3, KC)
                return product, begin

            def down(u0, g0, arrive):
                def product(i, c, first=False):
                    pe.wait_ge(gp_free[c], slot_free(g0) + i)
                    for t in range(3):
                        unit(u0 + i * 6 + c * 3 + t, (c * 3 + t) % 2, gp[c], S, AChi, AClo, 0,
                             range(min(KC, FC - t * KC)), first=t * KC, last=FC - 1,
                             arrive=arrive if first else None).then_inc(unit_done, 1)

                def begin(product):
                    product(0, 0, first=True)
                    product(0, 1)
                return product, begin

            def up(u0, g0, f, halves):
                first_pair(u0, g0, f, halves)
                with pe.Fori(1, FC) as i:
                    for c, (n, c0) in enumerate(halves):
                        pe.wait_ge(gp_free[c], slot_free(g0) + i)
                        unit(u0 + i * 2 + c, c, gp[c], n, XNhi, XNlo, c0, range(KC), last=KC - 1).then_inc(unit_done, 1)

            with_stats(1, *plain(U_OUT, G_OUT, MGhi, MGlo, 0, S, (merge_done, 1)))
            up(U_UP, G_UP, 1, ((S, META), (S, META)))
            with_stats(2, *down(U_DN, G_DN, (act_done, 1)))

            pe.wait_ge(meta_xn, 1)
            pe.wait_ge(con_in, 16)
            with pe.Fori(0, KC // 2) as i:
                for hh in range(2):
                    def gemm(c, k0=0, k1=KC):
                        g = (hh * 9 + c) % 2
                        pe.wait_ge(gp_free[g], slot_free(G_MIX2, hh * 9 + c) + i * 9)
                        u = U_MIX2 + i * 18 + hh * 9 + c
                        mm = unit(u, g, gp[g], T, XNhi, XNlo, 0, range(k0, k1), first=k0, last=KC - 1,
                                  arrive=(xn_ready, 2 * KC) if (hh, c) == (0, 0) else None)
                        if k1 == KC:
                            mm.then_inc(unit_done, 1)

                    def level(l):
                        b = LEVELS[l]
                        pe.wait_ge(lx_ready, i * 18 + hh * 9 + l + 2)
                        if l >= 2:
                            pe.wait_ge(lev_out, i * 16 + hh * 8 + l - 1)
                        for c in range(first_chunk(l), CH):
                            x = XX[:, l % 2, c * P:(c + 1) * P]
                            up = x.rearrange("p (j two b) -> p j two b", two=2, b=b)[:, :, 1, :]
                            mm = pe.matmul(A45[:, (l % 2) * 512 + c * 64:(l % 2) * 512 + (c + 1) * 64], x, up,
                                           start=True, stop=True)
                        mm.then_inc(lev_mm, 1)

                    gemm(0)
                    gemm(1)
                    gemm(2)
                    gemm(3)
                    pe.wait_ge(hvt_ready, i * 2 + hh + 1)
                    pe.wait_ge(on_ready, i * 2 + hh + 1)
                    for c in range(CH):
                        mm = pe.transpose(A67[:, c * P:(c + 1) * P], HVT[:, c * P:(c + 1) * P], ident)
                    mm.then_inc(hv_mm, 1)
                    pe.wait_ge(orstd_ready, i * 2 + hh + 1)
                    level(0)
                    level(1)
                    gemm(4)
                    level(2)
                    level(3)
                    gemm(5)
                    level(4)
                    level(5)
                    gemm(6)
                    level(6)
                    pe.wait_ge(lx_ready, i * 18 + hh * 9 + 8 + 1)
                    pe.wait_ge(hv_ready, i * 2 + hh + 1)
                    for a, w in ((0, 512), (512, TP - 512)):
                        mm = pe.matmul(A67[:, a:a + w], ones, XX[:, 1, a:a + w], start=True, stop=True)
                    mm.then_inc(lev_mm, 1)
                    gemm(7)
                    pe.wait_ge(lx_ready, i * 18 + hh * 9 + 9 + 1)
                    pe.wait_ge(lev_out, i * 16 + hh * 8 + 8)
                    for c in range(CH - 1):
                        mm = pe.transpose(A67[:, c * P:(c + 1) * P], XX[:, 0, c * P:(c + 1) * P], ident)
                    mm.then_inc(kdt_mm, 1)
                    gemm(8, 0, 2)
                    pe.wait_ge(kdt_ready, i * 2 + hh + 1)
                    for c in range(CH - 1):
                        mm = pe.matmul(A45[:, c * P:(c + 1) * P], KDT[:, c, :], HV[:, c, :], start=True, stop=True)
                    mm.then_inc(state_mm, 1)
                    gemm(8, 2, 6)
                    pe.wait_ge(state_ready, i * 2 + hh + 1)
                    pe.wait_ge(qg_ready, i * 2 + hh + 2)
                    for c in range(CH):
                        o = A67[:, c * P:(c + 1) * P]
                        mm = pe.matmul(o, HV[:, c, :], AT2[:, c, :], start=True, stop=(c == 0))
                        if c:
                            mm = pe.matmul(o, ST[:, c - 1, :], QG[:, c * P:(c + 1) * P], start=False, stop=True)
                    mm.then_inc(o_mm, 1)
                    gemm(8, 6)
                    pe.wait_ge(osq_ready, i * 2 + hh + 1)
                    b0 = region(T)
                    for a, w in spans(T):
                        mm = pe.matmul(A45[:, b0 + a:b0 + a + w], head_mean, SQ[:, a:a + w], start=True, stop=True)
                    mm.then_inc(ostat_mm, 1)

            with_stats(3, *plain(U_OUT2, G_OUT2, M2hi, M2lo, META - 2, S + 2, (mix2_done, 1)))
            up(U_UP2, G_UP2, 3, ((S + 2, META - 2), (S, META)))
            with_stats(4, *down(U_DN2, G_DN2, (act2_done, 1)))

        @block.scalar
        def _(act):
            def inverse_root(r, x, eps, done):
                act.activation(r, x, ACT.Ln, bias=eps)
                act.drain()
                act.activation(r, r, ACT.Exp, scale=-0.5).then_inc(done, 1)

            def norm_stats(m):
                q = NORMS[m]
                for k in range(KC):
                    if q["h0"] is not None:
                        act.wait_ge(h_ready, q["h0"] + k + 1)
                    if m == 0 and k >= 2:
                        act.wait_ge(stat_mm, k - 1)
                    if m and k >= 2:
                        act.wait_ge(sums_ready, (KC - 1) * (m - 1) + k - 1)
                    h = H[:, k, q["c0"]:q["c0"] + q["n"]]
                    act.activation(sq[:, k % 2, 0:q["n"]], h, ACT.Square).then_inc(sq_ready, 1)
                    if m == FUSED:
                        if k >= 2:
                            act.wait_ge(sumg_ready, k - 1)
                        act.activation(SQG[:, k % 2, :], h, ACT.Square, scale=vec("g_final", k)).then_inc(sqg_ready, 1)
                b = region(q["n"])
                if m == FUSED:
                    act.wait_ge(statg_mm, 1)
                    inverse_root(RSTD[:, 0:S], A45[:, 0:S], LAM[:, 8, 0:1], rstd_ready)
                    act.wait_ge(stat_mm, KC + m)
                    inverse_root(RST1[:, :], A67[:, 0:S], EPSC, rst1_ready)
                else:
                    act.wait_ge(stat_mm, KC + m)
                    inverse_root(RSTD[:, 0:q["n"]], A67[:, b:b + q["n"]], EPSC, rstd_ready)

            def norm_apply(m):
                q = NORMS[m]
                f, n = q["feeds"], q["n"]
                o0 = q["c0"]
                for k in range(KC):
                    act.wait_ge(nt_ready, KC * f + k + 1)
                    act.activation(XNhi[:, k, o0:o0 + n], nt[:, k % 3, 0:n], ACT.Identity,
                                   bias=scale_bias(m, k)[1]).then_inc(xhi_ready, 1)

            EPSC = LAM[:, 7, 0:1]
            act.wait_ge(row_mm, 1)
            act.activation(CS[:, :], A67[:, 0:D], ACT.Silu).then_inc(silu_c, 1)
            act.wait_ge(rb_mm, 1)
            act.activation(RB[:, :], A45[0:NH, 0:BIAS_W], ACT.Copy).then_inc(rb_copied, 1)
            act.wait_ge(eps_ready, 1)
            act.wait_ge(x_in, 32)
            act.activation(MSQ[:, :, :], H[:, :, 0:META], ACT.Square).then_inc(meta_sq, 1)
            norm_stats(0)
            act.wait_ge(mod_ready, 2)
            norm_apply(0)
            def relu(n):
                i = 1 + n // NH
                act.wait_ge(score_mm, n + 1)
                if n >= 2:
                    act.wait_ge(score_acc, n - 1)
                act.activation(RL[:, n % 2, 0:(i + 1) * P], (A45, A67)[n % 4 // 2][:, (n % 2) * 512:(n % 2) * 512 + (i + 1) * P],
                               ACT.Relu, scale=HD ** -0.5).then_inc(relu_done, 1)

            outs = ([(QI[:, j, :], vec("b_qi", j)) for j in range(4)] + [(KI[:, :], vec("b_ki", 0)), (WIT[:, :], vec("b_wi", 0))]
                    + [(Q[:, j, :], vec("b_q", j)) for j in range(4)])
            for u, (o, b) in enumerate(outs):
                act.wait_ge(unit_done, u + 1 + 2)
                act.activation(o, gp[u % 2][:, 0:S], ACT.Identity, bias=b).then_inc(gp_free[u % 2], 1)
                act.drain().then_inc(proj_out, 1)
                if u == 3:
                    act.wait_ge(meta_mm, 1)
                    inverse_root(MRS[:, :], gp[0][:, 512:512 + META], EPSC, meta_rstd)
                    act.wait_ge(lam_neg, 1)
                    act.activation(LAM[:, 1, :], LAM[:, 0, :], ACT.Exp).then_inc(lam_exp, 1)
                    act.wait_ge(lb_max, 2)
                    act.activation(LAM[:, 5, :], LAM[:, 3, :], ACT.Exp).then_inc(lb_exp, 1)
                    act.activation(LAM[:, 6, :], LAM[:, 4, :], ACT.Exp).then_inc(lb_exp, 1)
                if u > U_WI:
                    for n in range(6):
                        relu((u - U_WI - 1) * 6 + n)

            act.wait_ge(xr_pad, 1)
            act.wait_ge(lam_done, 1)
            act.wait_ge(score_acc, NH * (QT - 1))
            with act.Fori(0, KC // 2) as i:
                for b in range(2):
                    blk = i * 2 + b

                    def rv(c):
                        return V[:, bass.ds(VEC["rnn"] + i * 32 + b * 16 + c, 1)]

                    def psum(c):
                        g = b * 3 + c
                        act.wait_ge(unit_done, U_RNN + i * 6 + g + 1 + 2)
                        return gp[g % 2][:, 0:S], gp_free[g % 2]

                    act.wait_ge(gate_mm, i * 4 + b * 2 + 1)
                    act.dma_start(WG[:, :], gatew[bass.ds(blk, 1), :, :]).then_inc(gate_in, 16)
                    ps, free = psum(0)
                    act.wait_ge(xc_ready, blk + 1)
                    act.activation(XR[:, 3:3 + S], ps, ACT.Identity, bias=rv(0)).then_inc(free, 1)
                    act.drain()
                    act.wait_ge(u1_done, blk + 1)
                    act.activation(XC[:, :], XR[:, 3:3 + S], ACT.Identity, bias=rv(6), scale=rv(5)).then_inc(conv_first, 1)
                    ps, free = psum(1)
                    act.wait_ge(rnn_done, blk + 1)
                    act.activation(GY[:, :], ps, ACT.Gelu_apprx_tanh, bias=rv(1)).then_inc(free, 1)
                    act.drain().then_inc(gelu_ready, 1)
                    act.wait_ge(gate_mm, i * 4 + b * 2 + 3)
                    act.activation(RG[:, :], A45[:, 0:512], ACT.Sigmoid, bias=rv(7)).then_inc(ig_ready, 1)
                    act.activation(IG[:, :], A45[:, 512:1024], ACT.Sigmoid, bias=rv(8)).then_inc(ig_ready, 1)
                    act.drain()
                    act.activation(DA[:, :], RG[:, :], ACT.Exp, scale=LAM[:, 2, bass.ds(blk, 1)])
                    act.activation(TH[:, :], RG[:, :], ACT.Tanh, scale=LAM[:, 0, bass.ds(blk, 1)])
                    act.drain()
                    act.activation(A2[:, :], DA[:, :], ACT.Square).then_inc(a_ready, 1)
                    ps, free = psum(2)
                    act.activation(RG8[:, bass.ds(blk, 1), :].rearrange("p a n -> p (a n)"), ps, ACT.Sigmoid,
                                   bias=V[:, bass.ds(VEC["b_gates"] + i * 4 + b * 2 + 1, 1)]).then_inc(free, 1)
                    act.drain().then_inc(rgate_ready, 1)
                    act.wait_ge(m2_ready, blk + 1)
                    act.activation(MU[:, :], M2[:, :], ACT.Sqrt).then_inc(mult_ready, 1)

            for c, (o, b) in enumerate(((VV, "b_v"), (K[:, :], "b_k"))):
                act.wait_ge(unit_done, U_V + c + 1 + 2)
                act.activation(o, gp[c][:, 0:S], ACT.Identity, bias=vec(b, 0)).then_inc(gp_free[c], 1)
                act.drain().then_inc(proj_out, 1)
            act.wait_ge(v_mm, 1)
            act.activation(VT[:, :, :].rearrange("p t v -> p (t v)"), gp[0][:, 512:1024], ACT.Copy).then_inc(v_ready, 1)

            def exps(i, g):
                act.wait_ge(nmx_ready, i * 2 + g + 1)
                for j in range(4):
                    p = PR[:, g, j, 0:(i + 1) * P]
                    act.activation(p, p, ACT.Exp, bias=nmx[:, g, j:j + 1], accum_out=rs[:, g, j:j + 1]).then_inc(exp_done, 1)

            exps(0, 0)
            exps(0, 1)
            for i in range(QT):
                for g in range(2):
                    t0 = i * (i + 1) + g * (i + 1)
                    for t in range(t0, t0 + i + 1):
                        act.wait_ge(pt_mm, t + 1)
                        if t >= 2:
                            act.wait_ge(pv_mm, t - 1)
                        act.activation(PTs[:, t % 2, :], A67[:, (t % 2) * 512:(t % 2 + 1) * 512], ACT.Copy).then_inc(pt_copied, 1)
                    if g == 1:
                        act.wait_ge(pv_mm, (i + 1) * (i + 2))
                        act.activation(AThi[:, :, i * P:(i + 1) * P], gp[i % 2][:, 512:1024].rearrange("p (j q) -> p j q", j=4),
                                       ACT.Copy).then_inc(at_hi, 1)
                    if i + 1 < QT:
                        exps(i + 1, g)

            act.wait_ge(at_done, QT)
            with act.Fori(0, 2) as i:
                for pr in range(2):
                    for c in range(2):
                        act.wait_ge(unit_done, U_MRG + i * 6 + pr * 3 + c + 1 + 2)
                        act.wait_ge(merge_done, i * 4 + pr * 2 + 1)
                        act.activation(SG[:, c, :], gp[c][:, 0:S], ACT.Sigmoid,
                                       bias=V[:, bass.ds(VEC["b_gates"] + i * 8 + pr * 4 + c * 2, 1)]).then_inc(gp_free[c], 1)
                        act.drain().then_inc(sg_ready, 1)

            norm_stats(1)
            norm_apply(1)
            with act.Fori(0, FC) as i:
                def fv(c):
                    return V[:, bass.ds(VEC["ffn"] + i * 8 + c, 1)]
                act.wait_ge(unit_done, U_UP + i * 2 + 1 + 2)
                act.wait_ge(act_done, i + 1)
                act.activation(YV[:, :], gp[0][:, 0:S], ACT.Identity, bias=fv(3), scale=fv(2)).then_inc(yv_first, 1)
                act.wait_ge(unit_done, U_UP + i * 2 + 2 + 2)
                act.activation(YG[:, :], gp[1][:, 0:S], ACT.Identity, bias=fv(7), scale=fv(6)).then_inc(yg_first, 1)
                act.wait_ge(yg_ready, i + 1)
                act.activation(SL[:, :], YG[:, :], ACT.Silu).then_inc(silu_ready, 1)
            norm_stats(2)

            norm_apply(2)
            act.wait_ge(pads2, 1)
            act.wait_ge(lb_done, 1)
            with act.Fori(0, KC // 2) as i:
                for hh in range(2):
                    h = i * 2 + hh
                    b0 = region(T)

                    def psum(c):
                        g = (hh * 9 + c) % 2
                        act.wait_ge(unit_done, U_MIX2 + i * 18 + hh * 9 + c + 1 + 2)
                        return gp[g][:, b0:b0 + T], gp_free[g]

                    def decay(l, b):
                        act.wait_ge(d_ready, i * 16 + hh * 8 + l + 1)
                        n = i * 18 + hh * 9 + l
                        act.wait_ge(lx_ready, (n - 1 if l >= 2 else i * 18 + hh * 9) + 1)
                        dv, ev = [x[:, l % 2, :].rearrange("p (j two b) -> p j two b", two=2, b=b) for x in (DD, EE)]
                        act.activation(ev[:, :, 1, :], dv[:, :, 1, :], ACT.Exp)
                        act.activation(ev[:, :, 0, :], dv[:, :, 0, :], ACT.Exp, scale=-1.0).then_inc(e_ready, 1)

                    ps, free = psum(0)
                    act.wait_ge(f_ready, i * 4 + hh * 2 + 1)
                    act.activation(HF[:, PAD:TP], ps, ACT.Sigmoid).then_inc(free, 1)
                    act.drain().then_inc(sf_ready, 1)
                    act.activation(HL[:, PAD:TP], HF[:, PAD:TP], ACT.Ln, bias=LAM[:, 5, bass.ds(h, 1)],
                                   scale=LAM[:, 6, bass.ds(h, 1)]).then_inc(lf_ready, 1)
                    ps, free = psum(1)
                    act.wait_ge(qg_ready, h + 1)
                    act.activation(HQ[:, PAD:TP], ps, ACT.Silu).then_inc(free, 1)
                    act.drain().then_inc(hq_ready, 1)
                    ps, free = psum(2)
                    act.wait_ge(hv_mm, h + 1)
                    act.activation(HVT[:, PAD:TP], ps, ACT.Copy).then_inc(free, 1)
                    act.drain().then_inc(hvt_ready, 1)
                    decay(0, LEVELS[0])
                    decay(1, LEVELS[1])
                    ps, free = psum(3)
                    act.wait_ge(mix2_done, h + 1)
                    act.activation(CG[:, :], ps, ACT.Copy).then_inc(free, 1)
                    act.drain().then_inc(cg_ready, 1)
                    act.wait_ge(hv_mm, h + 2)
                    act.wait_ge(o_mm, h + 1)
                    act.activation(HV[:, :, :].rearrange("p c v -> p (c v)"), A67[:, 0:TP], ACT.Copy).then_inc(hv_ready, 1)
                    decay(2, LEVELS[2])
                    decay(3, LEVELS[3])
                    decay(4, LEVELS[4])
                    act.wait_ge(cx_ready, h + 1)
                    act.activation(YB[:, :], CX[:, 2:2 + T], ACT.Copy, scale=V[:, bass.ds(VEC["conv2"] + h * 4 + 2, 1)]).then_inc(yb_first, 1)
                    decay(5, LEVELS[5])
                    ps, free = psum(5)
                    act.activation(BG[:, :], ps, ACT.Copy).then_inc(free, 1)
                    act.drain().then_inc(side_ready, 1)
                    decay(6, LEVELS[6])
                    act.activation(EG[:, P:TP], HG[:, P:TP], ACT.Exp).then_inc(eg_ready, 1)
                    act.wait_ge(d_ready, i * 16 + hh * 8 + 8)
                    act.wait_ge(lx_ready, i * 18 + hh * 9 + 8 + 1)
                    act.activation(EE[:, 1, 0:TP - P], DD[:, 1, 0:TP - P], ACT.Exp, scale=-1.0).then_inc(e_ready, 1)
                    ps, free = psum(6)
                    act.activation(SO[:, :], ps, ACT.Silu).then_inc(free, 1)
                    act.drain().then_inc(side_ready, 1)
                    act.wait_ge(kdt_mm, h + 1)
                    act.activation(KDT[:, :, :].rearrange("p c d -> p (c d)"), A67[:, 0:TP - P], ACT.Copy).then_inc(kdt_ready, 1)
                    for c, t in ((7, SA), (8, SB2)):
                        if c == 8:
                            act.wait_ge(o_mm, h + 2)
                            act.activation(SQ[:, :], A67[:, PAD:TP], ACT.Square).then_inc(osq_ready, 1)
                        ps, free = psum(c)
                        act.activation(t[:, :], ps, ACT.Sigmoid).then_inc(free, 1)
                        act.drain().then_inc(side_ready, 1)
                    act.wait_ge(ostat_mm, h + 1)
                    act.activation(HRS[:, :], A45[:, b0:b0 + T], ACT.Ln, bias=EPSC)
                    act.drain()
                    act.activation(HRS[:, :], HRS[:, :], ACT.Exp, scale=-0.5).then_inc(orstd_ready, 1)

            norm_stats(3)
            norm_apply(3)
            with act.Fori(0, FC) as i:
                def fw(c):
                    return V[:, bass.ds(VEC["ffn2"] + i * 4 + c, 1)]
                b0 = region(S + 2)
                act.wait_ge(unit_done, U_UP2 + i * 2 + 1 + 2)
                act.wait_ge(act2_done, i + 1)
                act.activation(YV[:, :], gp[0][:, b0 + 2:b0 + 2 + S], ACT.Identity, bias=fw(3), scale=fw(2)).then_inc(ya_first, 1)
                act.wait_ge(ya_ready, i + 1)
                act.activation(SL[:, :], YV[:, :], ACT.Silu).then_inc(silu2_ready, 1)
            norm_stats(4)

        @block.vector
        def _(dve):
            def norm_split(m):
                q = NORMS[m]
                f, n, c0 = q["feeds"], q["n"], q["c0"]
                dve.wait_ge(rstd_ready, m + 1)

                def scaled(k):
                    dve.scalar_tensor_tensor(nt[:, k % 3, 0:n], H[:, k, c0:c0 + n], scale_bias(m, k)[0], RSTD[:, 0:n], ALU.mult,
                                             ALU.mult).then_inc(nt_ready, 1)

                scaled(0)
                scaled(1)
                for k in range(KC):
                    if k + 2 < KC:
                        if k:
                            dve.drain()
                        scaled(k + 2)
                    dve.wait_ge(xhi_ready, KC * f + k + 1)
                    dve.scalar_tensor_tensor(XNlo[:, k, c0:c0 + n], nt[:, k % 3, 0:n], scale_bias(m, k)[1],
                                             XNhi[:, k, c0:c0 + n].bitcast(F32), ALU.add, ALU.subtract).then_inc(xn_ready, 1)

            def norm_final(g, r):
                for k in range(KC):
                    ins = dve.scalar_tensor_tensor(H[:, k, META:T], H[:, k, META:T], vec(g, k), r, ALU.mult, ALU.mult)
                    if g == "final2":
                        ins.then_inc(out_ready, 1)

            def residual(m, u0, per, gate):
                c0, n = NORMS[m]["c0"], NORMS[m]["n"]
                b = region(n)
                dve.memset(SQS[:, 0:n], 0.0)
                if m == FUSED:
                    dve.memset(SQGS[:, :], 0.0)

                def chunk(i, c):
                    dve.wait_ge(unit_done, u0 + i * (2 * per) + (c + 1) * per + 2)
                    hk = H[:, bass.ds(i * 2 + c, 1), c0:c0 + n].rearrange("p a n -> p (a n)")
                    src = gp[c][:, b:b + n]
                    if gate is None:
                        dve.tensor_tensor(hk, src, hk, ALU.add).then_inc(h_ready, 1)
                    else:
                        dve.scalar_tensor_tensor(hk, src, MOD[:, bass.ds(gate + i * 2 + c, 1)], hk, ALU.mult,
                                                 ALU.add).then_inc(h_ready, 1)
                    dve.drain().then_inc(gp_free[c], 1)

                def add(i, c):
                    dve.wait_ge(sq_ready, KC * m + i * 2 + c)
                    dve.tensor_tensor(SQS[:, 0:n], SQS[:, 0:n], sq[:, 1 - c, 0:n], ALU.add).then_inc(sums_ready, 1)
                    if m == FUSED:
                        dve.wait_ge(sqg_ready, i * 2 + c)
                        dve.tensor_tensor(SQGS[:, :], SQGS[:, :], SQG[:, 1 - c, :], ALU.add).then_inc(sumg_ready, 1)
                    dve.drain()

                chunk(0, 0)
                add(0, 1)
                chunk(0, 1)
                with dve.Fori(1, KC // 2) as i:
                    for c in range(2):
                        add(i, c)
                        chunk(i, c)

            dve.memset(ONES[:, :], 1.0).then_inc(row_ready, 1)
            dve.memset(LAM[:, 8, :], EPS * EPS)
            dve.memset(LAM[:, 7, :], EPS)
            dve.drain().then_inc(eps_ready, 1)
            dve.memset(probe[0:1, 27:28], 0.0).then_inc(unit_done, 2)
            dve.memset(probe[0:1, 24:25], 0.0).then_inc(gp_free[0], 1)
            dve.memset(probe[0:1, 25:26], 0.0).then_inc(gp_free[1], 1)
            dve.memset(probe[0:1, 26:27], 0.0).then_inc(ada_done, ADA_SLOTS)
            for j, s in enumerate(one_ahead):
                dve.memset(probe[0:1, 4 + j:5 + j], 0.0).then_inc(s, 1)
            dve.drain()
            dve.wait_ge(small_in, 16 * 5)
            def modulation(first, last):
                for c in range(first, last):
                    w = AW[c % ADA_SLOTS]
                    dve.wait_ge(ada_in[c % ADA_SLOTS], 16 * (c // ADA_SLOTS + 1))
                    dve.tensor_tensor_reduce(w[:, :], w[:, :], CS[:, :], 1.0, 0.0, ALU.mult, ALU.add,
                                             MOD[:, c:c + 1]).then_inc(ada_done, 1)

            dve.wait_ge(silu_c, 1)
            modulation(0, ADA_FIRST)
            dve.drain()
            dve.tensor_tensor(MOD[:, 0:ADA_FIRST], MOD[:, 0:ADA_FIRST], vec("b_ada", 0, ADA_FIRST), ALU.add).then_inc(mod_ready, 1)
            dve.drain()
            dve.scalar_tensor_tensor(AB1[:, :], MOD[:, KC:2 * KC], 1.0, vec("g_mix", 0, KC), ALU.add, ALU.mult).then_inc(mod_ready, 1)
            dve.drain()
            norm_split(0)

            modulation(ADA_FIRST, ADA_FIRST + ADA_SECOND // 2)
            lam, l0, l1 = vec("lam", 0, KC), vec("lb0", 0, KC), vec("lb1", 0, KC)
            dve.scalar_tensor_tensor(LAM[:, 0, :], lam, -1.0, lam, ALU.mult, ALU.min).then_inc(lam_neg, 1)
            dve.tensor_tensor(LAM[:, 2, :], l0, l1, ALU.max)
            dve.drain()
            dve.tensor_tensor(LAM[:, 3, :], l0, LAM[:, 2, :], ALU.subtract).then_inc(lb_max, 1)
            dve.tensor_tensor(LAM[:, 4, :], l1, LAM[:, 2, :], ALU.subtract).then_inc(lb_max, 1)
            dve.wait_ge(lb_exp, 2)
            dve.tensor_tensor(LAM[:, 6, :], LAM[:, 5, :], LAM[:, 6, :], ALU.add)
            dve.drain()
            dve.reciprocal(LAM[:, 6, :], LAM[:, 6, :])
            dve.drain()
            dve.tensor_tensor(LAM[:, 5, :], LAM[:, 5, :], LAM[:, 6, :], ALU.mult)
            dve.drain()
            dve.tensor_scalar(LAM[:, 6, :], LAM[:, 5, :], -1.0, 1.0, ALU.mult, ALU.add).then_inc(lb_done, 1)
            dve.wait_ge(lam_exp, 1)
            u, z, z2, pl = LAM[:, 1, :], LAM[:, 2, :], LAM[:, 3, :], LAM[:, 4, :]
            dve.tensor_scalar(z, u, 2.0, None, ALU.add)
            dve.drain()
            dve.reciprocal(z, z)
            dve.drain()
            dve.tensor_tensor(z, z, u, ALU.mult)
            dve.drain()
            dve.tensor_tensor(z2, z, z, ALU.mult)
            dve.drain()
            dve.tensor_scalar(pl, z2, 1.0 / 17, 1.0 / 15, ALU.mult, ALU.add)
            dve.drain()
            for odd in (13, 11, 9, 7, 5, 3, 1):
                dve.tensor_tensor(pl, pl, z2, ALU.mult)
                dve.drain()
                dve.tensor_scalar(pl, pl, 1.0 / odd, None, ALU.add)
                dve.drain()
            dve.tensor_tensor(pl, pl, z, ALU.mult)
            dve.tensor_scalar(LAM[:, 1, :], lam, -1.0, 0.0, ALU.mult, ALU.max)
            dve.drain()
            dve.scalar_tensor_tensor(pl, pl, 2.0, LAM[:, 1, :], ALU.mult, ALU.add)
            dve.drain()
            dve.tensor_scalar(LAM[:, 2, :], pl, -8.0, None, ALU.mult)
            dve.tensor_scalar(LAM[:, 0, :], pl, 8.0, None, ALU.mult)
            dve.drain().then_inc(lam_done, 1)

            modulation(ADA_FIRST + ADA_SECOND // 2, ADA_FIRST + ADA_SECOND)
            dve.tensor_tensor(GW[:, :], vec("g_final", 0, KC), vec("attn_norm", 0, KC), ALU.mult)
            dve.wait_ge(meta_rstd, 1)
            for k in range(KC):
                dve.scalar_tensor_tensor(MSQ[:, k, :], H[:, k, 0:META], vec("attn_norm", k), MRS[:, :], ALU.mult, ALU.mult)
            dve.drain()
            dve.tensor_copy(XNhi[:, :, 0:META], MSQ[:, :, :])
            dve.drain()
            dve.tensor_tensor(XNlo[:, :, 0:META], MSQ[:, :, :], XNhi[:, :, 0:META].bitcast(F32), ALU.subtract).then_inc(meta_xn, 1)

            dve.wait_ge(con_in, 16)
            dve.wait_ge(wi_mm, 1)
            dve.tensor_scalar(WI[:, :, :].rearrange("p t h -> p (t h)"), gp[0][:, 512:512 + QT * NH], NH ** -0.5, None,
                              ALU.mult).then_inc(wi_ready, 1)
            dve.drain()
            for n in range(NH * (QT - 1)):
                i, h = 1 + n // NH, n % NH
                w = (i + 1) * P
                dve.wait_ge(relu_done, n + 1)
                if h == 0:
                    dve.tensor_scalar(SC[i][:, :], RL[:, n % 2, 0:w], WI[:, i, h:h + 1], None, ALU.mult).then_inc(score_acc, 1)
                else:
                    dve.drain()
                    dve.scalar_tensor_tensor(SC[i][:, :], RL[:, n % 2, 0:w], WI[:, i, h:h + 1], SC[i][:, :], ALU.mult,
                                             ALU.add).then_inc(score_acc, 1)
                if h == NH - 1:
                    dve.drain()
                    dve.tensor_tensor(SC[i][:, i * P:w], SC[i][:, i * P:w], tri, ALU.add)
                    dve.drain()

            def take(tiles):
                for i in tiles:
                    dve.max(m8[:, i, :], SC[i][:, :])
                dve.drain()
                for i in tiles:
                    dve.match_replace(SC[i][:, :], m8[:, i, :], SC[i][:, :], TAKEN)
                dve.drain()

            dve.wait_ge(bias_saved, 16)
            dve.memset(XR[:, 0:3], 0.0).then_inc(xr_pad, 1)
            assert KC * 2 * 8 == TOPK
            with dve.Fori(0, KC // 2) as i:
                for b in range(2):
                    blk = i * 2 + b

                    def rv(c):
                        return V[:, bass.ds(VEC["rnn"] + i * 32 + b * 16 + c, 1)]
                    dve.wait_ge(conv_first, blk + 1)
                    for tap in (2, 1, 0):
                        ins = dve.scalar_tensor_tensor(XC[:, :], XR[:, tap:tap + S], rv(2 + tap), XC[:, :], ALU.mult, ALU.add)
                        if tap:
                            dve.drain()
                    ins.then_inc(xc_ready, 1)
                    take((1, 2, 3))
                    dve.wait_ge(ig_ready, i * 4 + b * 2 + 3)
                    dve.tensor_tensor(U1[:, :], XC[:, :], IG[:, :], ALU.mult).then_inc(u1_done, 1)
                    dve.wait_ge(a_ready, blk + 1)
                    dve.scalar_tensor_tensor(M2[:, :], A2[:, :], 1.0, TH[:, :], ALU.add, ALU.mult).then_inc(m2_ready, 1)
                    take((1, 2, 3))
                    dve.wait_ge(mult_ready, blk + 1)
                    dve.tensor_tensor(UU[:, :], U1[:, :], MU[:, :], ALU.mult)
                    dve.drain()
                    dve.tensor_tensor_scan(HS[:, :], DA[:, :], UU[:, :], 0.0, ALU.mult, ALU.add)
                    dve.drain()
                    dve.wait_ge(gelu_ready, blk + 1)
                    dve.tensor_tensor(RF[:, :], HS[:, :], GY[:, :], ALU.mult)
                    dve.drain()
                    rhi, rlo = [x[:, bass.ds(blk, 1), :].rearrange("p a n -> p (a n)") for x in (RNhi, RNlo)]
                    dve.tensor_copy(rhi, RF[:, :])
                    dve.drain()
                    dve.tensor_tensor(rlo, RF[:, :], rhi.bitcast(F32), ALU.subtract).then_inc(rnn_done, 1)
            for i in range(1, QT):
                dve.tensor_scalar(NEG[i][:, :], SC[i][:, :], TAKEN, MASKED, ALU.not_equal, ALU.mult)
            dve.drain()
            dve.wait_ge(bias_in, 16)
            dve.wait_ge(rgate_ready, KC)

            def logits(i, g):
                w = (i + 1) * P
                if i >= 1:
                    dve.wait_ge(pt_mm, (i - 1) * i + (g + 1) * i)
                for j in range(4):
                    c = i * NH + g * 4 + j
                    pr = PR[:, g, j, 0:w]
                    dve.wait_ge(logit_mm, c + 1)
                    dve.scalar_tensor_tensor(pr, A45[:, (c % 2) * 512:(c % 2) * 512 + w], HD ** -0.5,
                                             BIAS[:, g * 4 + j, S - w:S], ALU.mult, ALU.add).then_inc(logit_out, 1)
                    dve.drain()
                    dve.tensor_tensor_reduce(pr, pr, NEG[i][:, 0:w], 1.0, MASKED, ALU.add, ALU.max, mx[:, g, j:j + 1])
                dve.drain()
                dve.tensor_scalar(nmx[:, g, :], mx[:, g, :], -1.0, None, ALU.mult).then_inc(nmx_ready, 1)

            def gated(j):
                dve.wait_ge(unit_done, U_ROUT + j + 1 + 2)
                dve.tensor_tensor(RG8[:, j, :], gp[j % 2][:, 0:S], RG8[:, j, :], ALU.mult).then_inc(gp_free[j % 2], 1)

            logits(0, 0)
            logits(0, 1)
            for i in range(QT):
                for g in range(2):
                    dve.wait_ge(exp_done, NH * i + 4 * (g + 1))
                    dve.reciprocal(rr[:, g, :], rs[:, g, :])
                    dve.drain()
                    for j in range(4):
                        pr = PR[:, g, j, 0:(i + 1) * P]
                        dve.tensor_scalar(pr, pr, rr[:, g, j:j + 1], None, ALU.mult)
                    dve.drain().then_inc(p_ready, 1)
                    if i or g:
                        gated(i * 2 + g - 1)
                    if i + 1 < QT:
                        logits(i + 1, g)
                dve.wait_ge(at_hi, i + 1)
                dve.tensor_tensor(ATlo[:, :, i * P:(i + 1) * P], gp[i % 2][:, 512:1024].rearrange("p (j q) -> p j q", j=4),
                                  AThi[:, :, i * P:(i + 1) * P].bitcast(F32), ALU.subtract).then_inc(at_done, 1)

            gated(KC - 1)

            dve.drain()
            with dve.Fori(0, 2) as i:
                for pr in range(2):
                    def two_chunks(n):
                        for c in range(n, n + 2):
                            dve.wait_ge(ada3_in[c % 2], i * 64 + pr * 32 + c // 2 * 16 + 16)
                            dve.memset(probe[0:1, 28 + c:29 + c], 0.0)
                            w = AWM[c % 2][:, :]
                            dve.tensor_tensor_reduce(w, w, CS[:, :], 1.0, 0.0, ALU.mult, ALU.add, MOD4[:, c:c + 1]).then_inc(ada_done, 1)

                    two_chunks(0)
                    dve.wait_ge(sg_ready, i * 4 + pr * 2 + 2)
                    for q in range(2):
                        dve.wait_ge(*((at_half, i * 2 + pr + 1), (unit_done, U_MRG + i * 6 + pr * 3 + 3 + 2))[q])
                        rg, mhi, mlo = [x[:, bass.ds(i * 4 + pr * 2 + q, 1), :].rearrange("p a n -> p (a n)") for x in (RG8, MGhi, MGlo)]
                        dve.tensor_tensor(MB[:, :], gp[q][:, 0:S], SG[:, q, :], ALU.mult).then_inc(gp_free[q], 1)
                        dve.drain()
                        dve.tensor_tensor(MF[:, :], MB[:, :], rg, ALU.add)
                        dve.drain()
                        dve.tensor_copy(mhi, MF[:, :])
                        dve.drain()
                        dve.tensor_tensor(mlo, MF[:, :], mhi.bitcast(F32), ALU.subtract).then_inc(merge_done, 1)
                        dve.drain()
                    two_chunks(2)
                    dve.drain()
                    dve.tensor_copy(MOD[:, bass.ds(ADA_FIRST + ADA_SECOND + i * 8 + pr * 4, 4)], MOD4[:, :])
                    dve.drain()
            dve.tensor_tensor(MOD[:, ADA_FIRST:], MOD[:, ADA_FIRST:], vec("b_ada", ADA_FIRST, 4 * KC), ALU.add)
            dve.drain()
            dve.scalar_tensor_tensor(AB2[:, :], MOD[:, 4 * KC:5 * KC], 1.0, vec("g_ffn", 0, KC), ALU.add, ALU.mult)
            dve.drain()
            residual(1, U_OUT, 1, 2 * KC)
            norm_split(1)

            def split_act(i, done):
                ahi, alo = [x[:, bass.ds(i, 1), :].rearrange("p a n -> p (a n)") for x in (AChi, AClo)]
                dve.drain()
                dve.tensor_copy(ahi, AF[:, :])
                dve.drain()
                dve.tensor_tensor(alo, AF[:, :], ahi.bitcast(F32), ALU.subtract).then_inc(done, 1)
                dve.drain()

            dve.drain()
            with dve.Fori(0, FC) as i:
                def fv(c):
                    return V[:, bass.ds(VEC["ffn"] + i * 8 + c, 1)]
                for c, (y, first) in enumerate(((YV, yv_first), (YG, yg_first))):
                    dve.wait_ge(first, i + 1)
                    dve.scalar_tensor_tensor(y[:, 1:S], gp[c][:, 0:S - 1], fv(4 * c + 1), y[:, 1:S], ALU.mult, ALU.add)
                    dve.drain()
                    dve.scalar_tensor_tensor(y[:, 2:S], gp[c][:, 0:S - 2], fv(4 * c), y[:, 2:S], ALU.mult,
                                             ALU.add).then_inc(gp_free[c], 1)
                dve.drain().then_inc(yg_ready, 1)
                dve.wait_ge(silu_ready, i + 1)
                dve.tensor_tensor(AF[:, :], SL[:, :], YV[:, :], ALU.mult)
                split_act(i, act_done)
            residual(2, U_DN, 3, 5 * KC)

            norm_split(2)
            dve.drain()
            dve.wait_ge(rst1_ready, 1)
            norm_final("g_final", RST1[:, :])
            dve.drain()
            for t in (HQ, HK, HL, HVT):
                dve.memset(t[:, 0:PAD], 0.0)
            dve.memset(AT2[:, :, :], 0.0)
            dve.memset(CX[:, 0:2], 0.0)
            dve.drain().then_inc(pads2, 1)
            with dve.Fori(0, KC // 2) as i:
                for hh in range(2):
                    h = i * 2 + hh
                    b0 = region(T)
                    dve.wait_ge(sf_ready, h + 1)
                    dve.tensor_scalar(HK[:, PAD:TP], HF[:, PAD:TP], LAM[:, 6, bass.ds(h, 1)], LAM[:, 5, bass.ds(h, 1)],
                                      ALU.mult, ALU.add).then_inc(f_ready, 1)
                    dve.drain()
                    dve.tensor_scalar(HK[:, PAD:TP], HK[:, PAD:TP], -1.0, 1.0, ALU.mult, ALU.add)
                    dve.wait_ge(lf_ready, h + 1)
                    dve.tensor_tensor_scan(HG[:, :], CON[:, C_RST:C_RST + TP], HL[:, :], 0.0, ALU.mult, ALU.add).then_inc(f_ready, 1)
                    dve.drain()

                    def boundary(l):
                        b = LEVELS[l]
                        g = HG[:, :].rearrange("p (j t) -> p j t", t=2 * b)
                        dve.tensor_tensor(DD[:, l % 2, :].rearrange("p (j t) -> p j t", t=2 * b), g,
                                          g[:, :, b - 1:b].to_broadcast([P, TP // (2 * b), 2 * b]), ALU.subtract).then_inc(d_ready, 1)

                    def weigh(l):
                        b = LEVELS[l]
                        dve.wait_ge(e_ready, i * 16 + hh * 8 + l + 1)
                        x, e, q, k = [t.rearrange("p (j two b) -> p j two b", two=2, b=b)
                                      for t in (XX[:, l % 2, :], EE[:, l % 2, :], HQ[:, :], HK[:, :])]
                        dve.tensor_tensor(x[:, :, 1, :], q[:, :, 1, :], e[:, :, 1, :], ALU.mult)
                        dve.tensor_tensor(x[:, :, 0, :], k[:, :, 0, :], e[:, :, 0, :], ALU.mult)
                        dve.drain().then_inc(lx_ready, 1)

                    def place(l):
                        b = LEVELS[l]
                        dve.wait_ge(lev_mm, i * 16 + hh * 8 + l + 1)
                        dve.memset(probe[0:1, 1:2], 0.0)
                        m = CON[:, C_LEV + 64 * l:C_LEV + 64 * (l + 1)].bitcast(U32)
                        c0 = first_chunk(l)
                        dve.copy_predicated(
                            AT2[:, c0:, :].rearrange("p c (j two b) -> p c j two b", two=2, b=b)[:, :, :, 1, :],
                            m.rearrange("p (o j b) -> p o j b", o=1, b=b).to_broadcast([P, CH - c0, 64 // b, b]),
                            A45[:, (l % 2) * 512 + c0 * 64:(l % 2) * 512 + CH * 64].rearrange("p (c j b) -> p c j b", c=CH - c0, b=b)
                        ).then_inc(lev_out, 1)

                    dve.wait_ge(hq_ready, h + 1)
                    dve.wait_ge(o_mm, h + 1)
                    boundary(0)
                    boundary(1)
                    for l in range(len(LEVELS)):
                        weigh(l)
                        if l + 2 < len(LEVELS):
                            boundary(l + 2)
                        if l >= 1:
                            place(l - 1)
                        if l == 3:
                            dve.wait_ge(cg_ready, h + 1)
                            dve.wait_ge(unit_done, U_MIX2 + i * 18 + hh * 9 + 4 + 1 + 2)
                            g = (hh * 9 + 4) % 2
                            dve.tensor_tensor(CX[:, 2:2 + T], gp[g][:, b0:b0 + T], CG[:, :], ALU.mult).then_inc(cx_ready, 1)
                            dve.drain().then_inc(gp_free[g], 1)
                    dve.tensor_tensor(XX[:, 1, :], HQ[:, :], HK[:, :], ALU.mult)
                    dve.drain().then_inc(lx_ready, 1)
                    g = HG[:, 0:TP - P].rearrange("p (c t) -> p c t", t=P)
                    dve.tensor_tensor(DD[:, 1, 0:TP - P].rearrange("p (c t) -> p c t", t=P), g,
                                      g[:, :, P - 1:P].to_broadcast([P, CH - 1, P]), ALU.subtract).then_inc(d_ready, 1)
                    place(len(LEVELS) - 1)
                    dve.drain()
                    dve.wait_ge(lev_mm, i * 16 + hh * 8 + 8)
                    dve.memset(probe[0:1, 2:3], 0.0)
                    dve.copy_predicated(AT2[:, :, :], ident.bitcast(U32).rearrange("p (o t) -> p o t", o=1).to_broadcast([P, CH, P]),
                                        A67[:, 0:TP].rearrange("p (c t) -> p c t", c=CH)).then_inc(lev_out, 1)
                    dve.wait_ge(e_ready, i * 16 + hh * 8 + 8)
                    dve.tensor_tensor(XX[:, 0, 0:TP - P], HK[:, 0:TP - P], EE[:, 1, 0:TP - P], ALU.mult)
                    dve.drain().then_inc(lx_ready, 1)
                    dve.wait_ge(eg_ready, h + 1)
                    dve.tensor_tensor(QG[:, P:TP], HQ[:, P:TP], EG[:, P:TP], ALU.mult).then_inc(qg_ready, 1)
                    dve.wait_ge(yb_first, h + 1)
                    for tap in (1, 0):
                        dve.scalar_tensor_tensor(YB[:, :], CX[:, tap:tap + T], V[:, bass.ds(VEC["conv2"] + h * 4 + tap, 1)],
                                                 YB[:, :], ALU.mult, ALU.add)
                        dve.drain()
                    dve.wait_ge(side_ready, i * 8 + hh * 4 + 1)
                    dve.tensor_tensor(YB[:, :], YB[:, :], BG[:, :], ALU.mult)
                    dve.wait_ge(state_mm, h + 1)
                    dve.tensor_copy(ST[:, 0, :], A45[:, 0:P])
                    for c in range(1, CH - 1):
                        dve.drain()
                        dve.scalar_tensor_tensor(ST[:, c, :], ST[:, c - 1, :], EG[:, c * P + P - 1:c * P + P],
                                                 A45[:, c * P:(c + 1) * P], ALU.mult, ALU.add)
                    dve.drain().then_inc(state_ready, 1)
                    dve.wait_ge(side_ready, i * 8 + hh * 4 + 4)
                    dve.tensor_tensor(YB[:, :], YB[:, :], SB2[:, :], ALU.mult)
                    dve.wait_ge(orstd_ready, h + 2)
                    dve.scalar_tensor_tensor(ON[:, :], A67[:, PAD:TP], vec("hgrn_norm", 0), HRS[:, :], ALU.mult,
                                             ALU.mult).then_inc(on_ready, 1)
                    dve.drain()
                    dve.tensor_tensor(ON[:, :], ON[:, :], SO[:, :], ALU.mult)
                    dve.drain()
                    dve.tensor_tensor(ON[:, :], ON[:, :], SA[:, :], ALU.mult)
                    dve.drain()
                    dve.tensor_tensor(MF2[:, :], ON[:, :], YB[:, :], ALU.add)
                    dve.drain()
                    mhi, mlo = [x[:, bass.ds(h, 1), :].rearrange("p a n -> p (a n)") for x in (M2hi, M2lo)]
                    dve.tensor_copy(mhi, MF2[:, :])
                    dve.drain()
                    dve.tensor_tensor(mlo, MF2[:, :], mhi.bitcast(F32), ALU.subtract).then_inc(mix2_done, 1)
                    dve.drain()
            residual(3, U_OUT2, 1, None)
            norm_split(3)

            dve.drain()
            with dve.Fori(0, FC) as i:
                b0 = region(S + 2)
                dve.wait_ge(ya_first, i + 1)
                for tap in (1, 0):
                    ins = dve.scalar_tensor_tensor(YV[:, :], gp[0][:, b0 + tap:b0 + tap + S],
                                                   V[:, bass.ds(VEC["ffn2"] + i * 4 + tap, 1)], YV[:, :], ALU.mult, ALU.add)
                    if tap:
                        dve.drain()
                ins.then_inc(gp_free[0], 1)
                dve.drain().then_inc(ya_ready, 1)
                dve.wait_ge(silu2_ready, i + 1)
                dve.wait_ge(unit_done, U_UP2 + i * 2 + 2 + 2)
                dve.tensor_tensor(AF[:, :], gp[1][:, 0:S], SL[:, :], ALU.mult).then_inc(gp_free[1], 1)
                split_act(i, act2_done)
            residual(4, U_DN2, 3, None)
            dve.wait_ge(rstd_ready, len(NORMS))
            norm_final("final2", RSTD[:, 0:S])


def _constants():
    c = np.zeros((P, NCONST), np.float32)
    c[:, C_ID:C_ID + P] = np.eye(P)
    c[:, C_ONE:C_ONE + P] = 1.0
    c[:, C_MEAN:C_MEAN + P] = 1.0 / D
    c[:, C_HMEAN:C_HMEAN + P] = 1.0 / P
    c[:, C_EMEAN:C_EMEAN + P] = EPS / D
    r = np.arange(P)
    c[:, C_TRI:C_TRI + P] = np.where(r[None, :] <= r[:, None], 0.0, MASKED)
    for l, b in enumerate(LEVELS):
        upper = r[(r % (2 * b)) >= b]
        c[:, C_LEV + 64 * l:C_LEV + 64 * (l + 1)] = ((r[:, None] // (2 * b) == upper[None, :] // (2 * b))
                                                     & (r[:, None] % (2 * b) < b))
    c[:, C_RST:] = (np.arange(TP) % P != 0)[None, :]
    return c


def _buckets():
    n = np.maximum(S - 1 - np.arange(BIAS_W), 0)
    large = 16 + (np.log(np.maximum(n, 1).astype(np.float32) / 16) / np.log(8.0) * 16).astype(np.int32)
    bucket = np.where(n < 16, n, np.minimum(large, 31))
    return (np.arange(32)[:, None] == bucket[None, :]).astype(np.float32)


def kernel(**inputs):
    import concourse.bacc as bacc
    from concourse.bass_utils import run_bass_kernel_spmd

    a = {k: np.ascontiguousarray(v) for k, v in inputs.items()}

    def chunks(w):
        k, n = w.shape
        return w.reshape(k // P, P, n // P, P).transpose(2, 1, 0, 3).reshape(n // P, P, (k // P) * P)

    def cols(v):
        return v.reshape(-1, P).T

    def heads(w, n):
        return w.reshape(w.shape[:-1] + (2, 4, HD)).swapaxes(-3, -2).reshape(w.shape[:-1] + (n,))

    w_in, b_in = a["w_in"][0], a["b_in"][0]
    cut = np.cumsum([512, 128, 128, 512, 64, 8, D, D, D, D])[:-1]
    wq, wk, wv, wqi, wki, wwi, wxr, wyr, wga, wgb = np.split(w_in, cut, axis=1)
    bq, bk, bv, bqi, bki, bwi, bxr, byr, bga, bgb = np.split(b_in, cut)
    wi_pad = np.concatenate([wwi, np.zeros((D, P - NH), np.float32)], 1)
    proj = [chunks(wqi), chunks(np.concatenate([wki, wki], 1)), chunks(wi_pad), chunks(heads(wq, 512))]
    rnn = np.stack([chunks(wxr), chunks(wyr), chunks(wgb)], 1).reshape(3 * KC, P, UNIT)
    woa = a["w_o_attn"][0].reshape(2, 4, HD, D).swapaxes(0, 1).reshape(512, D)
    woa = chunks(woa).reshape(KC // 2, 2, P, 512).transpose(0, 2, 1, 3).reshape(KC // 2, 1, P, UNIT)
    gates = chunks(wga).reshape(KC // 2, 2, P, UNIT)
    merge = np.concatenate([gates, woa], 1).reshape(-1, P, UNIT)

    def up(w):
        return chunks(w).reshape(2, FC, P, UNIT).swapaxes(0, 1).reshape(2 * FC, P, UNIT)

    def down(w):
        t = chunks(w)
        t = np.concatenate([t, np.zeros((KC, P, 3 * UNIT - FF), np.float32)], 2)
        return t.reshape(KC, P, 3, UNIT).transpose(0, 2, 1, 3).reshape(3 * KC, P, UNIT)

    w2 = chunks(a["w_in_2"][0]).reshape(9, KC, P, UNIT)
    mix2 = w2[[1, 0, 2, 5, 6, 4, 3, 7, 8]].swapaxes(0, 1).reshape(9 * KC, P, UNIT)
    units = np.concatenate(proj + [rnn, chunks(wv), chunks(wk), chunks(a["w_o_rnn"][0]), merge, chunks(a["w_out"][0]), up(a["w_up"][0]), down(a["w_down"][0]), mix2,
                                   chunks(a["w_out_2"][0]), up(a["w_up_2"][0]), down(a["w_down_2"][0])], 0)

    cw, fw, fb = a["conv_rnn_w"][0], a["conv_ffn_w"][0], a["conv_ffn_b"][0]
    rnn_rows = [bxr, byr, cw[0], cw[1], cw[2], cw[3], a["conv_rnn_b"][0], a["b_rg"][0], a["b_ig"][0]]
    rnn_rows += [np.zeros(D, np.float32)] * (16 - len(rnn_rows))

    def inter(rows):
        return np.stack([cols(r) for r in rows], 2).reshape(P, -1)

    ffn_rows = [fw[0, :FF], fw[1, :FF], fw[2, :FF], fb[:FF], fw[0, FF:], fw[1, FF:], fw[2, FF:], fb[FF:]]
    c2, f2 = a["conv_w_2"][0], a["ffn_conv_w_2"][0]
    parts = [("b_ada", cols(a["b_ada"][0])), ("g_mix", cols(a["g_mix"][0])), ("b_qi", cols(bqi)),
             ("b_ki", cols(np.concatenate([bki, bki]))),
             ("b_wi", cols(np.concatenate([bwi, np.zeros(P - NH, np.float32)]))), ("b_q", cols(heads(bq, 512))),
             ("b_v", cols(bv)), ("b_k", cols(bk)),
             ("rnn", inter(rnn_rows)), ("b_gates", inter([bga, bgb])), ("lam", cols(a["lru_lambda"][0])),
             ("g_ffn", cols(a["g_ffn"][0])), ("ffn", inter(ffn_rows)), ("g_final", cols(a["g_final"])),
             ("lb0", cols(a["lb_param_2"][0])), ("lb1", cols(a["lb_param_2"][1])), ("attn_norm", cols(a["attn_norm_w_2"][0])),
             ("hgrn_norm", cols(a["hgrn_norm_w_2"][0])), ("conv2", inter([c2[0], c2[1], c2[2], np.zeros(D, np.float32)])),
             ("ffn_norm", cols(a["ffn_norm_w_2"][0])),
             ("ffn2", inter([f2[0], f2[1], f2[2], a["ffn_conv_b_2"][0]])), ("final2", cols(a["final_norm_w_2"]))]
    assert [n for n, _ in parts] == list(VEC)
    gatew = np.concatenate([a["w_rg"][0], a["w_ig"][0]], 2)
    arrays = {
        "xT": a["x"][0].T.reshape(KC, P, S).swapaxes(0, 1),
        "metaT": a["meta_tokens_2"].T.reshape(KC, P, META).swapaxes(0, 1),
        "vecs": np.concatenate([v for _, v in parts], 1),
        "rel": a["rel_bias"],
        "onehot": _buckets(),
        "consts": _constants(),
        "crow": a["c"][0],
        "ada": a["w_ada"][0].T.reshape(6 * KC, P, D),
        "gatew": gatew,
        "units": units,
    }
    nc = bacc.Bacc("TRN2", target_bir_lowering=False, num_devices=1)
    args, feed = [], {}
    for name, v in arrays.items():
        feed[name] = np.ascontiguousarray(v)
        args.append(nc.dram_tensor(name, v.shape, F32, kind="ExternalInput").ap())
    args.append(nc.dram_tensor("bias_rows", (NH, P, BIAS_W), F32, kind="Internal").ap())
    args.append(nc.dram_tensor("out", (P, KC, S), F32, kind="ExternalOutput").ap())
    build(nc, *args)
    r = run_bass_kernel_spmd(nc, [feed], core_ids=[0])
    o = np.asarray(r.results[0]["out"])
    return np.ascontiguousarray(o.transpose(2, 1, 0)).reshape(1, S, D)
```
